# Optimizing a Trainium2 kernel written in Bass

```python
import math
import jax, jax.numpy as jnp
from jax import lax
import numpy as np
import jax
import jax.numpy as jnp

D_MODEL = 1024
BATCH = 1
SEQ = 256
DEPTH = 1

POOL_WIDTH = D_MODEL // 2
POOL_WINDOWS = (2, 4, 8, 16)
POOL_GROUPS = len(POOL_WINDOWS)
POOL_GC = POOL_WIDTH // POOL_GROUPS
HEAD_DIM = 64
ATTN_HEADS = (D_MODEL // 2) // HEAD_DIM
ATTN_WIDTH = ATTN_HEADS * HEAD_DIM
MOBA_BLOCK = 256
MOBA_TOPK = 3
QUERY_CHUNK = 64
ROPE_THETA = 500000.0
ROT_DIM = HEAD_DIM // 4
N_BRANCH = 2
IN_WIDTH = 2 * POOL_WIDTH + 4 * ATTN_WIDTH + N_BRANCH * D_MODEL
EPS = 1e-6


def rms_norm(x, g):
    xf = x.astype(jnp.float32)
    y = xf * lax.rsqrt(jnp.mean(xf * xf, axis=-1, keepdims=True) + EPS)
    return (y * g.astype(jnp.float32)).astype(x.dtype)

def partial_rope(x):
    S_ = x.shape[1]
    half = ROT_DIM // 2
    pos = jnp.arange(S_, dtype=jnp.float32)
    inv_freq = ROPE_THETA ** (-jnp.arange(0, ROT_DIM, 2, dtype=jnp.float32) / ROT_DIM)
    ang = pos[:, None] * inv_freq[None, :]
    cos = jnp.cos(ang)[None, :, None, :].astype(x.dtype)
    sin = jnp.sin(ang)[None, :, None, :].astype(x.dtype)
    x1 = x[..., :half]
    x2 = x[..., half:ROT_DIM]
    return jnp.concatenate([x1 * cos - x2 * sin, x2 * cos + x1 * sin, x[..., ROT_DIM:]], axis=-1)

def multiscale_pool(u, w_grp, scale):
    B_, S_, _ = u.shape
    ug = u.reshape(B_, S_, POOL_GROUPS, POOL_GC)
    uf = ug.astype(jnp.float32)
    cs = lax.cumsum(uf, axis=1)
    cs = jnp.concatenate([jnp.zeros_like(cs[:, :1]), cs], axis=1)
    t = jnp.arange(S_)
    means = []
    for g, w in enumerate(POOL_WINDOWS):
        hi = t + 1
        lo = jnp.maximum(t + 1 - w, 0)
        cnt = (hi - lo).astype(jnp.float32)[None, :, None]
        means.append((cs[:, hi, g] - cs[:, lo, g]) / cnt)
    d = (jnp.stack(means, axis=2) - uf).astype(u.dtype)
    y = jnp.einsum('bsgc,gcd->bsgd', d, w_grp).reshape(B_, S_, POOL_WIDTH)
    return y * scale

def moba_attention(q, k, v):
    B_, S_, H, Dh = q.shape
    q = q.transpose(0, 2, 1, 3)
    k = k.transpose(0, 2, 1, 3)
    v = v.transpose(0, 2, 1, 3)
    nb = -(-S_ // MOBA_BLOCK)
    s_pad = nb * MOBA_BLOCK
    pad = ((0, 0), (0, 0), (0, s_pad - S_), (0, 0))
    kb = jnp.pad(k, pad).reshape(B_, H, nb, MOBA_BLOCK, Dh)
    vb = jnp.pad(v, pad).reshape(B_, H, nb, MOBA_BLOCK, Dh)
    kmean = jnp.mean(kb.astype(jnp.float32), axis=3)
    n_sel = min(MOBA_TOPK, nb)
    nq = S_ // QUERY_CHUNK
    q_chunks = q.reshape(B_, H, nq, QUERY_CHUNK, Dh).transpose(2, 0, 1, 3, 4)
    scale = Dh ** -0.5
    bi = jnp.arange(B_)[:, None, None, None]
    hi = jnp.arange(H)[None, :, None, None]
    blk_ids = jnp.arange(nb)
    kr = jnp.arange(MOBA_BLOCK)

    def one_chunk(args):
        ci, qc = args
        q0 = ci * QUERY_CHUNK
        qblk = q0 // MOBA_BLOCK
        qpos = q0 + jnp.arange(QUERY_CHUNK)
        gate = jnp.einsum('bhqd,bhnd->bhqn', qc.astype(jnp.float32), kmean)
        gate = jnp.where(blk_ids < qblk, gate, -jnp.inf)
        _, sel = lax.top_k(gate, n_sel)
        sel_ok = sel < qblk
        ksel = kb[bi, hi, sel]
        vsel = vb[bi, hi, sel]
        s_sel = jnp.einsum('bhqd,bhqkjd->bhqkj', qc, ksel).astype(jnp.float32) * scale
        s_sel = jnp.where(sel_ok[..., None], s_sel, -jnp.inf)
        s_sel = s_sel.reshape(B_, H, QUERY_CHUNK, n_sel * MOBA_BLOCK)
        kown = lax.dynamic_index_in_dim(kb, qblk, axis=2, keepdims=False)
        vown = lax.dynamic_index_in_dim(vb, qblk, axis=2, keepdims=False)
        kpos = qblk * MOBA_BLOCK + kr
        s_own = jnp.einsum('bhqd,bhjd->bhqj', qc, kown).astype(jnp.float32) * scale
        s_own = jnp.where(kpos[None, :] <= qpos[:, None], s_own, -jnp.inf)
        p = jax.nn.softmax(jnp.concatenate([s_sel, s_own], axis=-1), axis=-1).astype(v.dtype)
        p_sel = p[..., :n_sel * MOBA_BLOCK].reshape(B_, H, QUERY_CHUNK, n_sel, MOBA_BLOCK)
        p_own = p[..., n_sel * MOBA_BLOCK:]
        return (jnp.einsum('bhqkj,bhqkjd->bhqd', p_sel, vsel)
                + jnp.einsum('bhqj,bhjd->bhqd', p_own, vown))

    out = lax.map(one_chunk, (jnp.arange(nq), q_chunks))
    return out.transpose(1, 0, 3, 2, 4).reshape(B_, S_, H * Dh)

def first_inputs(seed: int = 0) -> dict:
    key = jax.random.key(seed)
    ks = jax.random.split(key, 14)
    D = D_MODEL
    nrm = jax.random.normal
    return {
        "x": nrm(ks[0], (BATCH, SEQ, D), jnp.float32),
        "c": nrm(ks[1], (BATCH, D), jnp.float32),
        "w_ada": nrm(ks[2], (DEPTH, D, 3 * D), jnp.float32) * (0.3 * D ** -0.5),
        "b_ada": nrm(ks[3], (DEPTH, 3 * D), jnp.float32) * 0.01,
        "g_norm": 1.0 + 0.05 * nrm(ks[4], (DEPTH, D), jnp.float32),
        "w_in": nrm(ks[5], (DEPTH, D, IN_WIDTH), jnp.float32) * D ** -0.5,
        "w_pool_grp": nrm(ks[6], (DEPTH, POOL_GROUPS, POOL_GC, POOL_GC), jnp.float32) * POOL_GC ** -0.5,
        "pool_scale": 1.0 + 0.1 * nrm(ks[7], (DEPTH, POOL_WIDTH), jnp.float32),
        "w_pool_up": nrm(ks[8], (DEPTH, POOL_WIDTH, D), jnp.float32) * POOL_WIDTH ** -0.5,
        "w_attn_up": nrm(ks[9], (DEPTH, ATTN_WIDTH, D), jnp.float32) * ATTN_WIDTH ** -0.5,
        "w_out": nrm(ks[10], (DEPTH, D, D), jnp.float32) * D ** -0.5,
        "g_final": 1.0 + 0.05 * nrm(ks[11], (D,), jnp.float32),
    }

def first_block(x, c, w_ada, b_ada, g_norm, w_in, w_pool_grp, pool_scale, w_pool_up, w_attn_up, w_out, g_final):
    B_, S_, D = x.shape
    splits = np.cumsum([POOL_WIDTH, POOL_WIDTH, ATTN_WIDTH, ATTN_WIDTH, ATTN_WIDTH, ATTN_WIDTH, D_MODEL]).tolist()
    for l in range(DEPTH):
        mod = c @ w_ada[l] + b_ada[l]
        shift, scl, gate = jnp.split(mod, 3, axis=-1)
        h = rms_norm(x, g_norm[l]) * (1.0 + scl[:, None, :]) + shift[:, None, :]
        proj = h @ w_in[l]
        u_pool, z_pool, q, k, v, z_attn, m_pool, m_attn = jnp.split(proj, splits, axis=-1)
        y_pool = multiscale_pool(u_pool, w_pool_grp[l], pool_scale[l]) * jax.nn.silu(z_pool)
        y_pool = y_pool @ w_pool_up[l]
        q = partial_rope(q.reshape(B_, S_, ATTN_HEADS, HEAD_DIM))
        k = partial_rope(k.reshape(B_, S_, ATTN_HEADS, HEAD_DIM))
        v = v.reshape(B_, S_, ATTN_HEADS, HEAD_DIM)
        y_attn = moba_attention(q, k, v) * jax.nn.silu(z_attn)
        y_attn = y_attn @ w_attn_up[l]
        merged = jax.nn.sigmoid(m_pool) * y_pool + jax.nn.sigmoid(m_attn) * y_attn
        x = x + gate[:, None, :] * (merged @ w_out[l])
    return rms_norm(x, g_final)


DEPTH_2 = 2

CHUNK = 64
Q_BLOCK = 128
N_HEADS_SB = 8
N_HEADS_DIFF = 4
N_HEADS_CHUNK = D_MODEL // HEAD_DIM
D_SB = N_HEADS_SB * HEAD_DIM
D_DIFF = N_HEADS_DIFF * 2 * HEAD_DIM
D_MIX = D_SB + D_DIFF
D_IN_EVEN = 3 * D_SB + 3 * D_DIFF
ROT_DIM_2 = HEAD_DIM // 4
LEFT_CHUNKS = 8
BAND = (LEFT_CHUNKS + 1) * CHUNK
REL_CLIP = 128
N_REL = 2 * REL_CLIP + 1
D_FF_DENSE = 2816
N_EXPERTS = 8
TOP_K = 2
D_FF_EXPERT = 3584
RMS_EPS = 1e-6
N_EVEN = (DEPTH_2 + 1) // 2
N_ODD = DEPTH_2 // 2


F32 = jnp.float32

def rms_norm_2(x, g):
    xf = x.astype(F32)
    y = xf * lax.rsqrt(jnp.mean(xf * xf, axis=-1, keepdims=True) + RMS_EPS)
    return (y * g.astype(F32)).astype(x.dtype)

def rope_tables(positions):
    inv_freq = ROPE_THETA ** (-jnp.arange(0, ROT_DIM_2, 2, dtype=F32) / ROT_DIM_2)
    ang = positions.astype(F32)[..., None] * inv_freq
    return jnp.cos(ang)[:, None], jnp.sin(ang)[:, None]

def partial_rope_2(x, cos, sin):
    half = ROT_DIM_2 // 2
    x1 = x[..., :half].astype(F32)
    x2 = x[..., half:ROT_DIM_2].astype(F32)
    rot = jnp.concatenate([x1 * cos - x2 * sin, x2 * cos + x1 * sin], axis=-1)
    return jnp.concatenate([rot.astype(x.dtype), x[..., ROT_DIM_2:]], axis=-1)

def split_heads(t, n):
    b, s, _ = t.shape
    return t.reshape(b, s, n, -1).transpose(0, 2, 1, 3)

def merge_heads(o):
    b, h, s, d = o.shape
    return o.transpose(0, 2, 1, 3).reshape(b, s, h * d)

def to_query_blocks(q):
    b, h, s, d = q.shape
    return jnp.moveaxis(q.reshape(b, h, s // Q_BLOCK, Q_BLOCK, d), 2, 0)

def from_query_blocks(o):
    nb, b, h, qb, d = o.shape
    return jnp.moveaxis(o, 0, 2).reshape(b, h, nb * qb, d)

def stick_breaking_attention(q, k, v):
    s_len = q.shape[2]
    nb = s_len // Q_BLOCK
    scale = HEAD_DIM ** -0.5
    k_idx = jnp.arange(s_len)

    def block(args):
        q_blk, start = args
        z = jnp.einsum('bhqd,bhkd->bhqk', q_blk, k, preferred_element_type=F32) * scale
        t_idx = start + jnp.arange(Q_BLOCK)
        past = k_idx[None, :] < t_idx[:, None]
        log_stay = jnp.where(past, jax.nn.log_sigmoid(-z), 0.0)
        between = lax.cumsum(log_stay, axis=3, reverse=True) - log_stay
        w = jnp.where(past, jnp.exp(jax.nn.log_sigmoid(z) + between), 0.0)
        return jnp.einsum('bhqk,bhkd->bhqd', w.astype(v.dtype), v)

    out = lax.map(block, (to_query_blocks(q), jnp.arange(nb, dtype=jnp.int32) * Q_BLOCK))
    return from_query_blocks(out)

def differential_attention(q, k, v, lam):
    b, h, _, s_len, d = q.shape
    nb = s_len // Q_BLOCK
    scale = HEAD_DIM ** -0.5
    k_chunk = jnp.arange(s_len) // CHUNK
    q_blocks = jnp.moveaxis(q.reshape(b, h, 2, nb, Q_BLOCK, d), 3, 0)

    def block(args):
        q_blk, start = args
        sc = jnp.einsum('bhmqd,bhmkd->bhmqk', q_blk, k, preferred_element_type=F32) * scale
        t_chunk = (start + jnp.arange(Q_BLOCK)) // CHUNK
        visible = k_chunk[None, :] <= t_chunk[:, None]
        p = jax.nn.softmax(jnp.where(visible, sc, -jnp.inf), axis=-1)
        w = p[:, :, 0] - lam * p[:, :, 1]
        return jnp.einsum('bhqk,bhkv->bhqv', w.astype(v.dtype), v)

    out = lax.map(block, (q_blocks, jnp.arange(nb, dtype=jnp.int32) * Q_BLOCK))
    return from_query_blocks(out)

def chunk_band_attention(q, k, v, rel_table):
    b, h, s_len, d = q.shape
    nc = s_len // CHUNK
    pad = LEFT_CHUNKS * CHUNK
    scale = HEAD_DIM ** -0.5
    k_pad = jnp.pad(k, ((0, 0), (0, 0), (pad, 0), (0, 0)))
    v_pad = jnp.pad(v, ((0, 0), (0, 0), (pad, 0), (0, 0)))
    i = jnp.arange(CHUNK)
    j = jnp.arange(BAND)
    rel = jnp.clip(pad + i[:, None] - j[None, :], -REL_CLIP, REL_CLIP) + REL_CLIP
    bias = rel_table[:, rel].astype(F32)
    q_chunks = jnp.moveaxis(q.reshape(b, h, nc, CHUNK, d), 2, 0)

    def chunk(args):
        q_c, c = args
        start = c * CHUNK
        k_band = lax.dynamic_slice_in_dim(k_pad, start, BAND, axis=2)
        v_band = lax.dynamic_slice_in_dim(v_pad, start, BAND, axis=2)
        sc = jnp.einsum('bhqd,bhkd->bhqk', q_c, k_band, preferred_element_type=F32) * scale + bias
        valid = (start - pad + j) >= 0
        p = jax.nn.softmax(jnp.where(valid[None, None, None, :], sc, -jnp.inf), axis=-1)
        return jnp.einsum('bhqk,bhkd->bhqd', p.astype(v.dtype), v_band)

    out = lax.map(chunk, (q_chunks, jnp.arange(nc, dtype=jnp.int32)))
    return jnp.moveaxis(out, 0, 2).reshape(b, h, s_len, d)

def even_mixer(h, cos, sin, w_in, q_norm, k_norm, lam_q1, lam_k1, lam_q2, lam_k2, subln, w_out, layer):
    b, s, _ = h.shape
    proj = h @ w_in
    cuts = [D_SB, 2 * D_SB, 3 * D_SB, 3 * D_SB + D_DIFF, 3 * D_SB + 2 * D_DIFF]
    q_sb, k_sb, v_sb, q_df, k_df, v_df = jnp.split(proj, cuts, axis=-1)
    o_sb = stick_breaking_attention(split_heads(q_sb, N_HEADS_SB), split_heads(k_sb, N_HEADS_SB),
                                    split_heads(v_sb, N_HEADS_SB))
    qd = partial_rope_2(rms_norm_2(split_heads(q_df, 2 * N_HEADS_DIFF), q_norm), cos, sin)
    kd = partial_rope_2(rms_norm_2(split_heads(k_df, 2 * N_HEADS_DIFF), k_norm), cos, sin)
    qd = qd.reshape(b, N_HEADS_DIFF, 2, s, HEAD_DIM)
    kd = kd.reshape(b, N_HEADS_DIFF, 2, s, HEAD_DIM)
    vd = split_heads(v_df, N_HEADS_DIFF)
    lam_init = 0.8 - 0.6 * math.exp(-0.3 * layer)
    lam = (jnp.exp(jnp.sum(lam_q1.astype(F32) * lam_k1.astype(F32)))
           - jnp.exp(jnp.sum(lam_q2.astype(F32) * lam_k2.astype(F32))) + lam_init)
    o_df = rms_norm_2(differential_attention(qd, kd, vd, lam), subln) * (1.0 - lam_init)
    merged = jnp.concatenate([merge_heads(o_sb), merge_heads(o_df)], axis=-1)
    return merged @ w_out

def odd_mixer(h, w_qkv, q_norm, k_norm, rel_table, w_out):
    q, k, v = jnp.split(h @ w_qkv, 3, axis=-1)
    q = rms_norm_2(split_heads(q, N_HEADS_CHUNK), q_norm)
    k = rms_norm_2(split_heads(k, N_HEADS_CHUNK), k_norm)
    o = chunk_band_attention(q, k, split_heads(v, N_HEADS_CHUNK), rel_table)
    return merge_heads(o) @ w_out

def swiglu(h, w_gate, w_up, w_down):
    return (jax.nn.silu(h @ w_gate) * (h @ w_up)) @ w_down

def moe_swiglu(h, w_router, we_gate, we_up, we_down):
    b, s, d = h.shape
    t = h.reshape(b * s, d)
    logits = (t @ w_router).astype(F32)
    top_val, top_idx = lax.top_k(logits, TOP_K)
    gates = jax.nn.softmax(top_val, axis=-1)
    combine = jnp.einsum('tk,tke->te', gates, jax.nn.one_hot(top_idx, N_EXPERTS, dtype=F32))
    y = jnp.zeros_like(t)
    for e in range(N_EXPERTS):
        y = y + combine[:, e:e + 1].astype(t.dtype) * swiglu(t, we_gate[e], we_up[e], we_down[e])
    return y.reshape(b, s, d)

def second_inputs(seed: int = 0) -> dict:
    key = jax.random.key(seed)
    ks = jax.random.split(key, 32)

    def nrm(k, shape, scale):
        return jax.random.normal(k, shape, F32) * scale

    def gain(k, shape):
        return 1.0 + 0.02 * jax.random.normal(k, shape, F32)

    x = nrm(ks[0], (BATCH, SEQ, D_MODEL), 1.0)
    offsets = jax.random.randint(ks[1], (BATCH, 1), 0, 16, dtype=jnp.int32) * CHUNK
    positions = offsets + jnp.arange(SEQ, dtype=jnp.int32)[None, :]
    return {
        'x': x,
        'positions': positions,
        'ev_attn_norm': gain(ks[2], (N_EVEN, D_MODEL)),
        'ev_w_in': nrm(ks[3], (N_EVEN, D_MODEL, D_IN_EVEN), D_MODEL ** -0.5),
        'ev_q_norm': gain(ks[4], (N_EVEN, HEAD_DIM)),
        'ev_k_norm': gain(ks[5], (N_EVEN, HEAD_DIM)),
        'ev_lambda_q1': nrm(ks[6], (N_EVEN, HEAD_DIM), 0.1),
        'ev_lambda_k1': nrm(ks[7], (N_EVEN, HEAD_DIM), 0.1),
        'ev_lambda_q2': nrm(ks[8], (N_EVEN, HEAD_DIM), 0.1),
        'ev_lambda_k2': nrm(ks[9], (N_EVEN, HEAD_DIM), 0.1),
        'ev_subln': gain(ks[10], (N_EVEN, 2 * HEAD_DIM)),
        'ev_w_out': nrm(ks[11], (N_EVEN, D_MIX, D_MODEL), D_MIX ** -0.5),
        'ev_ffn_norm': gain(ks[12], (N_EVEN, D_MODEL)),
        'ev_w_gate': nrm(ks[13], (N_EVEN, D_MODEL, D_FF_DENSE), D_MODEL ** -0.5),
        'ev_w_up': nrm(ks[14], (N_EVEN, D_MODEL, D_FF_DENSE), D_MODEL ** -0.5),
        'ev_w_down': nrm(ks[15], (N_EVEN, D_FF_DENSE, D_MODEL), D_FF_DENSE ** -0.5),
        'od_attn_norm': gain(ks[16], (N_ODD, D_MODEL)),
        'od_w_qkv': nrm(ks[17], (N_ODD, D_MODEL, 3 * N_HEADS_CHUNK * HEAD_DIM), D_MODEL ** -0.5),
        'od_q_norm': gain(ks[18], (N_ODD, HEAD_DIM)),
        'od_k_norm': gain(ks[19], (N_ODD, HEAD_DIM)),
        'od_rel_bias': nrm(ks[20], (N_ODD, N_HEADS_CHUNK, N_REL), 0.5),
        'od_w_out': nrm(ks[21], (N_ODD, N_HEADS_CHUNK * HEAD_DIM, D_MODEL), (N_HEADS_CHUNK * HEAD_DIM) ** -0.5),
        'od_ffn_norm': gain(ks[22], (N_ODD, D_MODEL)),
        'od_router': nrm(ks[23], (N_ODD, D_MODEL, N_EXPERTS), D_MODEL ** -0.5),
        'od_we_gate': nrm(ks[24], (N_ODD, N_EXPERTS, D_MODEL, D_FF_EXPERT), D_MODEL ** -0.5),
        'od_we_up': nrm(ks[25], (N_ODD, N_EXPERTS, D_MODEL, D_FF_EXPERT), D_MODEL ** -0.5),
        'od_we_down': nrm(ks[26], (N_ODD, N_EXPERTS, D_FF_EXPERT, D_MODEL), D_FF_EXPERT ** -0.5),
    }

def second_block(x, positions, ev_attn_norm, ev_w_in, ev_q_norm, ev_k_norm, ev_lambda_q1, ev_lambda_k1,
              ev_lambda_q2, ev_lambda_k2, ev_subln, ev_w_out, ev_ffn_norm, ev_w_gate, ev_w_up, ev_w_down,
              od_attn_norm, od_w_qkv, od_q_norm, od_k_norm, od_rel_bias, od_w_out, od_ffn_norm, od_router,
              od_we_gate, od_we_up, od_we_down):
    cos, sin = rope_tables(positions)
    for layer in range(DEPTH_2):
        i = layer // 2
        if layer % 2 == 0:
            x = x + even_mixer(rms_norm_2(x, ev_attn_norm[i]), cos, sin, ev_w_in[i], ev_q_norm[i], ev_k_norm[i],
                               ev_lambda_q1[i], ev_lambda_k1[i], ev_lambda_q2[i], ev_lambda_k2[i],
                               ev_subln[i], ev_w_out[i], layer)
            x = x + swiglu(rms_norm_2(x, ev_ffn_norm[i]), ev_w_gate[i], ev_w_up[i], ev_w_down[i])
        else:
            x = x + odd_mixer(rms_norm_2(x, od_attn_norm[i]), od_w_qkv[i], od_q_norm[i], od_k_norm[i],
                              od_rel_bias[i], od_w_out[i])
            x = x + moe_swiglu(rms_norm_2(x, od_ffn_norm[i]), od_router[i], od_we_gate[i], od_we_up[i],
                               od_we_down[i])
    return x


DEPTH_3 = 2

N_MIXERS = 2
N_HEADS = 16
ATTN_WIDTH_3 = N_HEADS * HEAD_DIM
FOX_BLOCK = 128
FOX_IN = 4 * ATTN_WIDTH_3 + N_HEADS
NSA_GROUPS = 4
NSA_REP = N_HEADS // NSA_GROUPS
KV_WIDTH = NSA_GROUPS * HEAD_DIM
CMP_LEN = 32
CMP_STRIDE = 16
CMP_HIDDEN = 256
SEL_LEN = 64
N_SELECT = 8
SEL_QCHUNK = 32
WINDOW = 512
WIN_BLOCK = 128
N_BRANCH_3 = 3
NSA_IN = 2 * ATTN_WIDTH_3 + 6 * KV_WIDTH + N_BRANCH_3 * N_HEADS
ROPE_DIM = HEAD_DIM // 4
NORM_EPS = 1e-6
NEG = -1e30
FORCE = 1e6
N_FOX = (DEPTH_3 + 1) // 2
N_NSA = DEPTH_3 // 2


def rmsnorm(x, g):
    xf = x.astype(jnp.float32)
    y = xf * lax.rsqrt(jnp.mean(xf * xf, axis=-1, keepdims=True) + NORM_EPS)
    return (y * g.astype(jnp.float32)).astype(x.dtype)

def rope_partial(x, pos):
    half = ROPE_DIM // 2
    inv_freq = jnp.power(ROPE_THETA, -jnp.arange(half, dtype=jnp.float32) * (2.0 / ROPE_DIM))
    ang = pos.astype(jnp.float32)[:, None] * inv_freq[None, :]
    shape = (pos.shape[0],) + (1,) * (x.ndim - 3) + (half,)
    cos = jnp.cos(ang).reshape(shape)
    sin = jnp.sin(ang).reshape(shape)
    xr = x[..., :ROPE_DIM].astype(jnp.float32)
    x1, x2 = xr[..., :half], xr[..., half:]
    rot = jnp.concatenate([x1 * cos - x2 * sin, x1 * sin + x2 * cos], axis=-1).astype(x.dtype)
    return jnp.concatenate([rot, x[..., ROPE_DIM:]], axis=-1)

def fox_mixer(h, w_in, b_f, w_out):
    B, S, _ = h.shape
    W = ATTN_WIDTH_3
    proj = h @ w_in
    q, k, v, f, z = jnp.split(proj, [W, 2 * W, 3 * W, 3 * W + N_HEADS], axis=-1)
    q = q.reshape(B, S, N_HEADS, HEAD_DIM)
    k = k.reshape(B, S, N_HEADS, HEAD_DIM)
    v = v.reshape(B, S, N_HEADS, HEAD_DIM)
    log_f = jax.nn.log_sigmoid(f.astype(jnp.float32) + b_f.astype(jnp.float32))
    c = jnp.cumsum(log_f, axis=1).transpose(0, 2, 1)
    scale = HEAD_DIM ** -0.5
    outs = []
    for qb in range(S // FOX_BLOCK):
        s0, s1 = qb * FOX_BLOCK, (qb + 1) * FOX_BLOCK
        logits = jnp.einsum('bqhd,bkhd->bhqk', q[:, s0:s1], k[:, :s1]).astype(jnp.float32) * scale
        logits = logits + c[:, :, s0:s1, None] - c[:, :, None, :s1]
        tq = jnp.arange(s0, s1)
        tk = jnp.arange(s1)
        logits = jnp.where(tk[None, :] <= tq[:, None], logits, NEG)
        p = jax.nn.softmax(logits, axis=-1).astype(v.dtype)
        outs.append(jnp.einsum('bhqk,bkhd->bqhd', p, v[:, :s1]))
    o = jnp.concatenate(outs, axis=1).reshape(B, S, W)
    return (o * jax.nn.silu(z)) @ w_out

def compress_blocks(x, pe, w1, w2):
    B, S, G, D = x.shape
    n_chunk = S // CMP_STRIDE
    r = CMP_LEN // CMP_STRIDE
    n_cmp = n_chunk - r + 1
    ch = x.reshape(B, n_chunk, CMP_STRIDE, G, D)
    blk = jnp.concatenate([ch[:, j:j + n_cmp] for j in range(r)], axis=2)
    blk = blk + pe[None, None, :, None, :]
    blk = blk.transpose(0, 1, 3, 2, 4).reshape(B, n_cmp, G, CMP_LEN * D)
    return jax.nn.silu(blk @ w1) @ w2

def nsa_mixer(h, w_in, pe_k, w_ck1, w_ck2, pe_v, w_cv1, w_cv2, w_out):
    B, S, _ = h.shape
    G, R, D, W = NSA_GROUPS, NSA_REP, HEAD_DIM, ATTN_WIDTH_3
    proj = h @ w_in
    offs = [W + i * KV_WIDTH for i in range(1, 7)] + [W + 6 * KV_WIDTH + N_BRANCH_3 * N_HEADS]
    q, kc_raw, vc_raw, ks_raw, vs_raw, kw_raw, vw_raw, gate_raw, z = jnp.split(proj, [W] + offs, axis=-1)
    pos = jnp.arange(S)
    q = rope_partial(q.reshape(B, S, G, R, D), pos)
    scale = D ** -0.5

    kc = compress_blocks(kc_raw.reshape(B, S, G, D), pe_k, w_ck1, w_ck2)
    vc = compress_blocks(vc_raw.reshape(B, S, G, D), pe_v, w_cv1, w_cv2)
    n_cmp = kc.shape[1]
    cmp_end = jnp.arange(n_cmp) * CMP_STRIDE + CMP_LEN - 1
    kc = rope_partial(kc, cmp_end)
    lg_c = jnp.einsum('bsgrd,bcgd->bgrsc', q, kc).astype(jnp.float32) * scale
    mask_c = cmp_end[None, :] <= pos[:, None]
    p_c = jax.nn.softmax(jnp.where(mask_c, lg_c, NEG), axis=-1)
    p_c = jnp.where(mask_c, p_c, 0.0)
    o_c = jnp.einsum('bgrsc,bcgd->bsgrd', p_c.astype(vc.dtype), vc)

    n_sel_blk = S // SEL_LEN
    n_sel = min(N_SELECT, n_sel_blk)
    ci = jnp.arange(n_cmp) * CMP_STRIDE
    sj = jnp.arange(n_sel_blk) * SEL_LEN
    overlap = ((ci[:, None] < sj[None, :] + SEL_LEN) & (ci[:, None] + CMP_LEN > sj[None, :])).astype(jnp.float32)
    imp = jnp.einsum('bgsc,cj->bgsj', p_c.sum(axis=2), overlap)
    cur = pos // SEL_LEN
    blk_ids = jnp.arange(n_sel_blk)
    forced = (blk_ids[None, :] == 0) | (blk_ids[None, :] == cur[:, None]) | (blk_ids[None, :] == cur[:, None] - 1)
    causal = blk_ids[None, :] <= cur[:, None]
    imp = jnp.where(forced, FORCE, jnp.where(causal, imp, -1.0))
    _, idx = lax.top_k(imp, n_sel)

    ks = rope_partial(ks_raw.reshape(B, S, G, D), pos)
    vs = vs_raw.reshape(B, S, G, D)
    k_blocks = ks.reshape(B, n_sel_blk, SEL_LEN, G, D).transpose(0, 3, 1, 2, 4)
    v_blocks = vs.reshape(B, n_sel_blk, SEL_LEN, G, D).transpose(0, 3, 1, 2, 4)
    n_qc = S // SEL_QCHUNK
    q_ch = q.reshape(B, n_qc, SEL_QCHUNK, G, R, D).transpose(1, 0, 2, 3, 4, 5)
    idx_ch = idx.transpose(0, 2, 1, 3).reshape(B, n_qc, SEL_QCHUNK, G, n_sel).transpose(1, 0, 2, 3, 4)
    pos_ch = pos.reshape(n_qc, SEL_QCHUNK)
    bi = jnp.arange(B)[:, None, None, None]
    gi = jnp.arange(G)[None, None, :, None]
    l_off = jnp.arange(SEL_LEN)

    def sel_chunk(args):
        qc, ic, tc = args
        kb = k_blocks[bi, gi, ic]
        vb = v_blocks[bi, gi, ic]
        lg = jnp.einsum('btgrd,btgnld->btgrnl', qc, kb).astype(jnp.float32) * scale
        kpos = ic[..., None] * SEL_LEN + l_off
        m = (kpos <= tc[None, :, None, None, None])[:, :, :, None]
        lg = jnp.where(m, lg, NEG)
        p = jax.nn.softmax(lg.reshape(B, SEL_QCHUNK, G, R, n_sel * SEL_LEN), axis=-1)
        p = p.reshape(B, SEL_QCHUNK, G, R, n_sel, SEL_LEN).astype(vb.dtype)
        return jnp.einsum('btgrnl,btgnld->btgrd', p, vb)

    o_s = lax.map(sel_chunk, (q_ch, idx_ch, pos_ch))
    o_s = o_s.transpose(1, 0, 2, 3, 4, 5).reshape(B, S, G, R, D)

    kw = rope_partial(kw_raw.reshape(B, S, G, D), pos)
    vw = vw_raw.reshape(B, S, G, D)
    n_qb = S // WIN_BLOCK
    n_wb = -(-WINDOW // WIN_BLOCK)
    pad = n_wb * WIN_BLOCK
    band = (n_wb + 1) * WIN_BLOCK
    kpad = jnp.pad(kw, ((0, 0), (pad, 0), (0, 0), (0, 0))).reshape(B, n_qb + n_wb, WIN_BLOCK, G, D)
    vpad = jnp.pad(vw, ((0, 0), (pad, 0), (0, 0), (0, 0))).reshape(B, n_qb + n_wb, WIN_BLOCK, G, D)
    k_band = jnp.concatenate([kpad[:, j:j + n_qb] for j in range(n_wb + 1)], axis=2)
    v_band = jnp.concatenate([vpad[:, j:j + n_qb] for j in range(n_wb + 1)], axis=2)
    qb = q.reshape(B, n_qb, WIN_BLOCK, G, R, D)
    lg_w = jnp.einsum('bnqgrd,bnkgd->bngrqk', qb, k_band).astype(jnp.float32) * scale
    tq = pos.reshape(n_qb, WIN_BLOCK)
    tk = jnp.arange(n_qb)[:, None] * WIN_BLOCK - pad + jnp.arange(band)[None, :]
    m_w = (tk[:, None, :] <= tq[:, :, None]) & (tk[:, None, :] > tq[:, :, None] - WINDOW) & (tk[:, None, :] >= 0)
    lg_w = jnp.where(m_w[None, :, None, None], lg_w, NEG)
    p_w = jax.nn.softmax(lg_w, axis=-1).astype(v_band.dtype)
    o_w = jnp.einsum('bngrqk,bnkgd->bnqgrd', p_w, v_band).reshape(B, S, G, R, D)

    g = jax.nn.sigmoid(gate_raw.astype(jnp.float32)).reshape(B, S, G, R, N_BRANCH_3).astype(o_c.dtype)
    o = g[..., 0:1] * o_c + g[..., 1:2] * o_s + g[..., 2:3] * o_w
    return (o.reshape(B, S, W) * jax.nn.silu(z)) @ w_out

def third_inputs(seed: int = 0) -> dict:
    key = jax.random.key(seed)
    ks = jax.random.split(key, 16)
    f32 = jnp.float32
    W = ATTN_WIDTH_3
    cdim = CMP_LEN * HEAD_DIM
    return {
        "x": jax.random.normal(ks[0], (BATCH, SEQ, D_MODEL), f32),
        "norm_g": 1.0 + 0.1 * jax.random.normal(ks[1], (DEPTH_3, D_MODEL), f32),
        "fox_w_in": jax.random.normal(ks[2], (N_FOX, D_MODEL, FOX_IN), f32) * D_MODEL ** -0.5,
        "fox_b_f": jax.random.uniform(ks[3], (N_FOX, N_HEADS), f32, 1.0, 6.0),
        "fox_w_out": jax.random.normal(ks[4], (N_FOX, W, D_MODEL), f32) * W ** -0.5,
        "nsa_w_in": jax.random.normal(ks[5], (N_NSA, D_MODEL, NSA_IN), f32) * D_MODEL ** -0.5,
        "nsa_pe_k": 0.1 * jax.random.normal(ks[6], (N_NSA, CMP_LEN, HEAD_DIM), f32),
        "nsa_w_ck1": jax.random.normal(ks[7], (N_NSA, cdim, CMP_HIDDEN), f32) * cdim ** -0.5,
        "nsa_w_ck2": jax.random.normal(ks[8], (N_NSA, CMP_HIDDEN, HEAD_DIM), f32) * CMP_HIDDEN ** -0.5,
        "nsa_pe_v": 0.1 * jax.random.normal(ks[9], (N_NSA, CMP_LEN, HEAD_DIM), f32),
        "nsa_w_cv1": jax.random.normal(ks[10], (N_NSA, cdim, CMP_HIDDEN), f32) * cdim ** -0.5,
        "nsa_w_cv2": jax.random.normal(ks[11], (N_NSA, CMP_HIDDEN, HEAD_DIM), f32) * CMP_HIDDEN ** -0.5,
        "nsa_w_out": jax.random.normal(ks[12], (N_NSA, W, D_MODEL), f32) * W ** -0.5,
        "final_g": 1.0 + 0.1 * jax.random.normal(ks[13], (D_MODEL,), f32),
    }

def third_block(x, norm_g, fox_w_in, fox_b_f, fox_w_out, nsa_w_in, nsa_pe_k, nsa_w_ck1, nsa_w_ck2,
              nsa_pe_v, nsa_w_cv1, nsa_w_cv2, nsa_w_out, final_g):
    for i in range(DEPTH_3):
        h = rmsnorm(x, norm_g[i])
        j = i // N_MIXERS
        if i % N_MIXERS == 0:
            y = fox_mixer(h, fox_w_in[j], fox_b_f[j], fox_w_out[j])
        else:
            y = nsa_mixer(h, nsa_w_in[j], nsa_pe_k[j], nsa_w_ck1[j], nsa_w_ck2[j],
                          nsa_pe_v[j], nsa_w_cv1[j], nsa_w_cv2[j], nsa_w_out[j])
        x = x + y
    return rmsnorm(x, final_g)


def setup_inputs(seed=0):
    out = dict(first_inputs(seed))
    for name, value in second_inputs(seed + 1).items():
        if name != "x":
            out[name + "_2"] = value
    for name, value in third_inputs(seed + 2).items():
        if name != "x":
            out[name + "_3"] = value
    return out


def reference(
    x, c, w_ada, b_ada, g_norm, w_in, w_pool_grp, pool_scale, w_pool_up, w_attn_up, w_out,
    g_final, positions_2, ev_attn_norm_2, ev_w_in_2, ev_q_norm_2, ev_k_norm_2, ev_lambda_q1_2,
    ev_lambda_k1_2, ev_lambda_q2_2, ev_lambda_k2_2, ev_subln_2, ev_w_out_2, ev_ffn_norm_2,
    ev_w_gate_2, ev_w_up_2, ev_w_down_2, od_attn_norm_2, od_w_qkv_2, od_q_norm_2, od_k_norm_2,
    od_rel_bias_2, od_w_out_2, od_ffn_norm_2, od_router_2, od_we_gate_2, od_we_up_2,
    od_we_down_2, norm_g_3, fox_w_in_3, fox_b_f_3, fox_w_out_3, nsa_w_in_3, nsa_pe_k_3,
    nsa_w_ck1_3, nsa_w_ck2_3, nsa_pe_v_3, nsa_w_cv1_3, nsa_w_cv2_3, nsa_w_out_3, final_g_3,
):
    x = first_block(
        x, c, w_ada, b_ada, g_norm, w_in, w_pool_grp, pool_scale, w_pool_up, w_attn_up, w_out,
        g_final,
    )
    x = second_block(
        x, positions_2, ev_attn_norm_2, ev_w_in_2, ev_q_norm_2, ev_k_norm_2, ev_lambda_q1_2,
        ev_lambda_k1_2, ev_lambda_q2_2, ev_lambda_k2_2, ev_subln_2, ev_w_out_2, ev_ffn_norm_2,
        ev_w_gate_2, ev_w_up_2, ev_w_down_2, od_attn_norm_2, od_w_qkv_2, od_q_norm_2,
        od_k_norm_2, od_rel_bias_2, od_w_out_2, od_ffn_norm_2, od_router_2, od_we_gate_2,
        od_we_up_2, od_we_down_2,
    )
    return third_block(
        x, norm_g_3, fox_w_in_3, fox_b_f_3, fox_w_out_3, nsa_w_in_3, nsa_pe_k_3, nsa_w_ck1_3,
        nsa_w_ck2_3, nsa_pe_v_3, nsa_w_cv1_3, nsa_w_cv2_3, nsa_w_out_3, final_g_3,
    )


_drawn_inputs = setup_inputs


def setup_inputs(seed=0):
    import zlib

    import numpy as np

    out = dict(_drawn_inputs(seed))
    spreads = {}
    factors = {'b_ada': 2.69,
     'ev_q_norm_2': 3.016,
     'od_attn_norm_2': 2.671,
     'od_q_norm_2': 3.609,
     'od_k_norm_2': 3.009,
     'nsa_pe_k_3': 64.0,
     'nsa_pe_v_3': 4.875,
     'norm_g_3': 3.029,
     'nsa_w_ck1_3': 4.294,
     'nsa_w_ck2_3': 4.076}
    for name, (base, spread) in spreads.items():
        noise = np.random.default_rng([zlib.crc32(name.encode()), seed]).standard_normal(out[name].shape)
        drawn = base * np.exp(spread * noise) if base else spread * noise
        out[name] = jnp.asarray(drawn.astype(out[name].dtype))
    for name, factor in factors.items():
        out[name] = (out[name] * factor).astype(out[name].dtype)
    return out
```

```python
from contextlib import ExitStack

import numpy as np
import concourse.bass as bass
from concourse import mybir

F32 = mybir.dt.float32
BF16 = mybir.dt.bfloat16
I32 = mybir.dt.int32
ALU = mybir.AluOpType
ACT = mybir.ActivationFunctionType
AX = mybir.AxisListType

S = 256
TT = S // 128
D = 1024
KD = D // 128
DH = 64
RING = 7
SLOT = 4096
EPS = 1e-6
BIG = 1e30
F_DENSE = 2816
F_EXP = 3584
NEXP = 8
CF = F_EXP // 512
MOE_CHUNKS = 3 * CF
TILE_MAX = 11
NCMP = 15
CPAD = 32
ROPE_THETA = 500000.0
WINDOWS = (2, 4, 8, 16)
LAM_INIT = 0.2

VEC_ROWS = {}
_at = 0
for _name, _n in (("ev_attn", 8), ("ev_ffn", 8), ("od_attn", 8), ("od_ffn", 8), ("norm3", 16),
                  ("pool_scale", 4), ("c", 8), ("pe_k", 16), ("pe_v", 16)):
    VEC_ROWS[_name] = (_at, _n)
    _at += _n
NVEC = _at

SM = {}
_at = 0
for _name, _n in (("ev_q", 64), ("ev_k", 64), ("od_q", 64), ("od_k", 64), ("subln", 128), ("b_f", 16),
                  ("lq1", 64), ("lk1", 64), ("lq2", 64), ("lk2", 64)):
    SM[_name] = (_at, _n)
    _at += _n
NSM = _at

CO = {}
_at = 0
for _name, _n in (("cos", 16), ("sin", 16), ("ccos", 8), ("csin", 8), ("invf", 8), ("cm01", 64), ("cmadd", 64)):
    CO[_name] = (_at, _n)
    _at += _n
NCO = _at


def shape_constants():
    inv = (np.float32(ROPE_THETA) ** (-np.arange(0, 16, 2, dtype=np.float32) / np.float32(16))).astype(np.float32)
    co = np.zeros((128, NCO), np.float32)
    ang = (np.arange(S, dtype=np.float32)[:, None] * inv[None, :]).astype(np.float32)
    for key, fn in (("cos", np.cos), ("sin", np.sin)):
        tab = fn(ang).astype(np.float32).reshape(TT, 128, 8).transpose(1, 0, 2).reshape(128, 16)
        co[:, CO[key][0]:CO[key][0] + 16] = tab
    end = (np.arange(128) % CPAD) * 16 + 31
    cang = (end.astype(np.float32)[:, None] * inv[None, :]).astype(np.float32)
    co[:, CO["ccos"][0]:CO["ccos"][0] + 8] = np.cos(cang)
    co[:, CO["csin"][0]:CO["csin"][0] + 8] = np.sin(cang)
    co[:, CO["invf"][0]:CO["invf"][0] + 8] = inv
    c = np.arange(CPAD)
    seen = ((c * 16 + 31)[None, :] <= np.arange(S)[:, None]) & (c < NCMP)[None, :]
    seen = seen.astype(np.float32).reshape(TT, 128, CPAD).transpose(1, 0, 2).reshape(128, 64)
    co[:, CO["cm01"][0]:CO["cm01"][0] + 64] = seen
    co[:, CO["cmadd"][0]:CO["cmadd"][0] + 64] = (seen - 1) * np.float32(BIG)
    band = np.zeros((4, S, S), np.float32)
    for g, w in enumerate(WINDOWS):
        for t in range(S):
            lo = max(t + 1 - w, 0)
            band[g, lo:t + 1, t] = np.float32(1) / np.float32(t + 1 - lo)
            band[g, t, t] -= np.float32(1)
    packed = np.zeros((128, 4, 384), np.float32)
    packed[:, :, :256] = band[:, :128, :].transpose(1, 0, 2)
    packed[:, :, 256:] = band[:, 128:, 128:].transpose(1, 0, 2)
    return co, packed


def build(nc, t):
    ctx = ExitStack()
    with ctx:
        def sb(name, shape, dt=F32):
            return ctx.enter_context(nc.sbuf_tensor(name, shape, dt))

        def sem(name):
            return ctx.enter_context(nc.semaphore(name))

        X = sb("X", [128, TT, D])
        XT = sb("XT", [128, KD, S])
        P = sb("P", [128, TT, 5120])
        QT = sb("QT", [128, 8, S])
        KT = sb("KT", [128, 8, S])
        O = sb("O", [128, TT, D])
        ring = sb("ring", [128, RING, SLOT])
        ident = sb("ident", [128, 128])
        identb = sb("identb", [128, 128], BF16)
        mask_causal = sb("mask_causal", [128, 128], BF16)
        mask_chunk = sb("mask_chunk", [128, 128], BF16)
        mask_past = sb("mask_past", [128, 128], BF16)
        past01 = sb("past01", [128, 128])
        neg_tri = sb("neg_tri", [128, 128])
        neg_ones = sb("neg_ones", [128, 128])
        ones = sb("ones", [128, 128])
        scr = sb("scr", [128, 1536])
        vec = sb("vec", [128, NVEC])
        small = sb("small", [128, NSM])
        co = sb("co", [128, NCO])
        cs2 = sb("cs2", [128, 4, 16])
        stat = sb("stat", [128, 64])
        rs = sb("rs", [128, 2, 2, 8])
        rr = sb("rr", [128, 2, 8])
        nmax = sb("nmax", [128, 2, 2])
        lam = sb("lam", [128, 4])
        posi = sb("posi", [128, TT], I32)
        bank = [ctx.enter_context(nc.psum_tensor(f"bank{b}", [128, 512], F32)) for b in range(8)]

        E = [scr[:, 0:384], scr[:, 384:768]]
        PT = [scr[:, 768:1152], scr[:, 1152:1536]]

        def col(name, i=0):
            at = VEC_ROWS[name][0] + i
            return vec[:, at:at + 1]

        def row(name):
            at, n = SM[name]
            return small[:, at:at + n]

        def con(name):
            at, n = CO[name]
            return co[:, at:at + n]

        stream = []

        def chunk(ap, nk, n, what):
            stream.append((ap, nk, n))
            return len(stream) - 1

        def kcols(w, c0, n):
            return w[:, c0:c0 + n].rearrange("(k p) n -> p k n", p=128)

        def krows(w, k0, nk):
            return w[k0 * 128:(k0 + nk) * 128, :].rearrange("(k p) n -> p k n", p=128)

        w = {n: t[n][0] for n in ("w_ada", "w_in", "w_pool_up", "w_attn_up", "w_out", "ev_w_in_2", "ev_w_out_2",
                                  "ev_w_gate_2", "ev_w_up_2", "ev_w_down_2", "od_w_qkv_2", "od_w_out_2",
                                  "od_router_2", "fox_w_in_3", "fox_w_out_3", "nsa_w_in_3", "nsa_w_ck1_3",
                                  "nsa_w_ck2_3", "nsa_w_cv1_3", "nsa_w_cv2_3", "nsa_w_out_3")}
        c_ada = [chunk(kcols(w["w_ada"], 512 * i, 512), 8, 512, "ada") for i in range(6)]
        c_in1 = [chunk(kcols(w["w_in"], 512 * i, 512), 8, 512, "in") for i in range(10)]
        c_band = chunk(t["band"], 4, 384, "band")
        c_grp = chunk(t["w_pool_grp"][0].rearrange("g c d -> c g d"), 4, 128, "grp")
        c_pup = chunk(krows(w["w_pool_up"], 0, 4), 4, D, "pool_up")
        c_aup = chunk(krows(w["w_attn_up"], 0, 4), 4, D, "attn_up")
        c_out1 = [(chunk(krows(w["w_out"], 4 * i, 4), 4, D, "out"), 4) for i in range(2)]
        c_in2 = [chunk(kcols(w["ev_w_in_2"], 512 * i, 512), 8, 512, "ev_in") for i in range(6)]
        c_out2 = [(chunk(krows(w["ev_w_out_2"], 4 * i, 4), 4, D, "ev_out"), 4) for i in range(2)]
        ff = [(512 * i, min(512, F_DENSE - 512 * i)) for i in range(-(-F_DENSE // 512))]
        c_ff = [(chunk(kcols(w["ev_w_gate_2"], c0, n), 8, n, "gate"), chunk(kcols(w["ev_w_up_2"], c0, n), 8, n, "up"))
                for c0, n in ff]
        KF = F_DENSE // 128
        c_down = [(chunk(krows(w["ev_w_down_2"], k0, min(4, KF - k0)), min(4, KF - k0), D, "down"), min(4, KF - k0))
                  for k0 in range(0, KF, 4)]
        c_in3 = [chunk(kcols(w["od_w_qkv_2"], 512 * i, 512), 8, 512, "od_in") for i in range(6)]
        c_rel = chunk(t["rel"], 16, 256, "rel")
        c_out3 = [(chunk(krows(w["od_w_out_2"], 4 * i, 4), 4, D, "od_out"), 4) for i in range(2)]
        c_router = chunk(kcols(w["od_router_2"], 0, NEXP), 8, NEXP, "router")
        N0 = len(stream)
        c_in4 = [chunk(kcols(w["fox_w_in_3"], 512 * i, 512), 8, 512, "fox_in") for i in range(6)]
        c_f = chunk(kcols(w["fox_w_in_3"], 3072, 16), 8, 16, "fox_f")
        c_z4 = [chunk(kcols(w["fox_w_in_3"], 3088 + 512 * i, 512), 8, 512, "fox_z") for i in range(2)]
        c_out4 = [(chunk(krows(w["fox_w_out_3"], 4 * i, 4), 4, D, "fox_out"), 4) for i in range(2)]
        c_in5 = [chunk(kcols(w["nsa_w_in_3"], 512 * i, 512), 8, 512, "nsa_in") for i in range(5)]
        c_g5 = chunk(kcols(w["nsa_w_in_3"], 2560, 48), 8, 48, "nsa_g")
        c_z5 = [chunk(kcols(w["nsa_w_in_3"], 2608 + 512 * i, 512), 8, 512, "nsa_z") for i in range(2)]
        c_ck = [(chunk(krows(w["nsa_w_ck1_3"], 0, 16), 16, 256, "ck1"), chunk(krows(w["nsa_w_ck2_3"], 0, 2), 2, DH, "ck2")),
                (chunk(krows(w["nsa_w_cv1_3"], 0, 16), 16, 256, "cv1"), chunk(krows(w["nsa_w_cv2_3"], 0, 2), 2, DH, "cv2"))]
        c_out5 = [(chunk(krows(w["nsa_w_out_3"], 4 * i, 4), 4, D, "nsa_out"), 4) for i in range(2)]

        landed = [sem(f"landed{s}") for s in range(RING)]
        consumed = sem("consumed")

        def slot_ap(n, nk, width):
            return ring[:, n % RING, 0:nk * width].rearrange("p (k n) -> p k n", k=nk)

        def after_moe(n):
            return n >= N0

        small_in = sem("small_in")
        ones_set = sem("ones_set")
        const_set = sem("const_set")
        vec_ready = sem("vec_ready")
        vec_set = sem("vec_set")
        dve_chain = sem("dve_chain")
        act_chain = sem("act_chain")

        turn_ready, turn_act, turn_dve = sem("turn_ready"), sem("turn_act"), sem("turn_dve")
        proj_half, proj_act, proj_dve = sem("proj_half"), sem("proj_act"), sem("proj_dve")
        scored, maxed, exped, turned, copied, valued, grouped = (
            sem(x) for x in ("scored", "maxed", "exped", "turned", "copied", "valued", "grouped"))
        base = {"turn": 0, "turn_act": 0, "turn_dve": 0, "proj": 0, "proj_act": 0, "proj_dve": 0, "unit": 0, "group": 0}

        class Transposes:

            def __init__(self, items):
                self.items, self.n = items, -(-len(items) // 2)
                self.b, self.ba, self.bd = base["turn"], base["turn_act"], base["turn_dve"]
                base["turn"] += self.n
                base["turn_act"] += (self.n + 1) // 2
                base["turn_dve"] += self.n // 2

            def pe(self, pe):
                for i in range(self.n):
                    if i >= 4:
                        pe.wait_ge(turn_dve if i % 2 else turn_act, (self.bd if i % 2 else self.ba) + (i - 4) // 2 + 1)
                    for j, (src, _, _) in enumerate(self.items[2 * i:2 * i + 2]):
                        for tt in range(TT):
                            last = nc.tensor.transpose(bank[4 + i % 4][:, j * S + tt * 128:j * S + tt * 128 + 128],
                                                       src(tt), ident[:, :])
                    last.then_inc(turn_ready, 1)

            def act(self, act):
                for i in range(0, self.n, 2):
                    act.wait_ge(turn_ready, self.b + i + 1)
                    for j, (_, dest, scale) in enumerate(self.items[2 * i:2 * i + 2]):
                        last = nc.scalar.activation(dest, bank[4 + i % 4][:, j * S:j * S + S], ACT.Copy,
                                                    scale=1.0 if scale is None else scale)
                    last.then_inc(turn_act, 1)

            def dve(self, dve):
                for i in range(1, self.n, 2):
                    dve.wait_ge(turn_ready, self.b + i + 1)
                    for j, (_, dest, scale) in enumerate(self.items[2 * i:2 * i + 2]):
                        src = bank[4 + i % 4][:, j * S:j * S + S]
                        if scale is None:
                            last = nc.vector.tensor_copy(dest, src)
                        else:
                            last = nc.vector.tensor_scalar(dest, src, scale, None, ALU.mult)
                    last.then_inc(turn_dve, 1)

            def wait(self, eng):
                eng.wait_ge(turn_act, self.ba + (self.n + 1) // 2)
                if self.n > 1:
                    eng.wait_ge(turn_dve, self.bd + self.n // 2)

        class Project:

            def __init__(self, jobs, lhs):
                self.jobs, self.lhs = jobs, lhs
                self.b, self.ba, self.bd = base["proj"], base["proj_act"], base["proj_dve"]
                base["proj"] += len(jobs)
                base["proj_dve"] += 2 * sum(j[3] is None for j in jobs)
                base["proj_act"] += 2 * sum(j[3] is not None for j in jobs)

            def emptied(self, c):
                mine = [j[3] is None for j in self.jobs]
                done = 2 * sum(m == mine[c] for m in mine[:c + 1])
                return (proj_dve, self.bd + done) if mine[c] else (proj_act, self.ba + done)

            def pe(self, pe):
                for c, (n, width, _, _) in enumerate(self.jobs):
                    wt = take(pe, n)
                    if c >= 2:
                        pe.wait_ge(*self.emptied(c - 2))
                    for tt in range(TT):
                        for kt in range(KD):
                            last = nc.tensor.matmul(bank[(2 * c + tt) % 4][:, 0:width], self.lhs(kt, tt), wt[:, kt, :],
                                                    start=kt == 0, stop=kt == KD - 1)
                        last.then_inc(consumed if tt else proj_half, 1)

            def empty(self, eng, vector):
                for c, (n, width, dest, func) in enumerate(self.jobs):
                    if (func is None) != vector:
                        continue
                    for tt in range(TT):
                        if tt == 0:
                            eng.wait_ge(proj_half, self.b + c + 1)
                        else:
                            used(eng, n)
                        src = bank[(2 * c + tt) % 4][:, 0:width]
                        if vector:
                            nc.vector.tensor_copy(dest(tt), src).then_inc(proj_dve, 1)
                        else:
                            nc.scalar.activation(dest(tt), src, func).then_inc(proj_act, 1)

            def act(self, act):
                self.empty(act, False)

            def dve(self, dve):
                self.empty(dve, True)

            def wait(self, eng):
                for is_dve in (False, True):
                    n = sum((j[3] is None) == is_dve for j in self.jobs)
                    if n:
                        eng.wait_ge(*((proj_dve, self.bd + 2 * n) if is_dve else (proj_act, self.ba + 2 * n)))

        class OutProduct:

            def __init__(self, chunks, lhs):
                self.chunks, self.lhs = chunks, lhs

            def pe(self, pe):
                total, k = sum(nk for _, nk in self.chunks), 0
                for n, nk in self.chunks:
                    wt = take(pe, n)
                    for kk in range(nk):
                        for tt in range(TT):
                            for half in range(2):
                                last = nc.tensor.matmul(bank[2 * tt + half][:, :], self.lhs(k, tt),
                                                        wt[:, kk, half * 512:half * 512 + 512],
                                                        start=k == 0, stop=k == total - 1)
                        k += 1
                    last.then_inc(consumed, 1)

            def wait(self, eng):
                used(eng, self.chunks[-1][0])

        class Attention:

            def __init__(self, units, dv, mask, finish, extra=None):
                self.units, self.dv, self.mask, self.finish, self.extra = units, dv, mask, finish, extra
                self.G = 512 // dv
                self.u, self.g = base["unit"], base["group"]
                base["unit"] += len(units)
                base["group"] += len(units) // self.G

            def pe(self, pe):
                U, G = len(self.units), self.G
                for i in range(U + 2):
                    if i < U:
                        (qt_, qb), (kt_, kb), _ = self.units[i]
                        assert qb == kb
                        b = bank[4 + i % 2]
                        if i >= 2:
                            pe.wait_ge(exped, self.u + i - 1)
                        q, k = QT[qb:qb + 64, qt_, :], KT[kb:kb + 64, kt_, :]
                        for t0, (a, n) in enumerate(((0, 128), (128, 256))):
                            nc.tensor.matmul(b[:, a:a + n], q[:, t0 * 128:t0 * 128 + 128], k[:, 0:n], start=True,
                                             stop=False, skip_group_check=True)
                            if self.extra:
                                self.extra(i, t0, b[:, a:a + n])
                            last = nc.tensor.matmul(b[:, a + n - 128:a + n], identb[:, :], self.mask[:, :], start=False,
                                                    stop=True, skip_group_check=True)
                        last.then_inc(scored, 1)
                    if 1 <= i <= U:
                        j = i - 1
                        pe.wait_ge(exped, self.u + j + 1)
                        if j >= 2:
                            pe.wait_ge(copied, self.u + j - 1)
                        for c in range(3):
                            last = nc.tensor.transpose(bank[6 + j % 2][:, c * 128:c * 128 + 128],
                                                       E[j % 2][:, c * 128:c * 128 + 128], ident[:, :])
                        last.then_inc(turned, 1)
                    if i >= 2:
                        j = i - 2
                        g, uu = j // G, j % G
                        pe.wait_ge(copied, self.u + j + 1)
                        if uu == 0 and g >= 2:
                            pe.wait_ge(grouped, self.g + g - 1)
                        v, p, o = self.units[j][2], PT[j % 2], slice(uu * self.dv, (uu + 1) * self.dv)
                        nc.tensor.matmul(bank[g % 2 * 2][:, o], p[:, 0:128], v(0), start=True, stop=True,
                                         skip_group_check=True)
                        nc.tensor.matmul(bank[g % 2 * 2 + 1][:, o], p[:, 128:256], v(0), start=True, stop=False,
                                         skip_group_check=True)
                        nc.tensor.matmul(bank[g % 2 * 2 + 1][:, o], p[:, 256:384], v(1), start=False, stop=True,
                                         skip_group_check=True).then_inc(valued, 1)

            def act(self, act):
                for i in range(len(self.units)):
                    g, uu = i // self.G, i % self.G
                    act.wait_ge(maxed, self.u + i + 1)
                    if i >= 2:
                        act.wait_ge(turned, self.u + i - 1)
                    if uu == 0 and g >= 2:
                        act.wait_ge(grouped, self.g + g - 1)
                    for t0, (a, n) in enumerate(((0, 128), (128, 256))):
                        last = nc.scalar.activation(E[i % 2][:, a:a + n], bank[4 + i % 2][:, a:a + n], ACT.Exp,
                                                    bias=nmax[:, i % 2, t0:t0 + 1],
                                                    accum_out=rs[:, g % 2, t0, uu:uu + 1])
                    last.then_inc(exped, 1)

            def dve(self, dve):
                U = len(self.units)
                for i in range(U + 1):
                    if i < U:
                        dve.wait_ge(scored, self.u + i + 1)
                        if i >= 2:
                            dve.wait_ge(exped, self.u + i - 1)
                        for t0, (a, n) in enumerate(((0, 128), (128, 256))):
                            last = nc.vector.tensor_reduce(nmax[:, i % 2, t0:t0 + 1], bank[4 + i % 2][:, a:a + n],
                                                           AX.X, ALU.max, negate=True)
                        last.then_inc(maxed, 1)
                    if i >= 1:
                        j = i - 1
                        dve.wait_ge(turned, self.u + j + 1)
                        if j >= 2:
                            dve.wait_ge(valued, self.u + j - 1)
                        nc.vector.tensor_copy(PT[j % 2], bank[6 + j % 2][:, 0:384]).then_inc(copied, 1)
                        g = j // self.G
                        if j % self.G == self.G - 1:
                            dve.wait_ge(valued, self.u + j + 1)
                            link(dve, nc.vector.reciprocal(rr[:, :, 0:self.G], rs[:, g % 2, :, 0:self.G]))
                            self.finish(dve, g)

            def wait(self, eng):
                eng.wait_ge(grouped, self.g + len(self.units) // self.G)

            def bank_of(self, g, tt):
                return bank[g % 2 * 2 + tt][:, :].rearrange("p (u d) -> p u d", d=self.dv)

        def per_head(tt, G, dv):
            return rr[:, tt, 0:G].unsqueeze(2).to_broadcast([128, G, dv])

        def heads_T(cols, dests, scale):
            return [(lambda tt, c=c: P[:, tt, c:c + 128], d, scale) for c, d in zip(cols, dests)]

        def normed(dest, gain):
            return [(lambda tt, k=k: O[:, tt, k * 128:k * 128 + 128], dest[:, k, :], gain and col(gain[0], gain[1] + k))
                    for k in range(KD)]

        xt = lambda kt, tt: XT[:, kt, tt * 128:tt * 128 + 128]
        pcol = lambda c0, n: (lambda tt: P[:, tt, c0:c0 + n])

        ss_ready, ms_ready = sem("ss_ready"), sem("ms_ready")

        ada_ps, ada_used = sem("ada_ps"), sem("ada_used")
        h1 = sem("h1")
        T1 = Transposes(normed(XT, None))
        P1 = Project([(c_in1[0], 512, pcol(0, 512), None), (c_in1[1], 512, pcol(512, 512), ACT.Silu),
                            (c_in1[2], 512, pcol(1024, 512), None), (c_in1[3], 512, pcol(1536, 512), None),
                            (c_in1[4], 512, pcol(2048, 512), None), (c_in1[5], 512, pcol(2560, 512), ACT.Silu)]
                     + [(c_in1[6 + i], 512, pcol(3072 + 512 * i, 512), ACT.Sigmoid) for i in range(4)], xt)
        roped1 = sem("roped1")
        TQ1 = Transposes(heads_T([1024 + 128 * i for i in range(4)], [QT[:, i, :] for i in range(4)], 0.125)
                         + heads_T([1536 + 128 * i for i in range(4)], [KT[:, i, :] for i in range(4)], None))
        d_copied, y_gated = sem("d_copied"), sem("y_gated")
        TY1 = Transposes([(lambda tt, g=g: P[:, tt, g * 128:g * 128 + 128], XT[:, g, :], col("pool_scale", g))
                                 for g in range(4)])
        UP1 = OutProduct([(c_pup, 4)], xt)
        up_used = sem("up_used")
        TA1 = Transposes([(lambda tt, k=k: O[:, tt, k * 128:k * 128 + 128], XT[:, 4 + k, :], None) for k in range(4)])
        gated1 = sem("gated1")
        AUP1 = OutProduct([(c_aup, 4)], lambda kt, tt: XT[:, 4 + kt, tt * 128:tt * 128 + 128])
        merged = sem("merged")
        TM1 = Transposes([(lambda tt, k=k: P[:, tt, 3072 + k * 128:3200 + k * 128], XT[:, k, :], None) for k in range(8)])
        OUT1 = OutProduct(c_out1, xt)
        gfin_in, gfin2_in = sem("gfin_in"), sem("gfin2_in")

        SHIFT = O[:, 0, :]
        GAIN = KT[:, 4:8, :].rearrange("p k s -> p (k s)")
        GATE = QT[:, 4:8, :].rearrange("p k s -> p (k s)")
        B_ADA = P[:, 0, 0:3072]
        G_NORM = P[:, 1, 0:1024]
        XN = P[:, :, 3072:4096]

        def plain_finish(get):
            def finish(dve, g):
                for tt in range(TT):
                    last = nc.vector.tensor_tensor(O[:, tt, g * 512:g * 512 + 512].rearrange("p (u d) -> p u d", d=DH),
                                                   get().bank_of(g, tt), per_head(tt, 8, DH), ALU.mult)
                last.then_inc(grouped, 1)
            return finish

        def at(h):
            return h // 2, (h % 2) * 64

        def values(c0, n):
            return lambda kt: P[:, kt, c0:c0 + n]

        A1 = Attention([(at(h), at(h), values(2048 + 64 * h, 64)) for h in range(8)], 64, mask_causal,
                       plain_finish(lambda: A1))

        n2, roped2 = sem("n2"), sem("roped2")
        T2 = Transposes(normed(XT, ("ev_attn", 0)))
        P2 = Project([(c_in2[i], 512, pcol(512 * i, 512), None) for i in range(6)], xt)
        TS2 = Transposes(heads_T([128 * i for i in range(4)], [QT[:, i, :] for i in range(4)], 0.125)
                         + heads_T([512 + 128 * i for i in range(4)], [KT[:, i, :] for i in range(4)], None))
        TD2 = Transposes(heads_T([1536 + 128 * i for i in range(4)], [QT[:, 4 + i, :] for i in range(4)], 0.125)
                         + heads_T([2048 + 128 * i for i in range(4)], [KT[:, 4 + i, :] for i in range(4)], None))
        st_z, st_ln, st_sp, st_r, st_w, st_v, st_done = (sem("st_" + x) for x in ("z", "ln", "sp", "r", "w", "v", "done"))
        lam_dot, lam_exp = sem("lam_dot"), sem("lam_exp")
        cs_ang, cs_set = sem("cs_ang"), sem("cs_set")

        def diff_finish(dve, g):
            odd = rr[:, :, 0:4].rearrange("p t (h m) -> p t h m", m=2)[:, :, :, 1]
            link(dve, nc.vector.tensor_scalar(odd, odd, lam[:, 0:1], None, ALU.mult))
            for tt in range(TT):
                tmp = P[:, tt, 0:512].rearrange("p (u d) -> p u d", d=128)
                link(dve, nc.vector.tensor_tensor(tmp, A2.bank_of(g, tt), per_head(tt, 4, 128), ALU.mult))
                pair = P[:, tt, 0:512].rearrange("p (h m d) -> p h m d", m=2, d=128)
                last = nc.vector.tensor_tensor(O[:, tt, 512 + 256 * g:768 + 256 * g].rearrange("p (h d) -> p h d", d=128),
                                               pair[:, :, 0, :], pair[:, :, 1, :], ALU.add)
            last.then_inc(grouped, 1)
            dve.wait_ge(grouped, A2.g + g + 1)

        A2 = Attention([((4 + u // 2, (u % 2) * 64), (4 + u // 2, (u % 2) * 64), values(2560 + 128 * (u // 2), 128))
                              for u in range(8)], 128, mask_chunk, diff_finish)
        o2 = sem("o2")
        TO2 = Transposes(normed(XT, None))
        OUT2 = OutProduct(c_out2, xt)
        n3 = sem("n3")
        T3 = Transposes(normed(XT, ("ev_ffn", 0)))
        ffn_silu, ffn_mul, ffn_T, ffn_Tc = (sem("ffn_" + x) for x in ("silu", "mul", "T", "Tc"))
        HT = P[:, 0:2, :].rearrange("p t n -> p (t n)")[:, 0:KF * S].rearrange("p (k s) -> p k s", s=S)
        HID = P[:, 0:2, :].rearrange("p t n -> p (t n)")[:, KF * S:KF * S + 4 * 512].rearrange("p (a b n) -> p a b n", a=2, b=2)
        DOWN = OutProduct(c_down, lambda kt, tt: HT[:, kt, tt * 128:tt * 128 + 128])

        n4, roped4 = sem("n4"), sem("roped4")
        T4 = Transposes(normed(XT, ("od_attn", 0)))
        P4 = Project([(c_in3[i], 512, pcol(512 * i, 512), None) for i in range(6)], xt)
        TQ4 = Transposes(heads_T([128 * i for i in range(8)], [QT[:, i, :] for i in range(8)], 0.125)
                         + heads_T([1024 + 128 * i for i in range(8)], [KT[:, i, :] for i in range(8)], None))

        def rel_extra(i, t0, out):
            bias = slot_ap(c_rel, 16, 256)[:, i, :]
            nc.tensor.matmul(out, ident[:, :], bias[:, 128:256] if t0 == 0 else bias, start=False, stop=False,
                             skip_group_check=True)

        A4 = Attention([(at(h), at(h), values(2048 + 64 * h, 64)) for h in range(16)], 64, mask_chunk,
                       plain_finish(lambda: A4), rel_extra)
        TO4 = Transposes(normed(XT, None))
        OUT4 = OutProduct(c_out3, xt)
        n5 = sem("n5")
        T5 = Transposes(normed(XT, ("od_ffn", 0)))

        lg_ps, lg_exp, lg_exped, picked, cnt_ps, list_set = (sem("moe_" + x) for x in
                                                            ("lg", "lgexp", "lgexped", "picked", "cnt", "list"))
        m_sel, m_x, m_xa, m_xd, m_ct, m_ctc = (sem("m_" + x) for x in ("sel", "x", "xa", "xd", "ct", "ctc"))
        m_silu, m_mul, m_T, m_Tc = (sem("m_" + x) for x in ("silu", "mul", "T", "Tc"))
        m_y, m_ya, m_yd, m_s, m_acc = (sem("m_" + x) for x in ("y", "ya", "yd", "s", "acc"))
        flatP = P[:, :, :].rearrange("p t n -> p (t n)")
        at_ = [0]

        def pview(n):
            at_[0] += n
            return flatP[:, at_[0] - n:at_[0]]

        MHT = pview(28 * 128).rearrange("p (k s) -> p k s", s=128)
        MXT = pview(8 * 128).rearrange("p (k s) -> p k s", s=128)
        MHID = pview(4 * 512).rearrange("p (a b n) -> p a b n", a=2, b=2)
        MY = pview(D)
        MSEL = pview(2 * 128).rearrange("p (t s) -> p t s", t=2)
        MSELG = pview(2 * 128).rearrange("p (t s) -> p t s", t=2)
        MCOMB = pview(S)
        IOTA = pview(128)
        LG = pview(2 * NEXP).rearrange("p (t e) -> p t e", t=2)
        MASK = pview(2 * NEXP).rearrange("p (t e) -> p t e", t=2)
        OH1 = pview(2 * NEXP).rearrange("p (t e) -> p t e", t=2)
        OH2 = pview(2 * NEXP).rearrange("p (t e) -> p t e", t=2)
        GW = pview(2 * NEXP).rearrange("p (t e) -> p t e", t=2)
        KEY = pview(2 * NEXP).rearrange("p (t e) -> p t e", t=2)
        TMP = pview(2 * NEXP).rearrange("p (t e) -> p t e", t=2)
        IDX = pview(NEXP)
        RIDX = pview(NEXP)
        MM = pview(8).rearrange("p (t k) -> p t k", t=2)
        CNT = pview(NEXP)
        TE = pview(NEXP)
        CUM = pview(NEXP)
        WIDX = pview(TILE_MAX)
        WE = pview(TILE_MAX * NEXP).rearrange("p (w e) -> p w e", w=TILE_MAX)
        WE2 = pview(TILE_MAX * NEXP).rearrange("p (w e) -> p w e", w=TILE_MAX)
        EW = pview(TILE_MAX)
        JW = pview(TILE_MAX)
        KS = pview(2 * TILE_MAX).rearrange("p (t w) -> p t w", t=2)
        GSEL = pview(2 * TILE_MAX).rearrange("p (t w) -> p t w", t=2)
        WI = pview(2 * TILE_MAX * NEXP).rearrange("p (t w e) -> p t w e", t=2, w=TILE_MAX)
        WORK = pview(TILE_MAX + 1).bitcast(I32)
        iota_set = sem("iota_set")
        p_free = sem("p_free")

        n6 = sem("n6")
        T6 = Transposes(normed(XT, ("norm3", 0)))
        P6 = Project([(c_in4[i], 512, pcol(512 * i, 512), None) for i in range(6)]
                     + [(c_f, 16, pcol(3072, 16), None)]
                     + [(c_z4[i], 512, pcol(3584 + 512 * i, 512), ACT.Silu) for i in range(2)], xt)
        TQ6 = Transposes(heads_T([128 * i for i in range(8)], [QT[:, i, :] for i in range(8)], 0.125)
                         + heads_T([1024 + 128 * i for i in range(8)], [KT[:, i, :] for i in range(8)], None))
        f_in, f_ln, f_log, f_c, f_cc = (sem("f_" + x) for x in ("in", "ln", "log", "c", "cc"))
        FX = P[:, :, 3072:3088]
        FA = P[:, :, 3088:3104]
        FC = P[0:16, 0, 4608:4608 + S]

        def fox_extra(i, t0, out):
            nc.tensor.matmul(out, ident[0:16, i:i + 1].to_broadcast([16, 128]), FC[:, 0:128 + 128 * t0], start=False,
                             stop=False, skip_group_check=True)

        A6 = Attention([(at(h), at(h), values(2048 + 64 * h, 64)) for h in range(16)], 64, mask_causal,
                       plain_finish(lambda: A6), fox_extra)
        g6 = sem("g6")
        TO6 = Transposes(normed(XT, None))
        OUT6 = OutProduct(c_out4, xt)

        n7, roped7 = sem("n7"), sem("roped7")
        T7 = Transposes(normed(XT, ("norm3", 8)))
        P7 = Project([(c_in5[i], 512, pcol(512 * i, 512), None) for i in range(5)]
                     + [(c_g5, 48, pcol(2560, 48), ACT.Sigmoid)]
                     + [(c_z5[i], 512, pcol(3072 + 512 * i, 512), ACT.Silu) for i in range(2)], xt)

        twice_p = lambda n: (lambda tt: P[:, tt, 4096 + 128 * n:4224 + 128 * n])
        twice_o = lambda n: (lambda tt: O[:, tt, 128 * n:128 * n + 128])
        TQ7 = Transposes(heads_T([128 * i for i in range(8)], [QT[:, i, :] for i in range(8)], 0.125)
                         + [(twice_p(n), KT[:, n, :], None) for n in range(8)])
        c_T, c_A = sem("c_T"), sem("c_A")
        c_s, c_hT, c_hTc, c_roped, c_kT, c_kTc = (sem("cmp_" + x) for x in ("s", "hT", "hTc", "roped", "kT", "kTc"))
        q_s, q_m, q_e, q_p, q_T, q_Tc, q_v, q_o = (sem("cq_" + x) for x in ("s", "m", "e", "p", "T", "Tc", "v", "o"))
        block_tiles = lambda i, j: (P[:, j, 4096:5120].rearrange("p (k r) -> p k r", k=8) if i == 0
                                    else XT[:, 4 * j:4 * j + 4, :].rearrange("p k s -> p (k s)").rearrange("p (k r) -> p k r", k=8))
        CH = [scr[:, 0:256], scr[:, 256:512]]
        CHT = [scr[:, 512 + 256 * i:768 + 256 * i].rearrange("p (k r) -> p k r", k=2) for i in range(2)]
        KCN = scr[:, 1024:1152].rearrange("p (a d) -> p a d", a=2)
        KCT = scr[:, 1152:1280]
        VCB = scr[:, 1280:1536]
        CS, CPT = scr[:, 0:512], scr[:, 512:1024]

        def nsa_finish(dve, g):
            branch, h0 = 1 + g // 2, (g % 2) * 8
            gates = P[:, :, 2560:2608].rearrange("p t (h b) -> p t h b", b=3)[:, :, h0:h0 + 8, branch]
            link(dve, nc.vector.tensor_tensor(rr[:, :, :], rr[:, :, :], gates, ALU.mult))
            for tt in range(TT):
                tmp = P[:, tt, 4096:4608].rearrange("p (u d) -> p u d", d=DH)
                link(dve, nc.vector.tensor_tensor(tmp, A7.bank_of(g, tt), per_head(tt, 8, DH), ALU.mult))
                o = O[:, tt, h0 * 64:h0 * 64 + 512].rearrange("p (u d) -> p u d", d=DH)
                last = nc.vector.tensor_tensor(o, o, tmp, ALU.add)
            last.then_inc(grouped, 1)
            dve.wait_ge(grouped, A7.g + g + 1)

        def group_key(branch, h):
            return branch * 4 + h // 4, (h % 2) * 64

        A7 = Attention([(at(h), group_key(b, h), values((1792, 2304)[b] + 64 * (h // 4), 64))
                              for b in range(2) for h in range(16)], 64, mask_causal, nsa_finish)
        g7 = sem("g7")
        TO7 = Transposes(normed(XT, None))
        OUT7 = OutProduct(c_out5, xt)
        out_set, out_sent = sem("out_set"), sem("out_sent")

        counts = {"dve": 0, "act": 0}
        moe_tiles = {}

        def link(dve, ins):
            counts["dve"] += 1
            ins.then_inc(dve_chain, 1)
            dve.wait_ge(dve_chain, counts["dve"])

        def link_act(act, ins):
            counts["act"] += 1
            ins.then_inc(act_chain, 1)
            act.wait_ge(act_chain, counts["act"])

        def take(pe, n):
            _, nk, width = stream[n]
            value = 16 * (n // RING + 1)
            if after_moe(n):
                value = moe_tiles[pe.engine] * (16 * MOE_CHUNKS // RING) + value
            pe.wait_ge(landed[n % RING], value)
            return slot_ap(n, nk, width)

        def used(eng, n):
            value = n + 1
            if after_moe(n):
                value = moe_tiles[eng.engine] * MOE_CHUNKS + value
            eng.wait_ge(consumed, value)

        def mean_squares(dve, src, width, out):
            for tt in range(TT):
                last = nc.vector.tensor_tensor_reduce(out=O[:, tt, 0:width], in0=src(tt), in1=src(tt), scale=1.0,
                                                      scalar=0.0, op0=ALU.mult, op1=ALU.add, accum_out=out(tt))
            link(dve, last)

        def inverse_roots(dve, view, width):
            counts["root"] = counts.get("root", 0) + 1
            nc.vector.tensor_scalar(view, view, 1.0 / width, EPS, ALU.mult, ALU.add).then_inc(ss_ready, 1)
            dve.wait_ge(ms_ready, counts["root"])
            link(dve, nc.vector.reciprocal(view, view))

        def roots(act, view):
            counts["act_root"] = counts.get("act_root", 0) + 1
            act.wait_ge(ss_ready, counts["act_root"])
            nc.scalar.activation(view, view, ACT.Sqrt).then_inc(ms_ready, 1)

        def norm(dve, signal):
            mean_squares(dve, lambda tt: X[:, tt, :], D, lambda tt: stat[:, tt:tt + 1])
            inverse_roots(dve, stat[:, 0:2], D)
            for tt in range(TT):
                last = nc.vector.tensor_scalar(O[:, tt, :], X[:, tt, :], stat[:, tt:tt + 1], None, ALU.mult)
            last.then_inc(signal, 1)
            dve.wait_ge(signal, 1)

        def add_to_x(dve, stage):
            stage.wait(dve)
            for tt in range(TT):
                for half in range(2):
                    xs = X[:, tt, half * 512:half * 512 + 512]
                    last = nc.vector.tensor_tensor(xs, bank[2 * tt + half][:, :], xs, ALU.add)
            link(dve, last)

        def rope(dve, view, cos, sin, heads, tiles):
            v = view.rearrange("p t (h d) -> p t h d", d=DH)
            x1, x2 = v[:, :, :, 0:8], v[:, :, :, 8:16]
            n = tiles * heads * 8
            t1, t2, t3, t4 = (scr[:, i * 256:i * 256 + n].rearrange("p (t h d) -> p t h d", t=tiles, d=8) for i in range(4))
            for tt in range(tiles):
                c = cos[:, tt, :].unsqueeze(1).to_broadcast([128, heads, 8])
                s = sin[:, tt, :].unsqueeze(1).to_broadcast([128, heads, 8])
                nc.vector.tensor_tensor(t1[:, tt], x1[:, tt], c, ALU.mult)
                nc.vector.tensor_tensor(t2[:, tt], x2[:, tt], s, ALU.mult)
                nc.vector.tensor_tensor(t3[:, tt], x2[:, tt], c, ALU.mult)
                last = nc.vector.tensor_tensor(t4[:, tt], x1[:, tt], s, ALU.mult)
            link(dve, last)
            for tt in range(tiles):
                nc.vector.tensor_tensor(x1[:, tt], t1[:, tt], t2[:, tt], ALU.subtract)
                last = nc.vector.tensor_tensor(x2[:, tt], t3[:, tt], t4[:, tt], ALU.add)
            link(dve, last)

        def head_norm(dve, c0, gains):
            for tt in range(TT):
                last = nc.vector.tensor_tensor(O[:, tt, :], P[:, tt, c0:c0 + D], P[:, tt, c0:c0 + D], ALU.mult)
            link(dve, last)
            for tt in range(TT):
                last = nc.vector.tensor_reduce(stat[:, 16 + 16 * tt:32 + 16 * tt],
                                               O[:, tt, :].rearrange("p (h d) -> p h d", d=DH), AX.X, ALU.add)
            link(dve, last)
            inverse_roots(dve, stat[:, 16:48], DH)
            for tt in range(TT):
                v = P[:, tt, c0:c0 + D].rearrange("p (h d) -> p h d", d=DH)
                last = nc.vector.tensor_tensor(v, v, stat[:, 16 + 16 * tt:32 + 16 * tt].unsqueeze(2).to_broadcast([128, 16, DH]),
                                               ALU.mult)
            link(dve, last)
            for tt in range(TT):
                for h, n, name in gains:
                    v = P[:, tt, c0 + h * DH:c0 + (h + n) * DH].rearrange("p (h d) -> p h d", d=DH)
                    last = nc.vector.tensor_tensor(v, v, row(name).unsqueeze(1).to_broadcast([128, n, DH]), ALU.mult)
            link(dve, last)

        cos0 = con("cos").rearrange("p (t d) -> p t d", d=8)
        sin0 = con("sin").rearrange("p (t d) -> p t d", d=8)
        cos2 = cs2[:, 0, :].rearrange("p (t d) -> p t d", d=8)
        sin2 = cs2[:, 1, :].rearrange("p (t d) -> p t d", d=8)

        def ffn_copy(eng, f):
            tiles_ = ff[f][1] // 128
            eng.wait_ge(ffn_T, f + 1)
            for b in range(tiles_ // 2):
                last = nc.scalar.activation(HT[:, 4 * f + 2 * b:4 * f + 2 * b + 2, :],
                                            bank[4 + b][:, :].rearrange("p (k s) -> p k s", s=S), ACT.Copy)
            last.then_inc(ffn_Tc, 1)

        def moe_copy(eng, w, f):
            eng.wait_ge(m_T, w * CF + f + 1)
            nc.scalar.activation(MHT[:, 4 * f:4 * f + 4, :], bank[4 + f % 2][:, :].rearrange("p (k s) -> p k s", s=128),
                                 ACT.Copy).then_inc(m_Tc, 1)

        block = ctx.enter_context(nc.Block())

        @block.sync
        def _(sp):
            def load(n):
                ap, nk, width = stream[n]
                if n >= RING:
                    value = n - RING + 1
                    if after_moe(n):
                        value = moe_tiles[sp.engine] * MOE_CHUNKS + value
                    sp.wait_ge(consumed, value)
                sp.dma_start(slot_ap(n, nk, width), ap).then_inc(landed[n % RING], 16)

            for n in range(N0):
                load(n)
            sp.wait_ge(list_set, 1)
            tiles = sp.value_load(WORK[0:1, TILE_MAX:TILE_MAX + 1], min_val=4, max_val=TILE_MAX)
            moe_tiles[sp.engine] = tiles
            gate, up, down = (t[n][0] for n in ("od_we_gate_2", "od_we_up_2", "od_we_down_2"))
            with sp.Fori(0, tiles) as i:
                e = sp.value_load(WORK[0:1, bass.ds(i, 1)], min_val=0, max_val=NEXP - 1)
                for c in range(MOE_CHUNKS):
                    n = N0 + c
                    sp.wait_ge(consumed, i * MOE_CHUNKS + (n - RING + 1))
                    if c < 2 * CF:
                        src = (up if c % 2 else gate)[bass.ds(e, 1), :, 512 * (c // 2):512 * (c // 2) + 512]
                        src = src.rearrange("e (k p) n -> p (e k) n", p=128)
                        dst = slot_ap(n, 8, 512)
                    else:
                        k0 = 4 * (c - 2 * CF)
                        src = down[bass.ds(e, 1), k0 * 128:(k0 + 4) * 128, :].rearrange("e (k p) n -> p (e k) n", p=128)
                        dst = slot_ap(n, 4, D)
                    sp.dma_start(dst, src).then_inc(landed[n % RING], 16)
            for n in range(N0, len(stream)):
                load(n)
            sp.wait_ge(out_set, 1)
            sp.dma_start(t["out"].rearrange("b (t p) n -> p (b t) n", p=128), X[:, :, :]).then_inc(out_sent, 16)
            sp.wait_ge(out_sent, 16)

        @block.gpsimd
        def _(pool):
            for tile, value in ((ident, 0.0), (identb, 0.0), (mask_causal, 0.0), (mask_chunk, 0.0), (mask_past, 0.0),
                                (past01, 1.0), (neg_tri, -1.0), (neg_ones, -1.0), (ones, 1.0)):
                nc.gpsimd.memset(tile[:, :], value).then_inc(ones_set, 1)
            pool.wait_ge(ones_set, 9)

            def select(tile, step, base, multiplier, op, fill):
                nc.gpsimd.affine_select(out=tile[:, :], in_=tile[:, :], compare_op=op, fill=fill, base=base,
                                        pattern=[[step, 128]], channel_multiplier=multiplier).then_inc(const_set, 1)

            select(ident, -1, 0, 1, ALU.not_equal, 1.0)
            select(identb, -1, 0, 1, ALU.not_equal, 1.0)
            select(mask_causal, -1, 0, 1, ALU.is_ge, -BIG)
            select(mask_past, 1, 0, -1, ALU.is_gt, -BIG)
            select(past01, 1, 0, -1, ALU.is_gt, 0.0)
            select(neg_tri, -1, 0, 1, ALU.is_ge, 0.0)
            nc.gpsimd.memset(mask_chunk[0:64, 64:128], -BIG).then_inc(const_set, 1)
            pool.wait_ge(p_free, 1)
            nc.gpsimd.iota(IOTA, pattern=[[1, 128]], base=0, channel_multiplier=0,
                           allow_small_or_imprecise_dtypes=True).then_inc(iota_set, 1)
            nc.gpsimd.iota(IDX, pattern=[[1, NEXP]], base=0, channel_multiplier=0,
                           allow_small_or_imprecise_dtypes=True).then_inc(iota_set, 1)
            nc.gpsimd.iota(WIDX, pattern=[[1, TILE_MAX]], base=0, channel_multiplier=0,
                           allow_small_or_imprecise_dtypes=True).then_inc(iota_set, 1)
            pool.wait_ge(iota_set, 3)

        N_CONST = 7

        @block.scalar
        def _(act):
            act.dma_start(X[:, :, :], t["x"].rearrange("b (t p) n -> p (b t) n", p=128)).then_inc(small_in, 16)
            act.dma_start(O[0:NVEC, 1, 0:128], t["vec"]).then_inc(small_in, 16)
            act.dma_start(small[:, :], t["small"].partition_broadcast(128)).then_inc(small_in, 16)
            act.dma_start(co[:, :], t["co"]).then_inc(small_in, 16)
            act.dma_start(B_ADA, t["b_ada"].rearrange("a n -> (a n)").partition_broadcast(128)).then_inc(small_in, 16)
            act.dma_start(G_NORM, t["g_norm"].rearrange("a n -> (a n)").partition_broadcast(128)).then_inc(small_in, 16)
            with nc.allow_non_contiguous_dma(reason="256 positions"):
                act.dma_start(posi[:, :], t["positions_2"].rearrange("b (t p) -> p (b t)", p=128)).then_inc(small_in, 16)

            roots(act, stat[:, 0:2])
            T1.act(act)
            P1.act(act)
            TQ1.act(act)
            A1.act(act)
            TY1.act(act)
            TA1.act(act)
            act.wait_ge(h1, 1)
            act.dma_start(GAIN, t["g_final"].partition_broadcast(128)).then_inc(gfin_in, 16)
            TM1.act(act)
            roots(act, stat[:, 0:2])

            roots(act, stat[:, 0:2])
            T2.act(act)
            P2.act(act)
            act.wait_ge(cs_ang, 1)
            link_act(act, nc.scalar.activation(cs2[:, 0, :], cs2[:, 0, :], ACT.Sin))
            nc.scalar.activation(cs2[:, 1, :], cs2[:, 1, :], ACT.Sin).then_inc(cs_set, 1)
            act.wait_ge(lam_dot, 1)
            nc.scalar.activation(lam[:, 2:4], lam[:, 2:4], ACT.Exp).then_inc(lam_exp, 1)
            TS2.act(act)
            roots(act, stat[:, 16:48])
            TD2.act(act)
            for i in range(9):
                if i < 8:
                    act.wait_ge(st_z, i + 1)
                    if i >= 2:
                        act.wait_ge(st_r, i - 1)
                    e = E[i % 2]
                    link_act(act, nc.scalar.activation(e, bank[4 + i % 2][:, 0:384], ACT.Abs))
                    link_act(act, nc.scalar.activation(e, e, ACT.Exp, scale=-1.0))
                    nc.scalar.activation(e, e, ACT.Ln, bias=1.0).then_inc(st_ln, 1)
                if i >= 1:
                    j = i - 1
                    act.wait_ge(st_r, j + 1)
                    if j >= 2:
                        act.wait_ge(st_v, j - 1)
                    nc.scalar.activation(PT[j % 2], bank[6 + j % 2][:, 0:384], ACT.Exp).then_inc(st_w, 1)
            A2.act(act)
            roots(act, stat[:, 8:16])
            TO2.act(act)
            roots(act, stat[:, 0:2])
            T3.act(act)
            for f, (c0, n) in enumerate(ff):
                for tt in range(TT):
                    g = 2 * f + tt
                    used(act, c_ff[f][0])
                    if g >= 4:
                        act.wait_ge(ffn_T, f - 1)
                    nc.scalar.activation(HID[:, f % 2, tt, 0:n], bank[tt][:, 0:n], ACT.Silu).then_inc(ffn_silu, 1)
                if f >= 1:
                    ffn_copy(act, f - 1)
            ffn_copy(act, len(ff) - 1)

            roots(act, stat[:, 0:2])
            T4.act(act)
            P4.act(act)
            roots(act, stat[:, 16:48])
            roots(act, stat[:, 16:48])
            TQ4.act(act)
            A4.act(act)
            TO4.act(act)
            roots(act, stat[:, 0:2])
            T5.act(act)
            act.wait_ge(lg_exp, 1)
            nc.scalar.activation(MM[:, :, 2], MM[:, :, 2], ACT.Exp).then_inc(lg_exped, 1)

            act.wait_ge(list_set, 1)
            tiles = act.value_load(WORK[0:1, TILE_MAX:TILE_MAX + 1], min_val=4, max_val=TILE_MAX)
            moe_tiles[act.engine] = tiles
            with act.Fori(0, tiles) as w:
                act.wait_ge(m_x, w * 2 + 1)
                for k in range(4):
                    last = nc.scalar.activation(MXT[:, k, :], bank[4][:, k * 128:k * 128 + 128], ACT.Copy,
                                                scale=col("od_ffn", k))
                last.then_inc(m_xa, 1)
                for f in range(CF):
                    act.wait_ge(consumed, w * MOE_CHUNKS + (N0 + 2 * f + 1))
                    nc.scalar.activation(MHID[:, f % 2, 0, :], bank[f % 2 * 2][:, :], ACT.Silu).then_inc(m_silu, 1)
                    if f >= 1:
                        moe_copy(act, w, f - 1)
                moe_copy(act, w, CF - 1)
                act.wait_ge(consumed, w * MOE_CHUNKS + (N0 + MOE_CHUNKS))
                nc.scalar.activation(MY[:, 0:512], bank[6][:, :], ACT.Copy).then_inc(m_ya, 1)

            roots(act, stat[:, 0:2])
            T6.act(act)
            P6.act(act)
            act.wait_ge(f_in, 1)
            link_act(act, nc.scalar.activation(FA, FX, ACT.Abs))
            link_act(act, nc.scalar.activation(FA, FA, ACT.Exp, scale=-1.0))
            nc.scalar.activation(FA, FA, ACT.Ln, bias=1.0).then_inc(f_ln, 1)
            TQ6.act(act)
            A6.act(act)
            TO6.act(act)

            roots(act, stat[:, 0:2])
            T7.act(act)
            P7.act(act)
            TQ7.act(act)
            for i in range(2):
                used(act, c_ck[i][0])
                nc.scalar.activation(CH[i], bank[i][:, 0:256], ACT.Silu).then_inc(c_s, 1)
            for tt in range(TT):
                act.wait_ge(q_m, tt + 1)
                nc.scalar.activation(CS, CS, ACT.Exp).then_inc(q_e, 1)
            A7.act(act)
            A7.wait(act)
            act.dma_start(GAIN, t["final_g_3"].partition_broadcast(128)).then_inc(gfin2_in, 16)
            TO7.act(act)
            roots(act, stat[:, 0:2])

        @block.vector
        def _(dve):
            dve.wait_ge(small_in, 16 * 7)
            dve.wait_ge(const_set, N_CONST)
            dve.wait_ge(vec_ready, 1)
            link(dve, nc.vector.tensor_copy(vec[:, :], bank[7][:, 0:NVEC]))
            nc.vector.tensor_copy(scr[:, 0:1024].rearrange("p (k m) -> p k m", k=8),
                                  vec[:, VEC_ROWS["c"][0]:VEC_ROWS["c"][0] + 8].unsqueeze(2).to_broadcast([128, 8, 128])
                                  ).then_inc(vec_set, 1)
            for m in range(6):
                used(dve, c_ada[m])
                b = B_ADA[:, 512 * m:512 * m + 512]
                half = slice(512 * (m % 2), 512 * (m % 2) + 512)
                ps = bank[m % 4][:, :]
                dest = (SHIFT, GAIN, GATE)[m // 2][:, half]
                ins = nc.vector.tensor_tensor(dest, ps, b, ALU.add)
                ins.then_inc(ada_used, 1)
                if m // 2 == 1:
                    dve.wait_ge(ada_used, m + 1)
                    link(dve, nc.vector.scalar_tensor_tensor(out=dest, in0=dest, scalar=1.0, in1=G_NORM[:, half],
                                                             op0=ALU.add, op1=ALU.mult))
            dve.wait_ge(ada_used, 6)
            for tt in range(TT):
                last = nc.vector.tensor_tensor_reduce(out=XN[:, tt, :], in0=X[:, tt, :], in1=X[:, tt, :], scale=1.0,
                                                      scalar=0.0, op0=ALU.mult, op1=ALU.add, accum_out=stat[:, tt:tt + 1])
            link(dve, last)
            inverse_roots(dve, stat[:, 0:2], D)
            for tt in range(TT):
                last = nc.vector.scalar_tensor_tensor(out=XN[:, tt, :], in0=X[:, tt, :], scalar=stat[:, tt:tt + 1],
                                                      in1=GAIN, op0=ALU.mult, op1=ALU.mult)
            link(dve, last)
            link(dve, nc.vector.tensor_tensor(O[:, 1, :], XN[:, 1, :], SHIFT, ALU.add))
            nc.vector.tensor_tensor(O[:, 0, :], XN[:, 0, :], SHIFT, ALU.add).then_inc(h1, 1)
            T1.dve(dve)
            P1.dve(dve)
            P1.wait(dve)
            rope(dve, P[:, :, 1024:2048], cos0, sin0, 16, TT)
            dve.sem_inc(roped1, 1)
            TQ1.dve(dve)
            A1.dve(dve)
            A1.wait(dve)
            last = nc.vector.tensor_tensor(O[:, :, 0:512], O[:, :, 0:512], P[:, :, 2560:3072], ALU.mult)
            last.then_inc(gated1, 1)
            used(dve, c_band)
            for g in range(4):
                last = nc.vector.tensor_copy(scr[:, 256 * g:256 * g + 256], bank[4 + g // 2][:, 256 * (g % 2):256 * (g % 2) + 256])
            last.then_inc(d_copied, 1)
            used(dve, c_grp)
            for tt in range(TT):
                last = nc.vector.tensor_tensor(P[:, tt, 0:512], bank[2 + tt][:, :], P[:, tt, 512:1024], ALU.mult)
            last.then_inc(y_gated, 1)
            TY1.dve(dve)
            TA1.dve(dve)
            for stage, c0 in ((UP1, 3072), (AUP1, 4096)):
                stage.wait(dve)
                for tt in range(TT):
                    for half in range(2):
                        m = P[:, tt, c0 + half * 512:c0 + half * 512 + 512]
                        last = nc.vector.tensor_tensor(m, bank[2 * tt + half][:, :], m, ALU.mult)
                last.then_inc(up_used, 1)
            dve.wait_ge(up_used, 2)
            nc.vector.tensor_tensor(P[:, :, 3072:4096], P[:, :, 3072:4096], P[:, :, 4096:5120], ALU.add).then_inc(merged, 1)
            TM1.dve(dve)
            OUT1.wait(dve)
            for tt in range(TT):
                for half in range(2):
                    last = nc.vector.tensor_tensor(O[:, tt, half * 512:half * 512 + 512], bank[2 * tt + half][:, :],
                                                   GATE[:, half * 512:half * 512 + 512], ALU.mult)
            link(dve, last)
            link(dve, nc.vector.tensor_tensor(X[:, :, :], X[:, :, :], O[:, :, :], ALU.add))
            mean_squares(dve, lambda tt: X[:, tt, :], D, lambda tt: stat[:, tt:tt + 1])
            inverse_roots(dve, stat[:, 0:2], D)
            dve.wait_ge(gfin_in, 16)
            for tt in range(TT):
                last = nc.vector.scalar_tensor_tensor(out=X[:, tt, :], in0=X[:, tt, :], scalar=stat[:, tt:tt + 1],
                                                      in1=GAIN, op0=ALU.mult, op1=ALU.mult)
            link(dve, last)

            norm(dve, n2)
            T2.dve(dve)
            P2.dve(dve)
            P2.wait(dve)
            posf, ang, turns = stat[:, 48:50], cs2[:, 2, :], cs2[:, 3, :]
            link(dve, nc.vector.tensor_copy(posf, posi[:, :]))
            for tt in range(TT):
                last = nc.vector.tensor_scalar(ang[:, 8 * tt:8 * tt + 8], con("invf"), posf[:, tt:tt + 1], None, ALU.mult)
            link(dve, last)
            magic, two_pi = 12582912.0, 2.0 * np.pi
            hi = 6.28125
            mid = round((two_pi - hi) * 2 ** 24) / 2 ** 24
            lo = two_pi - hi - mid
            for k, quarter in ((0, 0.25), (1, 0.0)):
                r = cs2[:, k, :]
                link(dve, nc.vector.tensor_scalar(turns, ang, float(1.0 / two_pi), quarter, ALU.mult, ALU.add))
                link(dve, nc.vector.tensor_scalar(turns, turns, magic, None, ALU.add))
                link(dve, nc.vector.tensor_scalar(turns, turns, magic, None, ALU.subtract))
                link(dve, nc.vector.scalar_tensor_tensor(out=r, in0=turns, scalar=-hi, in1=ang, op0=ALU.mult, op1=ALU.add))
                link(dve, nc.vector.scalar_tensor_tensor(out=r, in0=turns, scalar=-mid, in1=r, op0=ALU.mult, op1=ALU.add))
                link(dve, nc.vector.scalar_tensor_tensor(out=r, in0=turns, scalar=-lo, in1=r, op0=ALU.mult, op1=ALU.add))
                if quarter:
                    link(dve, nc.vector.tensor_scalar(r, r, float(np.pi / 2), None, ALU.add))
                last = nc.vector.tensor_scalar(r, r, 3.1415925, -3.1415925, ALU.min, ALU.max)
                if k == 0:
                    link(dve, last)
            last.then_inc(cs_ang, 1)
            for k, (a, b) in enumerate((("lq1", "lk1"), ("lq2", "lk2"))):
                last = nc.vector.tensor_tensor_reduce(out=scr[:, 64 * k:64 * k + 64], in0=row(a), in1=row(b), scale=1.0,
                                                      scalar=0.0, op0=ALU.mult, op1=ALU.add, accum_out=lam[:, 2 + k:3 + k])
            last.then_inc(lam_dot, 1)
            dve.wait_ge(lam_exp, 1)
            link(dve, nc.vector.tensor_tensor(lam[:, 0:1], lam[:, 3:4], lam[:, 2:3], ALU.subtract))
            link(dve, nc.vector.tensor_scalar(lam[:, 0:1], lam[:, 0:1], -LAM_INIT, None, ALU.add))
            TS2.dve(dve)
            head_norm(dve, 1536, [(0, 8, "ev_q"), (8, 8, "ev_k")])
            dve.wait_ge(cs_set, 1)
            rope(dve, P[:, :, 1536:2560], cos2, sin2, 16, TT)
            dve.sem_inc(roped2, 1)
            TD2.dve(dve)
            for i in range(8):
                dve.wait_ge(st_ln, i + 1)
                e = E[i % 2]
                link(dve, nc.vector.scalar_tensor_tensor(out=e, in0=bank[4 + i % 2][:, 0:384], scalar=0.0, in1=e,
                                                         op0=ALU.max, op1=ALU.add))
                nc.vector.tensor_tensor(e[:, 0:128], e[:, 0:128], past01[:, :], ALU.mult)
                nc.vector.tensor_tensor(e[:, 256:384], e[:, 256:384], past01[:, :], ALU.mult).then_inc(st_sp, 1)
            dve.wait_ge(st_v, 8)
            for tt in range(TT):
                last = nc.vector.tensor_copy(O[:, tt, 0:512], bank[tt][:, :])
            last.then_inc(st_done, 1)
            A2.dve(dve)
            A2.wait(dve)
            for tt in range(TT):
                last = nc.vector.tensor_tensor(P[:, tt, 0:512], O[:, tt, 512:1024], O[:, tt, 512:1024], ALU.mult)
            link(dve, last)
            for tt in range(TT):
                last = nc.vector.tensor_reduce(stat[:, 8 + 4 * tt:12 + 4 * tt],
                                               P[:, tt, 0:512].rearrange("p (h d) -> p h d", d=128), AX.X, ALU.add)
            link(dve, last)
            inverse_roots(dve, stat[:, 8:16], 128)
            link(dve, nc.vector.tensor_scalar(stat[:, 8:16], stat[:, 8:16], 1.0 - LAM_INIT, None, ALU.mult))
            for tt in range(TT):
                v = O[:, tt, 512:1024].rearrange("p (h d) -> p h d", d=128)
                last = nc.vector.tensor_tensor(v, v, stat[:, 8 + 4 * tt:12 + 4 * tt].unsqueeze(2).to_broadcast([128, 4, 128]),
                                               ALU.mult)
            link(dve, last)
            for tt in range(TT):
                v = O[:, tt, 512:1024].rearrange("p (h d) -> p h d", d=128)
                last = nc.vector.tensor_tensor(v, v, row("subln").unsqueeze(1).to_broadcast([128, 4, 128]), ALU.mult)
            last.then_inc(o2, 1)
            TO2.dve(dve)
            add_to_x(dve, OUT2)
            TO2.wait(dve)
            norm(dve, n3)
            T3.dve(dve)
            for f, (c0, n) in enumerate(ff):
                for tt in range(TT):
                    dve.wait_ge(ffn_silu, 2 * f + tt + 1)
                    used(dve, c_ff[f][1])
                    h = HID[:, f % 2, tt, 0:n]
                    nc.vector.tensor_tensor(h, bank[2 + tt][:, 0:n], h, ALU.mult).then_inc(ffn_mul, 1)
            add_to_x(dve, DOWN)

            norm(dve, n4)
            T4.dve(dve)
            P4.dve(dve)
            P4.wait(dve)
            head_norm(dve, 0, [(0, 16, "od_q")])
            head_norm(dve, 1024, [(0, 16, "od_k")])
            dve.sem_inc(roped4, 1)
            TQ4.dve(dve)
            A4.dve(dve)
            A4.wait(dve)
            TO4.dve(dve)
            add_to_x(dve, OUT4)
            TO4.wait(dve)
            nc.vector.memset(stat[:, 60:61], 0.0).then_inc(p_free, 1)
            norm(dve, n5)
            T5.dve(dve)

            dve.wait_ge(iota_set, 3)
            used(dve, c_router)
            link(dve, nc.vector.tensor_copy(LG, bank[0][:, 0:2 * NEXP].rearrange("p (t e) -> p t e", t=2)))
            link(dve, nc.vector.tensor_scalar(RIDX, IDX, -1.0, float(NEXP), ALU.mult, ALU.add))
            ridx = RIDX.unsqueeze(1).to_broadcast([128, 2, NEXP])

            def spread(v):
                return v.unsqueeze(2).to_broadcast([128, 2, NEXP])

            for oh, top in ((OH1, MM[:, :, 0]), (OH2, MM[:, :, 1])):
                link(dve, nc.vector.tensor_reduce(top, LG, AX.X, ALU.max))
                link(dve, nc.vector.tensor_tensor(TMP, LG, spread(top), ALU.is_equal))
                link(dve, nc.vector.tensor_tensor(TMP, TMP, ridx, ALU.mult))
                link(dve, nc.vector.tensor_reduce(MM[:, :, 3], TMP, AX.X, ALU.max))
                link(dve, nc.vector.tensor_tensor(oh, ridx, spread(MM[:, :, 3]), ALU.is_equal))
                if oh is OH1:
                    link(dve, nc.vector.scalar_tensor_tensor(out=LG, in0=oh, scalar=-BIG, in1=LG, op0=ALU.mult, op1=ALU.add))
            nc.vector.tensor_tensor(MM[:, :, 2], MM[:, :, 1], MM[:, :, 0], ALU.subtract).then_inc(lg_exp, 1)
            link(dve, nc.vector.tensor_tensor(MASK, OH1, OH2, ALU.add))
            dve.sem_inc(picked, 1)
            dve.wait_ge(lg_exped, 1)
            link(dve, nc.vector.tensor_scalar(MM[:, :, 3], MM[:, :, 2], 1.0, None, ALU.add))
            link(dve, nc.vector.reciprocal(MM[:, :, 3], MM[:, :, 3]))
            link(dve, nc.vector.tensor_tensor(MM[:, :, 2], MM[:, :, 2], MM[:, :, 3], ALU.mult))
            link(dve, nc.vector.tensor_tensor(GW, OH1, spread(MM[:, :, 3]), ALU.mult))
            link(dve, nc.vector.tensor_tensor(TMP, OH2, spread(MM[:, :, 2]), ALU.mult))
            link(dve, nc.vector.tensor_tensor(GW, GW, TMP, ALU.add))
            dve.wait_ge(cnt_ps, 1)
            link(dve, nc.vector.tensor_copy(KEY, bank[1][:, 0:16].rearrange("p (t e) -> p t e", t=2)))
            link(dve, nc.vector.tensor_copy(CNT, bank[2][:, 0:NEXP]))
            link(dve, nc.vector.scalar_tensor_tensor(out=KEY, in0=KEY, scalar=1000.0, in1=MASK, op0=ALU.add, op1=ALU.mult))
            link(dve, nc.vector.tensor_scalar(KEY, KEY, -1000.0, None, ALU.add))
            link(dve, nc.vector.tensor_scalar(TE, CNT, 0.5, None, ALU.is_gt))
            link(dve, nc.vector.scalar_tensor_tensor(out=TE, in0=CNT, scalar=128.5, in1=TE, op0=ALU.is_gt, op1=ALU.add))
            link(dve, nc.vector.tensor_copy(CUM, TE))
            for e in range(1, NEXP):
                link(dve, nc.vector.tensor_tensor(CUM[:, e:e + 1], CUM[:, e:e + 1], CUM[:, e - 1:e], ALU.add))
            over_e = [128, TILE_MAX, NEXP]
            wide = WIDX.unsqueeze(2).to_broadcast(over_e)
            link(dve, nc.vector.tensor_tensor(WE, CUM.unsqueeze(1).to_broadcast(over_e), wide, ALU.is_le))
            link(dve, nc.vector.tensor_reduce(EW, WE, AX.X, ALU.add))
            link(dve, nc.vector.tensor_tensor(WE2, WE, TE.unsqueeze(1).to_broadcast(over_e), ALU.mult))
            link(dve, nc.vector.tensor_reduce(JW, WE2, AX.X, ALU.add))
            link(dve, nc.vector.tensor_tensor(JW, WIDX, JW, ALU.subtract))
            link(dve, nc.vector.tensor_scalar(JW, JW, 128.0, None, ALU.mult))
            link(dve, nc.vector.tensor_tensor(WE, IDX.unsqueeze(1).to_broadcast(over_e), EW.unsqueeze(2).to_broadcast(over_e),
                                              ALU.is_equal))
            for tt in range(TT):
                for src, dest in ((KEY, KS), (GW, GSEL)):
                    link(dve, nc.vector.tensor_tensor(WI[:, tt], WE, src[:, tt, :].unsqueeze(1).to_broadcast(over_e), ALU.mult))
                    link(dve, nc.vector.tensor_reduce(dest[:, tt, :], WI[:, tt], AX.X, ALU.add))
                link(dve, nc.vector.tensor_tensor(KS[:, tt, :], KS[:, tt, :], JW, ALU.subtract))
            link(dve, nc.vector.tensor_copy(WORK[:, 0:TILE_MAX], EW))
            nc.vector.tensor_copy(WORK[:, TILE_MAX:TILE_MAX + 1], CUM[:, NEXP - 1:NEXP]).then_inc(list_set, 1)

            dve.wait_ge(list_set, 1)
            tiles = dve.value_load(WORK[0:1, TILE_MAX:TILE_MAX + 1], min_val=4, max_val=TILE_MAX)
            moe_tiles[dve.engine] = tiles
            with dve.Fori(0, tiles) as w:
                for tt in range(TT):
                    nc.vector.tensor_scalar(MSEL[:, tt, :], IOTA, KS[:, tt, bass.ds(w, 1)], None, ALU.is_equal)
                    last = nc.vector.tensor_scalar(MSELG[:, tt, :], IOTA, KS[:, tt, bass.ds(w, 1)],
                                                   GSEL[:, tt, bass.ds(w, 1)], ALU.is_equal, ALU.mult)
                last.then_inc(m_sel, 1)
                dve.wait_ge(m_x, w * 2 + 2)
                for k in range(4, 8):
                    last = nc.vector.tensor_scalar(MXT[:, k, :], bank[5][:, (k - 4) * 128:(k - 4) * 128 + 128],
                                                   col("od_ffn", k), None, ALU.mult)
                last.then_inc(m_xd, 1)
                dve.wait_ge(m_ct, w + 1)
                nc.vector.tensor_copy(MCOMB, bank[6][:, 0:S]).then_inc(m_ctc, 1)
                for f in range(CF):
                    dve.wait_ge(m_silu, w * CF + f + 1)
                    dve.wait_ge(consumed, w * MOE_CHUNKS + (N0 + 2 * f + 2))
                    if f >= 2:
                        dve.wait_ge(m_T, w * CF + f - 1)
                    nc.vector.tensor_tensor(MHID[:, f % 2, 1, :], bank[f % 2 * 2 + 1][:, :], MHID[:, f % 2, 0, :],
                                            ALU.mult).then_inc(m_mul, 1)
                dve.wait_ge(consumed, w * MOE_CHUNKS + (N0 + MOE_CHUNKS))
                nc.vector.tensor_copy(MY[:, 512:1024], bank[7][:, :]).then_inc(m_yd, 1)
                dve.wait_ge(m_s, w + 1)
                for tt in range(TT):
                    for half in range(2):
                        xs = X[:, tt, half * 512:half * 512 + 512]
                        last = nc.vector.tensor_tensor(xs, bank[2 * tt + half][:, :], xs, ALU.add)
                last.then_inc(m_acc, 1)
                dve.wait_ge(m_acc, w + 1)

            norm(dve, n6)
            T6.dve(dve)
            P6.dve(dve)
            P6.wait(dve)
            for tt in range(TT):
                last = nc.vector.tensor_tensor(FX[:, tt, :], FX[:, tt, :], row("b_f"), ALU.add)
            last.then_inc(f_in, 1)
            dve.wait_ge(f_ln, 1)
            nc.vector.scalar_tensor_tensor(out=FX, in0=FX, scalar=0.0, in1=FA, op0=ALU.min, op1=ALU.subtract).then_inc(f_log, 1)
            dve.wait_ge(f_c, 1)
            nc.vector.tensor_scalar(FC, bank[0][0:16, 0:S], -1.0, None, ALU.mult).then_inc(f_cc, 1)
            TQ6.dve(dve)
            A6.dve(dve)
            A6.wait(dve)
            nc.vector.tensor_tensor(O[:, :, :], O[:, :, :], P[:, :, 3584:4608], ALU.mult).then_inc(g6, 1)
            TO6.dve(dve)
            add_to_x(dve, OUT6)
            TO6.wait(dve)

            norm(dve, n7)
            T7.dve(dve)
            P7.dve(dve)
            P7.wait(dve)
            T7.wait(dve)
            rope(dve, P[:, :, 0:1024], cos0, sin0, 16, TT)
            rope(dve, P[:, :, 1536:1792], cos0, sin0, 4, TT)
            rope(dve, P[:, :, 2048:2304], cos0, sin0, 4, TT)
            for tt in range(TT):
                for src, dest in ((1536, P[:, tt, 4096:4608]), (2048, P[:, tt, 4608:5120]),
                                  (1024, O[:, tt, 0:512]), (1280, O[:, tt, 512:1024])):
                    last = nc.vector.tensor_copy(dest.rearrange("p (g a d) -> p g a d", g=4, a=2),
                                                 P[:, tt, src:src + 256].rearrange("p (g d) -> p g d", g=4)
                                                 .unsqueeze(2).to_broadcast([128, 4, 2, DH]))
            last.then_inc(roped7, 1)
            TQ7.dve(dve)
            TQ7.wait(dve)
            for i in range(2):
                for j in range(2):
                    link(dve, nc.vector.memset(block_tiles(i, j), 0.0))
            link(dve, nc.vector.memset(VCB, 0.0))
            for i in range(2):
                for g in range(4):
                    n = 4 * i + g
                    dve.wait_ge(c_T, n + 1)
                    src = bank[n % 4][:, 0:S].rearrange("p (c l) -> p l c", l=16)
                    pe_cols = vec[:, VEC_ROWS["pe_k" if i == 0 else "pe_v"][0]:][:, 0:16]
                    for h in range(2):
                        rows = slice(64 * h, 64 * h + 64)
                        for j in range(2):
                            dest = block_tiles(i, j)[rows, :, g * CPAD:g * CPAD + NCMP]
                            last = nc.vector.tensor_tensor(dest, src[rows, h::2, j:j + NCMP],
                                                           pe_cols[rows, 8 * j:8 * j + 8].unsqueeze(2).to_broadcast([64, 8, NCMP]),
                                                           ALU.add)
                    last.then_inc(c_A, 1)
            for i in range(2):
                dve.wait_ge(c_hT, i + 1)
                nc.vector.tensor_copy(CHT[i], bank[2 + i][:, 0:256].rearrange("p (k r) -> p k r", k=2)).then_inc(c_hTc, 1)
            used(dve, c_ck[1][1])
            link(dve, nc.vector.tensor_copy(KCN[:, 0, :], bank[4][:, 0:DH]))
            for g in range(4):
                last = nc.vector.tensor_copy(VCB[32 * g:32 * g + 32, 64 * g:64 * g + 64], bank[5][32 * g:32 * g + 32, 0:DH])
            link(dve, last)
            rope(dve, KCN[:, 0:1, :], con("ccos").unsqueeze(1), con("csin").unsqueeze(1), 1, 1)
            nc.vector.tensor_copy(KCN[:, 1, :], KCN[:, 0, :]).then_inc(c_roped, 1)
            dve.wait_ge(c_kT, 1)
            nc.vector.tensor_copy(KCT, bank[6][:, 0:128]).then_inc(c_kTc, 1)
            cs_v = CS.rearrange("p (a c) -> p a c", c=CPAD)
            for tt in range(TT):
                dve.wait_ge(q_s, tt + 1)
                add = con("cmadd")[:, tt * CPAD:tt * CPAD + CPAD].unsqueeze(1).to_broadcast([128, 16, CPAD])
                keep = con("cm01")[:, tt * CPAD:tt * CPAD + CPAD].unsqueeze(1).to_broadcast([128, 16, CPAD])
                if tt:
                    dve.wait_ge(q_T, tt)
                for odd in range(2):
                    last = nc.vector.tensor_tensor(cs_v[:, 8 * odd:8 * odd + 8, :],
                                                   bank[2 * tt + odd][:, 0:256].rearrange("p (a c) -> p a c", c=CPAD),
                                                   add[:, 0:8, :], ALU.add)
                link(dve, last)
                link(dve, nc.vector.tensor_reduce(stat[:, 16:32], cs_v, AX.X, ALU.max))
                nc.vector.tensor_tensor(cs_v, cs_v, stat[:, 16:32].unsqueeze(2).to_broadcast([128, 16, CPAD]),
                                        ALU.subtract).then_inc(q_m, 1)
                dve.wait_ge(q_e, tt + 1)
                link(dve, nc.vector.tensor_reduce(stat[:, 16:32], cs_v, AX.X, ALU.add))
                link(dve, nc.vector.reciprocal(stat[:, 16:32], stat[:, 16:32]))
                gates = P[:, tt, 2560:2608].rearrange("p (g r q b) -> p q r g b", r=2, q=2, b=3)[:, :, :, :, 0]
                sv = stat[:, 16:32].rearrange("p (q r g) -> p q r g", q=2, r=2)
                link(dve, nc.vector.tensor_tensor(sv, sv, gates, ALU.mult))
                link(dve, nc.vector.tensor_tensor(cs_v, cs_v, keep, ALU.mult))
                nc.vector.tensor_tensor(cs_v, cs_v, stat[:, 16:32].unsqueeze(2).to_broadcast([128, 16, CPAD]),
                                        ALU.mult).then_inc(q_p, 1)
                dve.wait_ge(q_T, tt + 1)
                nc.vector.tensor_copy(CPT, bank[7][:, :]).then_inc(q_Tc, 1)
                dve.wait_ge(q_v, tt + 1)
                ov = O[:, tt, :].rearrange("p (g r d) -> p r g d", g=4, r=4)
                for b in range(2):
                    for r in range(2):
                        src = bank[4 + b][:, 256 * r:256 * r + 256].rearrange("p (g d) -> p g d", g=4)
                        last = nc.vector.tensor_copy(ov[:, 2 * r + b], src)
                last.then_inc(q_o, 1)
                dve.wait_ge(q_o, tt + 1)
            A7.dve(dve)
            A7.wait(dve)
            nc.vector.tensor_tensor(O[:, :, :], O[:, :, :], P[:, :, 3072:4096], ALU.mult).then_inc(g7, 1)
            TO7.dve(dve)
            add_to_x(dve, OUT7)
            TO7.wait(dve)
            mean_squares(dve, lambda tt: X[:, tt, :], D, lambda tt: stat[:, tt:tt + 1])
            inverse_roots(dve, stat[:, 0:2], D)
            dve.wait_ge(gfin2_in, 16)
            for tt in range(TT):
                last = nc.vector.scalar_tensor_tensor(out=X[:, tt, :], in0=X[:, tt, :], scalar=stat[:, tt:tt + 1],
                                                      in1=GAIN, op0=ALU.mult, op1=ALU.mult)
            last.then_inc(out_set, 1)

        @block.tensor
        def _(pe):
            pe.wait_ge(small_in, 16 * 7)
            pe.wait_ge(const_set, N_CONST)
            nc.tensor.transpose(bank[7][:, 0:NVEC], O[0:NVEC, 1, 0:128], ident[0:NVEC, 0:NVEC]).then_inc(vec_ready, 1)
            pe.wait_ge(vec_set, 1)
            for m in range(6):
                wt = take(pe, c_ada[m])
                if m >= 4:
                    pe.wait_ge(ada_used, m - 3)
                for kt in range(KD):
                    last = nc.tensor.matmul(bank[m % 4][:, :], scr[:, 128 * kt:128 * kt + 128], wt[:, kt, :],
                                            start=kt == 0, stop=kt == KD - 1)
                last.then_inc(consumed, 1)
            pe.wait_ge(h1, 1)
            T1.pe(pe)
            pe.wait_ge(ada_used, 6)
            T1.wait(pe)
            P1.pe(pe)
            pe.wait_ge(roped1, 1)
            P1.wait(pe)
            TQ1.pe(pe)
            TQ1.wait(pe)
            A1.pe(pe)
            A1.wait(pe)
            wt = take(pe, c_band)
            for g in range(4):
                out = bank[4 + g // 2][:, 256 * (g % 2):256 * (g % 2) + 256]
                nc.tensor.matmul(out, P[:, 0, g * 128:g * 128 + 128], wt[:, g, 0:256], start=True, stop=False,
                                 skip_group_check=True)
                last = nc.tensor.matmul(out[:, 128:256], P[:, 1, g * 128:g * 128 + 128], wt[:, g, 256:384], start=False,
                                        stop=True, skip_group_check=True)
                if g == 3:
                    last.then_inc(consumed, 1)
            wt = take(pe, c_grp)
            pe.wait_ge(d_copied, 1)
            for tt in range(TT):
                for g in range(4):
                    last = nc.tensor.matmul(bank[2 + tt][:, g * 128:g * 128 + 128],
                                            scr[:, 256 * g + 128 * tt:256 * g + 128 * tt + 128], wt[:, g, :], start=True,
                                            stop=True, skip_group_check=True)
            last.then_inc(consumed, 1)
            pe.wait_ge(y_gated, 1)
            TY1.pe(pe)
            pe.wait_ge(gated1, 1)
            TY1.wait(pe)
            TA1.pe(pe)
            UP1.pe(pe)
            TA1.wait(pe)
            pe.wait_ge(up_used, 1)
            AUP1.pe(pe)
            pe.wait_ge(merged, 1)
            TM1.pe(pe)
            TM1.wait(pe)
            OUT1.pe(pe)

            pe.wait_ge(n2, 1)
            T2.pe(pe)
            T2.wait(pe)
            P2.pe(pe)
            P2.wait(pe)
            TS2.pe(pe)
            pe.wait_ge(roped2, 1)
            TS2.wait(pe)
            TD2.pe(pe)
            TD2.wait(pe)
            for i in range(10):
                if i < 8:
                    if i >= 2:
                        pe.wait_ge(st_sp, i - 1)
                    (a, b) = at(i)
                    q, k = QT[b:b + 64, a, :], KT[b:b + 64, a, :]
                    z = bank[4 + i % 2]
                    nc.tensor.matmul(z[:, 0:256], k[:, 0:128], q, start=True, stop=True, skip_group_check=True)
                    nc.tensor.matmul(z[:, 256:384], k[:, 128:256], q[:, 128:256], start=True, stop=True,
                                     skip_group_check=True).then_inc(st_z, 1)
                if 1 <= i <= 8:
                    j = i - 1
                    pe.wait_ge(st_sp, j + 1)
                    if j >= 2:
                        pe.wait_ge(st_w, j - 1)
                    (a, b) = at(j)
                    q, k = QT[b:b + 64, a, :], KT[b:b + 64, a, :]
                    r, e = bank[6 + j % 2], E[j % 2]
                    nc.tensor.matmul(r[:, 0:256], k[:, 0:128], q, start=True, stop=False, skip_group_check=True)
                    nc.tensor.matmul(r[:, 0:256], neg_tri[:, :], e[:, 0:256], start=False, stop=False, skip_group_check=True)
                    nc.tensor.matmul(r[:, 128:256], neg_ones[:, :], e[:, 256:384], start=False, stop=False,
                                     skip_group_check=True)
                    nc.tensor.matmul(r[:, 0:128], identb[:, :], mask_past[:, :], start=False, stop=True,
                                     skip_group_check=True)
                    nc.tensor.matmul(r[:, 256:384], k[:, 128:256], q[:, 128:256], start=True, stop=False,
                                     skip_group_check=True)
                    nc.tensor.matmul(r[:, 256:384], neg_tri[:, :], e[:, 256:384], start=False, stop=False,
                                     skip_group_check=True)
                    nc.tensor.matmul(r[:, 256:384], identb[:, :], mask_past[:, :], start=False, stop=True,
                                     skip_group_check=True).then_inc(st_r, 1)
                if i >= 2:
                    j = i - 2
                    pe.wait_ge(st_w, j + 1)
                    p, o = PT[j % 2], slice(j * 64, j * 64 + 64)
                    v = values(1024 + 64 * j, 64)
                    nc.tensor.matmul(bank[0][:, o], p[:, 0:128], v(0), start=True, stop=True, skip_group_check=True)
                    nc.tensor.matmul(bank[1][:, o], p[:, 128:256], v(0), start=True, stop=False, skip_group_check=True)
                    nc.tensor.matmul(bank[1][:, o], p[:, 256:384], v(1), start=False, stop=True,
                                     skip_group_check=True).then_inc(st_v, 1)
            pe.wait_ge(st_done, 1)
            A2.pe(pe)
            pe.wait_ge(o2, 1)
            A2.wait(pe)
            TO2.pe(pe)
            TO2.wait(pe)
            OUT2.pe(pe)
            pe.wait_ge(n3, 1)
            T3.pe(pe)
            T3.wait(pe)
            def hidden_T(f):
                pe.wait_ge(ffn_mul, 2 * f + 2)
                if f >= 1:
                    pe.wait_ge(ffn_Tc, f)
                for k in range(ff[f][1] // 128):
                    for tt in range(TT):
                        last = nc.tensor.transpose(bank[4 + k // 2][:, (k % 2) * S + tt * 128:(k % 2) * S + tt * 128 + 128],
                                                   HID[:, f % 2, tt, k * 128:k * 128 + 128], ident[:, :])
                last.then_inc(ffn_T, 1)

            for f, (c0, n) in enumerate(ff):
                gate, up = take(pe, c_ff[f][0]), take(pe, c_ff[f][1])
                for tt in range(TT):
                    if f >= 1:
                        pe.wait_ge(ffn_silu, 2 * f - 1 + tt)
                    for kt in range(KD):
                        last = nc.tensor.matmul(bank[tt][:, 0:n], xt(kt, tt), gate[:, kt, :], start=kt == 0, stop=kt == KD - 1)
                last.then_inc(consumed, 1)
                for tt in range(TT):
                    if f >= 1:
                        pe.wait_ge(ffn_mul, 2 * f - 1 + tt)
                    for kt in range(KD):
                        last = nc.tensor.matmul(bank[2 + tt][:, 0:n], xt(kt, tt), up[:, kt, :], start=kt == 0, stop=kt == KD - 1)
                last.then_inc(consumed, 1)
                if f >= 1:
                    hidden_T(f - 1)
            hidden_T(len(ff) - 1)
            pe.wait_ge(ffn_Tc, len(ff))
            DOWN.pe(pe)

            pe.wait_ge(n4, 1)
            T4.pe(pe)
            T4.wait(pe)
            P4.pe(pe)
            pe.wait_ge(roped4, 1)
            TQ4.pe(pe)
            TQ4.wait(pe)
            take(pe, c_rel)
            A4.pe(pe)
            A4.wait(pe)
            pe.sem_inc(consumed, 1)
            TO4.pe(pe)
            TO4.wait(pe)
            OUT4.pe(pe)
            pe.wait_ge(n5, 1)
            T5.pe(pe)
            T5.wait(pe)
            wt = take(pe, c_router)
            for tt in range(TT):
                for kt in range(KD):
                    last = nc.tensor.matmul(bank[0][:, NEXP * tt:NEXP * tt + NEXP], xt(kt, tt), wt[:, kt, :],
                                            start=kt == 0, stop=kt == KD - 1, skip_group_check=True)
            last.then_inc(consumed, 1)
            pe.wait_ge(picked, 1)
            nc.tensor.matmul(bank[1][:, 0:8], past01[:, :], MASK[:, 0, :], start=True, stop=True, skip_group_check=True)
            nc.tensor.matmul(bank[1][:, 8:16], ones[:, :], MASK[:, 0, :], start=True, stop=False, skip_group_check=True)
            nc.tensor.matmul(bank[1][:, 8:16], past01[:, :], MASK[:, 1, :], start=False, stop=True, skip_group_check=True)
            nc.tensor.matmul(bank[2][:, 0:8], ones[:, :], MASK[:, 0, :], start=True, stop=False)
            nc.tensor.matmul(bank[2][:, 0:8], ones[:, :], MASK[:, 1, :], start=False, stop=True).then_inc(cnt_ps, 1)

            pe.wait_ge(list_set, 1)
            tiles = pe.value_load(WORK[0:1, TILE_MAX:TILE_MAX + 1], min_val=4, max_val=TILE_MAX)
            with pe.Fori(0, tiles) as w:
                def moe_take(c):
                    n = N0 + c
                    pe.wait_ge(landed[n % RING], w * (16 * MOE_CHUNKS // RING) + 16 * (n // RING + 1))
                    return slot_ap(n, 8, 512) if c < 2 * CF else slot_ap(n, 4, D)

                def moe_T(f):
                    pe.wait_ge(m_mul, w * CF + f + 1)
                    if f >= 2:
                        pe.wait_ge(m_Tc, w * CF + f - 1)
                    for k in range(4):
                        last = nc.tensor.transpose(bank[4 + f % 2][:, k * 128:k * 128 + 128],
                                                   MHID[:, f % 2, 1, k * 128:k * 128 + 128], ident[:, :])
                    last.then_inc(m_T, 1)

                pe.wait_ge(m_sel, w + 1)
                for k in range(8):
                    for tt in range(TT):
                        last = nc.tensor.matmul(bank[4 + k // 4][:, (k % 4) * 128:(k % 4) * 128 + 128],
                                                O[:, tt, k * 128:k * 128 + 128], MSEL[:, tt, :], start=tt == 0, stop=tt == 1,
                                                skip_group_check=True)
                    if k % 4 == 3:
                        last.then_inc(m_x, 1)
                for tt in range(TT):
                    last = nc.tensor.transpose(bank[6][:, tt * 128:tt * 128 + 128], MSELG[:, tt, :], ident[:, :])
                last.then_inc(m_ct, 1)
                pe.wait_ge(m_xa, w + 1)
                pe.wait_ge(m_xd, w + 1)
                pe.wait_ge(m_acc, w)
                for f in range(CF):
                    for c, b in ((2 * f, f % 2 * 2), (2 * f + 1, f % 2 * 2 + 1)):
                        wt = moe_take(c)
                        if f >= 2:
                            pe.wait_ge(m_mul if c % 2 else m_silu, w * CF + f - 1)
                        for kt in range(KD):
                            last = nc.tensor.matmul(bank[b][:, :], MXT[:, kt, :], wt[:, kt, :], start=kt == 0, stop=kt == KD - 1)
                        last.then_inc(consumed, 1)
                    if f >= 1:
                        moe_T(f - 1)
                moe_T(CF - 1)
                pe.wait_ge(m_ctc, w + 1)
                for f in range(CF):
                    wt = moe_take(2 * CF + f)
                    pe.wait_ge(m_Tc, w * CF + f + 1)
                    for kk in range(4):
                        for half in range(2):
                            last = nc.tensor.matmul(bank[6 + half][:, :], MHT[:, 4 * f + kk, :],
                                                    wt[:, kk, half * 512:half * 512 + 512],
                                                    start=f == 0 and kk == 0, stop=f == CF - 1 and kk == 3)
                    last.then_inc(consumed, 1)
                pe.wait_ge(m_ya, w + 1)
                pe.wait_ge(m_yd, w + 1)
                for tt in range(TT):
                    for half in range(2):
                        last = nc.tensor.matmul(bank[2 * tt + half][:, :], MCOMB[:, tt * 128:tt * 128 + 128],
                                                MY[:, half * 512:half * 512 + 512], start=True, stop=True)
                last.then_inc(m_s, 1)
            moe_tiles[pe.engine] = tiles

            pe.wait_ge(n6, 1)
            T6.pe(pe)
            T6.wait(pe)
            P6.pe(pe)
            pe.wait_ge(f_log, 1)
            FL = lambda tt: FX[:, tt, :]
            nc.tensor.matmul(bank[0][0:16, 0:128], FL(0), past01[:, :], start=True, stop=False, skip_group_check=True)
            nc.tensor.matmul(bank[0][0:16, 0:128], FL(0), ident[:, :], start=False, stop=True, skip_group_check=True)
            nc.tensor.matmul(bank[0][0:16, 128:256], FL(0), ones[:, :], start=True, stop=False, skip_group_check=True)
            nc.tensor.matmul(bank[0][0:16, 128:256], FL(1), past01[:, :], start=False, stop=False, skip_group_check=True)
            nc.tensor.matmul(bank[0][0:16, 128:256], FL(1), ident[:, :], start=False, stop=True,
                             skip_group_check=True).then_inc(f_c, 1)
            P6.wait(pe)
            TQ6.pe(pe)
            TQ6.wait(pe)
            pe.wait_ge(f_cc, 1)
            A6.pe(pe)
            pe.wait_ge(g6, 1)
            TO6.pe(pe)
            TO6.wait(pe)
            OUT6.pe(pe)

            pe.wait_ge(n7, 1)
            T7.pe(pe)
            T7.wait(pe)
            P7.pe(pe)
            P7.wait(pe)
            pe.wait_ge(roped7, 1)
            TQ7.pe(pe)
            for n in range(8):
                if n >= 4:
                    pe.wait_ge(c_A, n - 3)
                for tt in range(TT):
                    last = nc.tensor.transpose(bank[n % 4][:, tt * 128:tt * 128 + 128],
                                               twice_o(n)(tt), ident[:, :])
                last.then_inc(c_T, 1)
            for i in range(2):
                wt = take(pe, c_ck[i][0])
                pe.wait_ge(c_A, 4 + 4)
                for k in range(16):
                    last = nc.tensor.matmul(bank[i][:, 0:256], block_tiles(i, k // 8)[:, k % 8, :], wt[:, k, :], start=k == 0, stop=k == 15)
                last.then_inc(consumed, 1)
                pe.wait_ge(c_s, i + 1)
                for k in range(2):
                    last = nc.tensor.transpose(bank[2 + i][:, k * 128:k * 128 + 128], CH[i][:, k * 128:k * 128 + 128], ident[:, :])
                last.then_inc(c_hT, 1)
                if i == 0:
                    TQ7.wait(pe)
                pe.wait_ge(c_hTc, i + 1)
                wt = take(pe, c_ck[i][1])
                for k in range(2):
                    last = nc.tensor.matmul(bank[4 + i][:, 0:DH], CHT[i][:, k, :], wt[:, k, :], start=k == 0, stop=k == 1)
                last.then_inc(consumed, 1)
            pe.wait_ge(c_roped, 1)
            nc.tensor.transpose(bank[6][:, 0:128], KCN.rearrange("p a d -> p (a d)"), ident[:, :]).then_inc(c_kT, 1)
            pe.wait_ge(c_kTc, 1)
            for tt in range(TT):
                for r in range(4):
                    for g in range(4):
                        a, b = at(4 * g + r)
                        c = (r // 2) * 128 + g * CPAD
                        last = nc.tensor.matmul(bank[2 * tt + r % 2][:, c:c + CPAD],
                                                QT[b:b + 64, a, tt * 128:tt * 128 + 128], KCT[b:b + 64, g * CPAD:g * CPAD + CPAD],
                                                start=True, stop=True, skip_group_check=True)
                last.then_inc(q_s, 1)
            for tt in range(TT):
                pe.wait_ge(q_p, tt + 1)
                for r in range(4):
                    last = nc.tensor.transpose(bank[7][:, r * 128:r * 128 + 128], CS[:, r * 128:r * 128 + 128], ident[:, :])
                last.then_inc(q_T, 1)
                pe.wait_ge(q_Tc, tt + 1)
                if tt:
                    pe.wait_ge(q_o, tt)
                for r in range(4):
                    last = nc.tensor.matmul(bank[4 + r // 2][:, 256 * (r % 2):256 * (r % 2) + 256],
                                            CPT[:, r * 128:r * 128 + 128], VCB, start=True, stop=True, skip_group_check=True)
                last.then_inc(q_v, 1)
            pe.wait_ge(q_o, 2)
            A7.pe(pe)
            pe.wait_ge(g7, 1)
            TO7.pe(pe)
            TO7.wait(pe)
            OUT7.pe(pe)


def kernel(**inputs):
    import concourse.bacc as bacc
    from concourse.bass_utils import run_bass_kernel_spmd

    arrays = {n: np.ascontiguousarray(inputs[n]) for n in (
        "x", "w_ada", "b_ada", "g_norm", "w_in", "w_pool_grp", "w_pool_up", "w_attn_up", "w_out", "g_final",
        "positions_2", "ev_w_in_2", "ev_w_out_2", "ev_w_gate_2", "ev_w_up_2", "ev_w_down_2", "od_w_qkv_2", "od_w_out_2",
        "od_router_2", "od_we_gate_2", "od_we_up_2", "od_we_down_2", "fox_w_in_3", "fox_w_out_3", "nsa_w_in_3",
        "nsa_w_ck1_3", "nsa_w_ck2_3", "nsa_w_cv1_3", "nsa_w_cv2_3", "nsa_w_out_3", "final_g_3")}
    arrays["vec"] = np.concatenate([np.asarray(inputs[n]).reshape(-1, 128) for n in (
        "ev_attn_norm_2", "ev_ffn_norm_2", "od_attn_norm_2", "od_ffn_norm_2", "norm_g_3", "pool_scale", "c",
        "nsa_pe_k_3", "nsa_pe_v_3")])
    arrays["small"] = np.concatenate([np.asarray(inputs[n]).reshape(-1) for n in (
        "ev_q_norm_2", "ev_k_norm_2", "od_q_norm_2", "od_k_norm_2", "ev_subln_2", "fox_b_f_3", "ev_lambda_q1_2",
        "ev_lambda_k1_2", "ev_lambda_q2_2", "ev_lambda_k2_2")])
    distance = np.clip(128 + np.arange(128)[:, None] - np.arange(256)[None, :], -128, 128) + 128
    arrays["rel"] = np.ascontiguousarray(np.asarray(inputs["od_rel_bias_2"])[0][:, distance].transpose(1, 0, 2))
    arrays["co"], arrays["band"] = shape_constants()

    nc = bacc.Bacc("TRN2", target_bir_lowering=False, num_devices=1)
    tensors = {n: nc.dram_tensor(f"in_{n}", a.shape, mybir.dt.from_np(a.dtype), kind="ExternalInput").ap()
               for n, a in arrays.items()}
    tensors["out"] = nc.dram_tensor("out_x", (1, S, D), F32, kind="ExternalOutput").ap()
    build(nc, tensors)
    result = run_bass_kernel_spmd(nc, [{f"in_{n}": a for n, a in arrays.items()}], core_ids=[0])
    return result.results[0]["out_x"]
```

```python
from contextlib import ExitStack

import numpy as np
import concourse.bass as bass
from concourse import mybir

F32 = mybir.dt.float32
F32R = mybir.dt.float32r
BF16 = mybir.dt.bfloat16
I32 = mybir.dt.int32
ALU = mybir.AluOpType
ACT = mybir.ActivationFunctionType
AX = mybir.AxisListType

S = 256
TT = S // 128
D = 1024
KD = D // 128
DH = 64
RING = 6
SPLIT = 3
SLOT = 2048
EPS = 1e-6
BIG = 1e30
F_DENSE = 2816
F_EXP = 3584
NEXP = 8
CF = F_EXP // 512
MOE_CHUNKS = 6 * CF
TILE_MAX = 11
NCMP = 15
CPAD = 32
ROPE_THETA = 500000.0
WINDOWS = (2, 4, 8, 16)
LAM_INIT = 0.2

VEC_ROWS = {}
_at = 0
for _name, _n in (("ev_attn", 8), ("ev_ffn", 8), ("od_attn", 8), ("od_ffn", 8), ("norm3", 16),
                  ("pool_scale", 4), ("c", 8), ("pe_k", 16), ("pe_v", 16)):
    VEC_ROWS[_name] = (_at, _n)
    _at += _n
NVEC = _at

SM = {}
_at = 0
for _name, _n in (("ev_q", 64), ("ev_k", 64), ("od_q", 64), ("od_k", 64), ("subln", 128), ("b_f", 16),
                  ("lq1", 64), ("lk1", 64), ("lq2", 64), ("lk2", 64)):
    SM[_name] = (_at, _n)
    _at += _n
NSM = _at

CO = {}
_at = 0
for _name, _n in (("cos", 16), ("sin", 16), ("ccos", 8), ("csin", 8), ("invf", 8), ("cm01", 64), ("cmadd", 64)):
    CO[_name] = (_at, _n)
    _at += _n
NCO = _at


def shape_constants():
    inv = (np.float32(ROPE_THETA) ** (-np.arange(0, 16, 2, dtype=np.float32) / np.float32(16))).astype(np.float32)
    co = np.zeros((128, NCO), np.float32)
    ang = (np.arange(S, dtype=np.float32)[:, None] * inv[None, :]).astype(np.float32)
    for key, fn in (("cos", np.cos), ("sin", np.sin)):
        tab = fn(ang).astype(np.float32).reshape(TT, 128, 8).transpose(1, 0, 2).reshape(128, 16)
        co[:, CO[key][0]:CO[key][0] + 16] = tab
    end = (np.arange(128) % CPAD) * 16 + 31
    cang = (end.astype(np.float32)[:, None] * inv[None, :]).astype(np.float32)
    co[:, CO["ccos"][0]:CO["ccos"][0] + 8] = np.cos(cang)
    co[:, CO["csin"][0]:CO["csin"][0] + 8] = np.sin(cang)
    co[:, CO["invf"][0]:CO["invf"][0] + 8] = inv
    c = np.arange(CPAD)
    seen = ((c * 16 + 31)[None, :] <= np.arange(S)[:, None]) & (c < NCMP)[None, :]
    seen = seen.astype(np.float32).reshape(TT, 128, CPAD).transpose(1, 0, 2).reshape(128, 64)
    co[:, CO["cm01"][0]:CO["cm01"][0] + 64] = seen
    co[:, CO["cmadd"][0]:CO["cmadd"][0] + 64] = (seen - 1) * np.float32(BIG)
    band = np.zeros((4, S, S), np.float32)
    for g, w in enumerate(WINDOWS):
        for t in range(S):
            lo = max(t + 1 - w, 0)
            band[g, lo:t + 1, t] = np.float32(1) / np.float32(t + 1 - lo)
            band[g, t, t] -= np.float32(1)
    packed = np.zeros((128, 4, 384), np.float32)
    packed[:, :, :256] = band[:, :128, :].transpose(1, 0, 2)
    packed[:, :, 256:] = band[:, 128:, 128:].transpose(1, 0, 2)
    return co, packed


def build(nc, t):
    ctx = ExitStack()
    with ctx:
        def sb(name, shape, dt=F32):
            return ctx.enter_context(nc.sbuf_tensor(name, shape, dt))

        def sem(name):
            return ctx.enter_context(nc.semaphore(name))

        X = sb("X", [128, TT, D])
        XTH = sb("XTH", [128, KD, S], F32R)
        XTL = sb("XTL", [128, KD, S], F32R)
        HTH = sb("HTH", [128, 4, S], F32R)
        HTL = sb("HTL", [128, 4, S], F32R)
        P = sb("P", [128, TT, 5120])
        QT = sb("QT", [128, 8, S])
        KT = sb("KT", [128, 8, S])
        O = sb("O", [128, TT, D])
        ring = sb("ring", [128, RING, SLOT])
        WH = sb("WH", [128, SPLIT, SLOT], F32R)
        WL = sb("WL", [128, SPLIT, SLOT], F32R)
        ident = sb("ident", [128, 128])
        identb = sb("identb", [128, 128], BF16)
        mask_causal = sb("mask_causal", [128, 128], BF16)
        mask_chunk = sb("mask_chunk", [128, 128], BF16)
        mask_past = sb("mask_past", [128, 128], BF16)
        past01 = sb("past01", [128, 128])
        neg_tri = sb("neg_tri", [128, 128])
        neg_ones = sb("neg_ones", [128, 128])
        ones = sb("ones", [128, 128])
        scr = sb("scr", [128, 1920])
        vec = sb("vec", [128, NVEC])
        small = sb("small", [128, NSM])
        co = sb("co", [128, NCO])
        cs2 = sb("cs2", [128, 4, 16])
        stat = sb("stat", [128, 64])
        rs = sb("rs", [128, 2, 2, 8])
        rr = sb("rr", [128, 2, 8])
        nmax = sb("nmax", [128, 3, 2])
        lam = sb("lam", [128, 4])
        posi = sb("posi", [128, TT], I32)
        bank = [ctx.enter_context(nc.psum_tensor(f"bank{b}", [128, 512], F32)) for b in range(8)]

        E = [scr[:, 384 * i:384 * i + 384] for i in range(3)]
        PT = [scr[:, 1152:1536], scr[:, 1536:1920]]

        def col(name, i=0):
            at = VEC_ROWS[name][0] + i
            return vec[:, at:at + 1]

        def row(name):
            at, n = SM[name]
            return small[:, at:at + n]

        def con(name):
            at, n = CO[name]
            return co[:, at:at + n]

        stream = []

        def chunk(ap, nk, n):
            assert nk * n <= SLOT
            stream.append((ap, nk, n))
            return len(stream) - 1

        def kcols(w, c0, n, k0=0, nk=KD):
            return w[k0 * 128:(k0 + nk) * 128, c0:c0 + n].rearrange("(k p) n -> p k n", p=128)

        def cols(w, c0, n):
            k = w.shape[0] // 128
            nk = min(k, SLOT // n)
            return [(chunk(kcols(w, c0, n, k0, nk), nk, n), k0, nk) for k0 in range(0, k, nk)]

        def rows_of(w, k0, k):
            return [(chunk(kcols(w, 0, D, a, 2), 2, D), a - k0, 2) for a in range(k0, k0 + k, 2)]

        w = {n: t[n][0] for n in ("w_ada", "w_in", "w_pool_up", "w_attn_up", "w_out", "ev_w_in_2", "ev_w_out_2",
                                  "ev_w_gate_2", "ev_w_up_2", "ev_w_down_2", "od_w_qkv_2", "od_w_out_2",
                                  "od_router_2", "fox_w_in_3", "fox_w_out_3", "nsa_w_in_3", "nsa_w_ck1_3",
                                  "nsa_w_ck2_3", "nsa_w_cv1_3", "nsa_w_cv2_3", "nsa_w_out_3")}
        ada_order = [2, 3, 0, 1, 4, 5]
        c_ada = [cols(w["w_ada"], 512 * i, 512) for i in ada_order]
        in1_order = [1024, 1536, 2048, 0, 512, 2560, 3072, 3584, 4096, 4608]
        c_in1 = [cols(w["w_in"], c, 512) for c in in1_order]
        c_pup, c_aup = rows_of(w["w_pool_up"], 0, 4), rows_of(w["w_attn_up"], 0, 4)
        c_out1 = rows_of(w["w_out"], 0, KD)
        in2_order = [1536, 2048, 0, 512, 1024, 2560]
        c_in2 = [cols(w["ev_w_in_2"], c, 512) for c in in2_order]
        c_out2 = rows_of(w["ev_w_out_2"], 0, KD)
        ff = [(512 * i, min(512, F_DENSE - 512 * i)) for i in range(-(-F_DENSE // 512))]
        NF = len(ff)
        c_gate, c_up, c_down = [None] * NF, [None] * NF, [None] * NF
        for f, (c0, n) in enumerate(ff):
            c_gate[f], c_up[f] = cols(w["ev_w_gate_2"], c0, n), cols(w["ev_w_up_2"], c0, n)
            if f:
                c_down[f - 1] = rows_of(w["ev_w_down_2"], 4 * (f - 1), 4)
        c_down[NF - 1] = rows_of(w["ev_w_down_2"], 4 * (NF - 1), ff[-1][1] // 128)
        c_in3 = [cols(w["od_w_qkv_2"], 512 * i, 512) for i in range(6)]
        c_out3 = rows_of(w["od_w_out_2"], 0, KD)
        c_router = cols(w["od_router_2"], 0, NEXP)
        N0 = len(stream)
        c_in4 = [cols(w["fox_w_in_3"], 512 * i, 512) for i in range(6)]
        c_f = cols(w["fox_w_in_3"], 3072, 16)
        c_z4 = [cols(w["fox_w_in_3"], 3088 + 512 * i, 512) for i in range(2)]
        c_out4 = rows_of(w["fox_w_out_3"], 0, KD)
        in5_order = [0, 512, 1536, 2048, 1024]
        c_in5 = [cols(w["nsa_w_in_3"], c, 512) for c in in5_order]
        c_g5 = [(chunk(kcols(w["nsa_w_in_3"], 2560, 48), KD, 48), 0, KD)]
        c_z5 = [cols(w["nsa_w_in_3"], 2608 + 512 * i, 512) for i in range(2)]
        c_ck = [(cols(w["nsa_w_ck1_3"], 0, 256), cols(w["nsa_w_ck2_3"], 0, DH)),
                (cols(w["nsa_w_cv1_3"], 0, 256), cols(w["nsa_w_cv2_3"], 0, DH))]
        c_out5 = rows_of(w["nsa_w_out_3"], 0, KD)

        moe_order = []
        for f in range(CF):
            moe_order += [(what, f, i) for what in ("gate", "up") for i in range(2)]
            if f:
                moe_order += [("down", f - 1, i) for i in range(2)]
        moe_order += [("down", CF - 1, i) for i in range(2)]
        moe_at = {key: c for c, key in enumerate(moe_order)}
        assert len(moe_order) == MOE_CHUNKS and MOE_CHUNKS % RING == 0 and MOE_CHUNKS % SPLIT == 0

        landed = [sem(f"landed{s}") for s in range(RING)]
        hi_made, lo_made = sem("hi_made"), sem("lo_made")
        consumed = sem("consumed")

        def slot_ap(n, nk, width):
            return ring[:, n % RING, 0:nk * width].rearrange("p (k n) -> p k n", k=nk)

        def parts(n, nk, width):
            return [x[:, n % SPLIT, 0:nk * width].rearrange("p (k n) -> p k n", k=nk) for x in (WH, WL)]

        def after_moe(n):
            return n >= N0

        vec_in = sem("vec_in")
        ada_in = sem("ada_in")
        small_in = sem("small_in")
        ones_set = sem("ones_set")
        const_set = sem("const_set")
        vec_ready = sem("vec_ready")
        vec_set = sem("vec_set")
        dve_chain = sem("dve_chain")
        act_chain = sem("act_chain")

        turn_ready, turn_act, turn_dve = sem("turn_ready"), sem("turn_act"), sem("turn_dve")
        proj_act = sem("proj_act")
        scored, maxed, exped, turned, copied, valued, grouped = (
            sem(x) for x in ("scored", "maxed", "exped", "turned", "copied", "valued", "grouped"))
        base = {"turn": 0, "turn_act": 0, "turn_dve": 0, "proj_act": 0, "unit": 0, "group": 0}

        class Transposes:

            def __init__(self, items, split=False):
                self.items, self.n, self.split = items, -(-len(items) // 2), split
                self.b, self.ba, self.bd = base["turn"], base["turn_act"], base["turn_dve"]
                self.na = self.n if split else (self.n + 1) // 2
                self.nd = self.n if split else self.n // 2
                base["turn"] += self.n
                base["turn_act"] += self.na
                base["turn_dve"] += self.nd

            def pe(self, pe):
                for i in range(self.n):
                    if i >= 4 and self.split:
                        pe.wait_ge(turn_dve, self.bd + i - 3)
                    elif i >= 4:
                        pe.wait_ge(turn_dve if i % 2 else turn_act, (self.bd if i % 2 else self.ba) + (i - 4) // 2 + 1)
                    for j, (src, _, _) in enumerate(self.items[2 * i:2 * i + 2]):
                        for tt in range(TT):
                            last = nc.tensor.transpose(bank[4 + i % 4][:, j * S + tt * 128:j * S + tt * 128 + 128],
                                                       src(tt), ident[:, :])
                    last.then_inc(turn_ready, 1)

            def act(self, act):
                for i in range(0, self.n, 1 if self.split else 2):
                    act.wait_ge(turn_ready, self.b + i + 1)
                    for j, (_, dest, scale) in enumerate(self.items[2 * i:2 * i + 2]):
                        last = nc.scalar.activation(dest[0] if self.split else dest, bank[4 + i % 4][:, j * S:j * S + S],
                                                    ACT.Copy, scale=1.0 if scale is None else scale)
                    last.then_inc(turn_act, 1)

            def dve(self, dve):
                for i in range(0 if self.split else 1, self.n, 1 if self.split else 2):
                    if self.split:
                        dve.wait_ge(turn_act, self.ba + i + 1)
                    else:
                        dve.wait_ge(turn_ready, self.b + i + 1)
                    for j, (_, dest, scale) in enumerate(self.items[2 * i:2 * i + 2]):
                        src = bank[4 + i % 4][:, j * S:j * S + S]
                        if self.split:
                            last = nc.vector.scalar_tensor_tensor(out=dest[1], in0=src, scalar=1.0 if scale is None else scale,
                                                                  in1=dest[0].bitcast(F32), op0=ALU.mult, op1=ALU.subtract)
                        elif scale is None:
                            last = nc.vector.tensor_copy(dest, src)
                        else:
                            last = nc.vector.tensor_scalar(dest, src, scale, None, ALU.mult)
                    last.then_inc(turn_dve, 1)

            def wait(self, eng):
                eng.wait_ge(turn_act, self.ba + self.na)
                if self.nd:
                    eng.wait_ge(turn_dve, self.bd + self.nd)

            def wait_tiles(self, eng, n):
                eng.wait_ge(turn_dve, self.bd + -(-n // 2))

        def three(out, x, wt, k, start, stop, check=False):
            nc.tensor.matmul(out, x[0], wt[0][:, k, :], start=start, stop=False, skip_group_check=check)
            nc.tensor.matmul(out, x[0], wt[1][:, k, :], start=False, stop=False, skip_group_check=check)
            return nc.tensor.matmul(out, x[1], wt[0][:, k, :], start=False, stop=stop, skip_group_check=check)

        class Project:

            def __init__(self, jobs, lhs):
                self.jobs, self.lhs = jobs, lhs
                self.ba = base["proj_act"]
                base["proj_act"] += len(jobs)

            def pe(self, pe, operand):
                for c, (chunks, width, _, _) in enumerate(self.jobs):
                    if c >= 2:
                        pe.wait_ge(proj_act, self.ba + c - 1)
                    for n, k0, nk in chunks:
                        if c == 0:
                            operand.wait_tiles(pe, k0 + nk)
                        wt = take(pe, n)
                        for tt in range(TT):
                            for k in range(nk):
                                last = three(bank[(2 * c + tt) % 4][:, 0:width], self.lhs(k0 + k, tt), wt, k,
                                             k0 + k == 0, k0 + k == KD - 1, check=True)
                        last.then_inc(consumed, 1)

            def act(self, act, beside={}):
                for c, (chunks, width, dest, func) in enumerate(self.jobs):
                    split_until(act, chunks[-1][0] + SPLIT)
                    used(act, chunks[-1][0])
                    for tt in range(TT):
                        last = nc.scalar.activation(dest(tt), bank[(2 * c + tt) % 4][:, 0:width], func)
                    last.then_inc(proj_act, 1)
                    if c in beside:
                        beside[c]()

            def dve(self, dve, beside={}):
                for c, (chunks, _, _, _) in enumerate(self.jobs):
                    split_until(dve, chunks[-1][0] + SPLIT)
                    if c in beside:
                        dve.wait_ge(proj_act, self.ba + c + 1)
                        beside[c]()

            def wait(self, eng):
                eng.wait_ge(proj_act, self.ba + len(self.jobs))

        class OutProduct:

            def __init__(self, chunks, lhs):
                self.chunks, self.lhs = chunks, lhs

            def pe(self, pe, first=True, last_=True, operand=None):
                total = self.chunks[-1][1] + self.chunks[-1][2]
                for n, k0, nk in self.chunks:
                    if operand:
                        operand.wait_tiles(pe, k0 + nk)
                    wt = take(pe, n)
                    for k in range(nk):
                        for tt in range(TT):
                            for half in range(2):
                                cut = [x[:, :, half * 512:half * 512 + 512] for x in wt]
                                last = three(bank[2 * tt + half][:, :], self.lhs(k0 + k, tt), cut, k,
                                             first and k0 + k == 0, last_ and k0 + k == total - 1, check=True)
                    last.then_inc(consumed, 1)

            def splits(self, eng):
                split_until(eng, self.chunks[-1][0] + SPLIT)

            def wait(self, eng):
                used(eng, self.chunks[-1][0])

        class Attention:

            def __init__(self, units, dv, mask, finish, extra=None, fill=0):
                self.units, self.dv, self.mask, self.finish, self.extra = units, dv, mask, finish, extra
                self.fill = fill
                self.G = 512 // dv
                self.u, self.g = base["unit"], base["group"]
                base["unit"] += len(units)
                base["group"] += len(units) // self.G

            def pe(self, pe):
                U, G = len(self.units), self.G
                for i in range(U + 3):
                    if i < U:
                        (qt_, qb), (kt_, kb), _ = self.units[i]
                        assert qb == kb
                        b = bank[4 + i % 3]
                        if i >= 3:
                            pe.wait_ge(exped, self.u + i - 2)
                        if self.fill and i % 8 == 4:
                            keep_warm(4 + i % 3, self.fill)
                        q, k = QT[qb:qb + 64, qt_, :], KT[kb:kb + 64, kt_, :]
                        for t0, (a, n) in enumerate(((0, 128), (128, 256))):
                            nc.tensor.matmul(b[:, a:a + n], q[:, t0 * 128:t0 * 128 + 128], k[:, 0:n], start=True,
                                             stop=False, skip_group_check=True)
                            if self.extra:
                                self.extra(i, t0, b[:, a:a + n])
                            last = nc.tensor.matmul(b[:, a + n - 128:a + n], identb[:, :], self.mask[:, :], start=False,
                                                    stop=True, skip_group_check=True)
                        last.then_inc(scored, 1)
                    if 2 <= i < U + 2:
                        j = i - 2
                        pe.wait_ge(exped, self.u + j + 1)
                        if j >= 1:
                            pe.wait_ge(copied, self.u + j)
                        for c in range(3):
                            last = nc.tensor.transpose(bank[7][:, c * 128:c * 128 + 128],
                                                       E[j % 3][:, c * 128:c * 128 + 128], ident[:, :])
                        last.then_inc(turned, 1)
                    if i >= 3:
                        j = i - 3
                        g, uu = j // G, j % G
                        pe.wait_ge(copied, self.u + j + 1)
                        if uu == 0 and g >= 2:
                            pe.wait_ge(grouped, self.g + g - 1)
                        v, p, o = self.units[j][2], PT[j % 2], slice(uu * self.dv, (uu + 1) * self.dv)
                        nc.tensor.matmul(bank[g % 2 * 2][:, o], p[:, 0:128], v(0), start=True, stop=True,
                                         skip_group_check=True)
                        nc.tensor.matmul(bank[g % 2 * 2 + 1][:, o], p[:, 128:256], v(0), start=True, stop=False,
                                         skip_group_check=True)
                        nc.tensor.matmul(bank[g % 2 * 2 + 1][:, o], p[:, 256:384], v(1), start=False, stop=True,
                                         skip_group_check=True).then_inc(valued, 1)

            def act(self, act):
                for i in range(len(self.units)):
                    g, uu = i // self.G, i % self.G
                    act.wait_ge(maxed, self.u + i + 1)
                    if i >= 3:
                        act.wait_ge(turned, self.u + i - 2)
                    if uu == 0 and g >= 2:
                        act.wait_ge(grouped, self.g + g - 1)
                    for t0, (a, n) in enumerate(((0, 128), (128, 256))):
                        last = nc.scalar.activation(E[i % 3][:, a:a + n], bank[4 + i % 3][:, a:a + n], ACT.Exp,
                                                    bias=nmax[:, i % 3, t0:t0 + 1],
                                                    accum_out=rs[:, g % 2, t0, uu:uu + 1])
                    last.then_inc(exped, 1)

            def dve(self, dve):
                U, G = len(self.units), self.G
                for i in range(U + 3):
                    if i < U:
                        dve.wait_ge(scored, self.u + i + 1)
                        if i >= 3:
                            dve.wait_ge(exped, self.u + i - 2)
                        for t0, (a, n) in enumerate(((0, 128), (128, 256))):
                            last = nc.vector.tensor_reduce(nmax[:, i % 3, t0:t0 + 1], bank[4 + i % 3][:, a:a + n],
                                                           AX.X, ALU.max, negate=True)
                        last.then_inc(maxed, 1)
                    if 2 <= i < U + 2:
                        j = i - 2
                        dve.wait_ge(turned, self.u + j + 1)
                        if j >= 2:
                            dve.wait_ge(valued, self.u + j - 1)
                        nc.vector.tensor_copy(PT[j % 2], bank[7][:, 0:384]).then_inc(copied, 1)
                    if i >= 3 and (i - 3) % G == G - 1:
                        g = (i - 3) // G
                        dve.wait_ge(valued, self.u + i - 2)
                        link(dve, nc.vector.reciprocal(rr[:, :, 0:G], rs[:, g % 2, :, 0:G]))
                        self.finish(dve, g)

            def wait(self, eng):
                eng.wait_ge(grouped, self.g + len(self.units) // self.G)

            def bank_of(self, g, tt):
                return bank[g % 2 * 2 + tt][:, :].rearrange("p (u d) -> p u d", d=self.dv)

        def per_head(tt, G, dv):
            return rr[:, tt, 0:G].unsqueeze(2).to_broadcast([128, G, dv])

        def heads_T(cols, dests, scale):
            return [(lambda tt, c=c: P[:, tt, c:c + 128], d, scale) for c, d in zip(cols, dests)]

        def xt_dest(k):
            return XTH[:, k, :], XTL[:, k, :]

        def normed(gain):
            return [(lambda tt, k=k: O[:, tt, k * 128:k * 128 + 128], xt_dest(k), gain and col(gain[0], gain[1] + k))
                    for k in range(KD)]

        xt = lambda kt, tt: (XTH[:, kt, tt * 128:tt * 128 + 128], XTL[:, kt, tt * 128:tt * 128 + 128])
        pcol = lambda c0, n: (lambda tt: P[:, tt, c0:c0 + n])

        ss_ready, ms_ready = sem("ss_ready"), sem("ms_ready")
        x_ready, squared, scale_set, n_made = (sem("norm_" + x) for x in ("x", "squared", "scale", "made"))
        band_in, rel_in, c_hi0, c_lo0 = sem("band_in"), sem("rel_in"), sem("c_hi0"), sem("c_lo0")

        ada_ps, ada_used = sem("ada_ps"), sem("ada_used")
        h1 = sem("h1")
        T1 = Transposes(normed(None), split=True)
        P1 = Project([(c_in1[i], 512, pcol(in1_order[i], 512), {512: ACT.Silu, 2560: ACT.Silu}.get(in1_order[i], ACT.Copy)
                       if in1_order[i] < 3072 else ACT.Sigmoid) for i in range(10)], xt)
        roped1 = sem("roped1")
        TQ1 = Transposes(heads_T([1024 + 128 * i for i in range(4)], [QT[:, i, :] for i in range(4)], 0.125)
                         + heads_T([1536 + 128 * i for i in range(4)], [KT[:, i, :] for i in range(4)], None))
        d_made, d_copied, y_made, y_gated = sem("d_made"), sem("d_copied"), sem("y_made"), sem("y_gated")
        O_FLAT = O[:, :, :].rearrange("p t n -> p (t n)")
        BAND = O_FLAT[:, 0:1536].rearrange("p (g n) -> p g n", g=4)
        GRP = O_FLAT[:, 1536:2048].rearrange("p (g n) -> p g n", g=4)
        C_COLUMNS = vec[:, VEC_ROWS["c"][0]:VEC_ROWS["c"][0] + 8].unsqueeze(2).to_broadcast([128, 8, 128])
        C_PARTS = [x[:, :, :].rearrange("p k s -> p (k s)").rearrange("p (k m) -> p k m", k=KD) for x in (HTH, HTL)]
        TY1 = Transposes([(lambda tt, g=g: P[:, tt, g * 128:g * 128 + 128], xt_dest(g), col("pool_scale", g))
                                 for g in range(4)], split=True)
        UP1 = OutProduct(c_pup, xt)
        up_used = sem("up_used")
        TA1 = Transposes([(lambda tt, k=k: O[:, tt, k * 128:k * 128 + 128], xt_dest(4 + k), None) for k in range(4)],
                         split=True)
        gated1 = sem("gated1")
        AUP1 = OutProduct(c_aup, lambda kt, tt: xt(4 + kt, tt))
        merged = sem("merged")
        TM1 = Transposes([(lambda tt, k=k: P[:, tt, 3072 + k * 128:3200 + k * 128], xt_dest(k), None) for k in range(8)],
                         split=True)
        OUT1 = OutProduct(c_out1, xt)
        gfin_in, gfin2_in = sem("gfin_in"), sem("gfin2_in")

        SHIFT = O[:, 0, :]
        GAIN = KT[:, 4:8, :].rearrange("p k s -> p (k s)")
        GATE = QT[:, 4:8, :].rearrange("p k s -> p (k s)")
        B_ADA = P[:, 0, 0:3072]
        G_NORM = P[:, 1, 0:1024]
        XN = P[:, :, 3072:4096]

        def plain_finish(get):
            def finish(dve, g):
                for tt in range(TT):
                    last = nc.vector.tensor_tensor(O[:, tt, g * 512:g * 512 + 512].rearrange("p (u d) -> p u d", d=DH),
                                                   get().bank_of(g, tt), per_head(tt, 8, DH), ALU.mult)
                last.then_inc(grouped, 1)
            return finish

        def at(h):
            return h // 2, (h % 2) * 64

        def values(c0, n):
            return lambda kt: P[:, kt, c0:c0 + n]

        A1 = Attention([(at(h), at(h), values(2048 + 64 * h, 64)) for h in range(8)], 64, mask_causal,
                       plain_finish(lambda: A1))

        roped2 = sem("roped2")
        T2 = Transposes(normed(("ev_attn", 0)), split=True)
        P2 = Project([(c_in2[i], 512, pcol(in2_order[i], 512), ACT.Copy) for i in range(6)], xt)
        TS2 = Transposes(heads_T([128 * i for i in range(4)], [QT[:, i, :] for i in range(4)], 0.125)
                         + heads_T([512 + 128 * i for i in range(4)], [KT[:, i, :] for i in range(4)], None))
        TD2 = Transposes(heads_T([1536 + 128 * i for i in range(4)], [QT[:, 4 + i, :] for i in range(4)], 0.125)
                         + heads_T([2048 + 128 * i for i in range(4)], [KT[:, 4 + i, :] for i in range(4)], None))
        st_z, st_ln, st_sp, st_r, st_w, st_v, st_done = (sem("st_" + x) for x in ("z", "ln", "sp", "r", "w", "v", "done"))
        lam_dot, lam_exp = sem("lam_dot"), sem("lam_exp")
        cs_ang, cs_set = sem("cs_ang"), sem("cs_set")

        def diff_finish(dve, g):
            odd = rr[:, :, 0:4].rearrange("p t (h m) -> p t h m", m=2)[:, :, :, 1]
            link(dve, nc.vector.tensor_scalar(odd, odd, lam[:, 0:1], None, ALU.mult))
            for tt in range(TT):
                tmp = P[:, tt, 0:512].rearrange("p (u d) -> p u d", d=128)
                link(dve, nc.vector.tensor_tensor(tmp, A2.bank_of(g, tt), per_head(tt, 4, 128), ALU.mult))
                pair = P[:, tt, 0:512].rearrange("p (h m d) -> p h m d", m=2, d=128)
                last = nc.vector.tensor_tensor(O[:, tt, 512 + 256 * g:768 + 256 * g].rearrange("p (h d) -> p h d", d=128),
                                               pair[:, :, 0, :], pair[:, :, 1, :], ALU.add)
            last.then_inc(grouped, 1)
            dve.wait_ge(grouped, A2.g + g + 1)

        A2 = Attention([((4 + u // 2, (u % 2) * 64), (4 + u // 2, (u % 2) * 64), values(2560 + 128 * (u // 2), 128))
                              for u in range(8)], 128, mask_chunk, diff_finish)
        o2 = sem("o2")
        TO2 = [Transposes(normed(None)[4 * i:4 * i + 4], split=True) for i in range(2)]
        OUT2 = [OutProduct(c_out2[2 * i:2 * i + 2], xt) for i in range(2)]
        T3 = Transposes(normed(("ev_ffn", 0)), split=True)
        ffn_silu, ffn_mul, ffn_T, ffn_Th, ffn_Tl = (sem("ffn_" + x) for x in ("silu", "mul", "T", "Th", "Tl"))
        ht = lambda kt, tt: (HTH[:, kt, tt * 128:tt * 128 + 128], HTL[:, kt, tt * 128:tt * 128 + 128])
        DOWN = [OutProduct(c_down[f], ht) for f in range(NF)]
        HID = P[:, 0, 0:2048].rearrange("p (f t n) -> p f t n", f=2, t=TT)
        roped4 = sem("roped4")
        T4 = Transposes(normed(("od_attn", 0)), split=True)
        P4 = Project([(c_in3[i], 512, pcol(512 * i, 512), ACT.Copy) for i in range(6)], xt)
        TQ4 = Transposes(heads_T([128 * i for i in range(8)], [QT[:, i, :] for i in range(8)], 0.125)
                         + heads_T([1024 + 128 * i for i in range(8)], [KT[:, i, :] for i in range(8)], None))

        def rel_extra(i, t0, out):
            bias = P[:, i // 8, 3072 + 256 * (i % 8):3328 + 256 * (i % 8)]
            nc.tensor.matmul(out, ident[:, :], bias[:, 128:256] if t0 == 0 else bias, start=False, stop=False,
                             skip_group_check=True)

        A4 = Attention([(at(h), at(h), values(2048 + 64 * h, 64)) for h in range(16)], 64, mask_chunk,
                       plain_finish(lambda: A4), rel_extra, fill=0)
        TO4 = Transposes(normed(None), split=True)
        OUT4 = OutProduct(c_out3, xt)
        T5 = Transposes(normed(("od_ffn", 0)), split=True)

        lg_ps, lg_exp, lg_exped, picked, cnt_ps, list_set = (sem("moe_" + x) for x in
                                                            ("lg", "lgexp", "lgexped", "picked", "cnt", "list"))
        m_sel, m_selg, m_x, m_xh, m_xl, m_ct, m_ctc = (sem("m_" + x) for x in ("sel", "selg", "x", "xh", "xl", "ct", "ctc"))
        m_silu, m_mul, m_T, m_Th, m_Tl = (sem("m_" + x) for x in ("silu", "mul", "T", "Th", "Tl"))
        m_y, m_ya, m_yd, m_s, m_acc = (sem("m_" + x) for x in ("y", "ya", "yd", "s", "acc"))
        flatP = P[:, :, :].rearrange("p t n -> p (t n)")
        at_ = [0]

        def pview(n):
            at_[0] += n
            return flatP[:, at_[0] - n:at_[0]]

        MHT = [[x[:, :, :].rearrange("p k s -> p (k s)")[:, 512 * b:512 * b + 512] for x in (HTH, HTL)] for b in range(2)]
        MHID = pview(4 * 512).rearrange("p (a b n) -> p a b n", a=2, b=2)
        MY = pview(D)
        MSEL = pview(2 * 128).rearrange("p (t s) -> p t s", t=2)
        MSELG = pview(2 * 128).rearrange("p (t s) -> p t s", t=2)
        MCOMB = pview(S)
        IOTA = pview(128)
        LG = pview(2 * NEXP).rearrange("p (t e) -> p t e", t=2)
        MASK = pview(2 * NEXP).rearrange("p (t e) -> p t e", t=2)
        OH1 = pview(2 * NEXP).rearrange("p (t e) -> p t e", t=2)
        OH2 = pview(2 * NEXP).rearrange("p (t e) -> p t e", t=2)
        GW = pview(2 * NEXP).rearrange("p (t e) -> p t e", t=2)
        KEY = pview(2 * NEXP).rearrange("p (t e) -> p t e", t=2)
        TMP = pview(2 * NEXP).rearrange("p (t e) -> p t e", t=2)
        IDX = pview(NEXP)
        RIDX = pview(NEXP)
        MM = pview(8).rearrange("p (t k) -> p t k", t=2)
        CNT = pview(NEXP)
        TE = pview(NEXP)
        CUM = pview(NEXP)
        WIDX = pview(TILE_MAX)
        WE = pview(TILE_MAX * NEXP).rearrange("p (w e) -> p w e", w=TILE_MAX)
        WE2 = pview(TILE_MAX * NEXP).rearrange("p (w e) -> p w e", w=TILE_MAX)
        EW = pview(TILE_MAX)
        JW = pview(TILE_MAX)
        KS = pview(2 * (TILE_MAX + 1)).rearrange("p (t w) -> p t w", t=2)
        GSEL = pview(2 * TILE_MAX).rearrange("p (t w) -> p t w", t=2)
        WI = pview(2 * TILE_MAX * NEXP).rearrange("p (t w e) -> p t w e", t=2, w=TILE_MAX)
        WORK = pview(TILE_MAX + 1).bitcast(I32)
        iota_set = sem("iota_set")
        p_free = sem("p_free")

        T6 = Transposes(normed(("norm3", 0)), split=True)
        P6 = Project([(c_in4[i], 512, pcol(512 * i, 512), ACT.Copy) for i in range(6)]
                     + [(c_f, 16, pcol(3072, 16), ACT.Copy)]
                     + [(c_z4[i], 512, pcol(3584 + 512 * i, 512), ACT.Silu) for i in range(2)], xt)
        TQ6 = Transposes(heads_T([128 * i for i in range(8)], [QT[:, i, :] for i in range(8)], 0.125)
                         + heads_T([1024 + 128 * i for i in range(8)], [KT[:, i, :] for i in range(8)], None))
        f_in, f_ln, f_log, f_c, f_cc = (sem("f_" + x) for x in ("in", "ln", "log", "c", "cc"))
        FX = P[:, :, 3072:3088]
        FA = P[:, :, 3088:3104]
        FC = P[0:16, 0, 4608:4608 + S]

        def fox_extra(i, t0, out):
            nc.tensor.matmul(out, ident[0:16, i:i + 1].to_broadcast([16, 128]), FC[:, 0:128 + 128 * t0], start=False,
                             stop=False, skip_group_check=True)

        A6 = Attention([(at(h), at(h), values(2048 + 64 * h, 64)) for h in range(16)], 64, mask_causal,
                       plain_finish(lambda: A6), fox_extra, fill=12)
        g6 = sem("g6")
        TO6 = Transposes(normed(None), split=True)
        OUT6 = OutProduct(c_out4, xt)

        roped7 = sem("roped7")
        T7 = Transposes(normed(("norm3", 8)), split=True)
        P7 = Project([(c_in5[i], 512, pcol(in5_order[i], 512), ACT.Copy) for i in range(5)]
                     + [(c_g5, 48, pcol(2560, 48), ACT.Sigmoid)]
                     + [(c_z5[i], 512, pcol(3072 + 512 * i, 512), ACT.Silu) for i in range(2)], xt)

        twice_p = lambda n: (lambda tt: P[:, tt, 4096 + 128 * n:4224 + 128 * n])
        twice_o = lambda n: (lambda tt: O[:, tt, 128 * n:128 * n + 128])
        TQ7 = Transposes(heads_T([128 * i for i in range(8)], [QT[:, i, :] for i in range(8)], 0.125)
                         + [(twice_p(n), KT[:, n, :], None) for n in range(8)])
        c_T, c_A, c_full, c_hi, c_lo = (sem("c_" + x) for x in ("T", "A", "full", "hi", "lo"))
        c_s, c_hT, c_hTh, c_hTl, c_roped, c_kT, c_kTc = (sem("cmp_" + x) for x in
                                                         ("s", "hT", "hTh", "hTl", "roped", "kT", "kTc"))
        q_s, q_m, q_e, q_p, q_T, q_Tc, q_v, q_o = (sem("cq_" + x) for x in ("s", "m", "e", "p", "T", "Tc", "v", "o"))
        block_tiles = lambda j: P[:, j, 4096:5120].rearrange("p (k r) -> p k r", k=8)
        xblocks = [x[:, :, :].rearrange("p k s -> p (k s)").rearrange("p (k r) -> p k r", k=16) for x in (XTH, XTL)]
        CH = [scr[:, 0:256], scr[:, 256:512]]
        CHT = [[x[:, i, :].rearrange("p (k r) -> p k r", k=2) for x in (HTH, HTL)] for i in range(2)]
        KCN = scr[:, 1024:1152].rearrange("p (a d) -> p a d", a=2)
        KCT = scr[:, 1152:1280]
        VCB = scr[:, 1280:1536]
        CS, CPT = scr[:, 0:512], scr[:, 512:1024]

        def nsa_finish(dve, g):
            branch, h0 = 1 + g // 2, (g % 2) * 8
            gates = P[:, :, 2560:2608].rearrange("p t (h b) -> p t h b", b=3)[:, :, h0:h0 + 8, branch]
            link(dve, nc.vector.tensor_tensor(rr[:, :, :], rr[:, :, :], gates, ALU.mult))
            for tt in range(TT):
                tmp = P[:, tt, 4096:4608].rearrange("p (u d) -> p u d", d=DH)
                link(dve, nc.vector.tensor_tensor(tmp, A7.bank_of(g, tt), per_head(tt, 8, DH), ALU.mult))
                o = O[:, tt, h0 * 64:h0 * 64 + 512].rearrange("p (u d) -> p u d", d=DH)
                last = nc.vector.tensor_tensor(o, o, tmp, ALU.add)
            last.then_inc(grouped, 1)
            dve.wait_ge(grouped, A7.g + g + 1)

        def group_key(branch, h):
            return branch * 4 + h // 4, (h % 2) * 64

        A7 = Attention([(at(h), group_key(b, h), values((1792, 2304)[b] + 64 * (h // 4), 64))
                              for b in range(2) for h in range(16)], 64, mask_causal, nsa_finish, fill=12)
        g7 = sem("g7")
        TO7 = Transposes(normed(None), split=True)
        OUT7 = OutProduct(c_out5, xt)
        out_set, out_sent = sem("out_set"), sem("out_sent")

        counts = {"dve": 0, "act": 0}
        moe_tiles = {}

        def link(dve, ins):
            counts["dve"] += 1
            ins.then_inc(dve_chain, 1)
            dve.wait_ge(dve_chain, counts["dve"])

        def link_act(act, ins):
            counts["act"] += 1
            ins.then_inc(act_chain, 1)
            act.wait_ge(act_chain, counts["act"])

        def keep_warm(b, n):
            for _ in range(n):
                nc.tensor.matmul(bank[b][:, 0:128], ones[:, :], ident[:, :], start=True, stop=True, skip_group_check=True)

        def reach(eng, signal, count, n, per_tile=MOE_CHUNKS):
            eng.wait_ge(signal, moe_tiles[eng.engine] * per_tile + count if after_moe(n) else count)

        def take(pe, n):
            _, nk, width = stream[n]
            reach(pe, lo_made, n + 1, n)
            return parts(n, nk, width)

        next_split = {}

        def split_hi(act, n, nk, width):
            wh = parts(n, nk, width)[0]
            nc.scalar.activation(wh, slot_ap(n, nk, width), ACT.Copy).then_inc(hi_made, 1)

        def split_lo(dve, n, nk, width):
            wh, wl = parts(n, nk, width)
            nc.vector.tensor_tensor(wl, slot_ap(n, nk, width), wh.bitcast(F32), ALU.subtract).then_inc(lo_made, 1)

        def split_until(eng, end):
            start = next_split.get(eng.engine, 0)
            limit = len(stream) if after_moe(start) or eng.engine in moe_tiles else N0
            for n in range(start, min(end, limit)):
                _, nk, width = stream[n]
                if eng.engine == mybir.EngineType.Activation:
                    reach(eng, landed[n % RING], 16 * (n // RING + 1), n, 16 * MOE_CHUNKS // RING)
                    if n >= SPLIT:
                        reach(eng, consumed, n - SPLIT + 1, n)
                    split_hi(eng, n, nk, width)
                else:
                    reach(eng, hi_made, n + 1, n)
                    split_lo(eng, n, nk, width)
                next_split[eng.engine] = n + 1

        def used(eng, n):
            reach(eng, consumed, n + 1, n)

        def inverse_roots(dve, view, width):
            counts["root"] = counts.get("root", 0) + 1
            nc.vector.tensor_scalar(view, view, 1.0 / width, EPS, ALU.mult, ALU.add).then_inc(ss_ready, 1)
            dve.wait_ge(ms_ready, counts["root"])
            link(dve, nc.vector.reciprocal(view, view))

        def roots(act, view):
            counts["act_root"] = counts.get("act_root", 0) + 1
            act.wait_ge(ss_ready, counts["act_root"])
            nc.scalar.activation(view, view, ACT.Sqrt).then_inc(ms_ready, 1)

        def rms(dve):
            counts["rms"] = counts.get("rms", 0) + 1
            counts["root"] = counts.get("root", 0) + 1
            dve.wait_ge(squared, TT * counts["rms"])
            link(dve, nc.vector.tensor_scalar(stat[:, 0:2], stat[:, 0:2], 1.0 / D, EPS, ALU.mult, ALU.add))
            nc.vector.reciprocal(stat[:, 0:2], stat[:, 0:2]).then_inc(ss_ready, 1)
            dve.wait_ge(ms_ready, counts["root"])

        def rms_act(act, scratch):
            for tt in range(TT):
                counts["act_rms"] = counts.get("act_rms", 0) + 1
                act.wait_ge(x_ready, counts["act_rms"])
                nc.scalar.activation(scratch[:, tt, :], X[:, tt, :], ACT.Square,
                                     accum_out=stat[:, tt:tt + 1]).then_inc(squared, 1)
            roots(act, stat[:, 0:2])

        def norm(dve):
            rms(dve)
            nc.vector.tensor_scalar(O[:, 0, :], X[:, 0, :], stat[:, 0:1], None, ALU.mult).then_inc(n_made, 1)

        def norm_act(act):
            rms_act(act, O)
            act.wait_ge(ms_ready, counts["act_root"])
            nc.scalar.activation(O[:, 1, :], X[:, 1, :], ACT.Copy, scale=stat[:, 1:2]).then_inc(n_made, 1)

        def add_to_x(dve, stage):
            stage.splits(dve)
            stage.wait(dve)
            for tt in range(TT):
                for half in range(2):
                    xs = X[:, tt, half * 512:half * 512 + 512]
                    last = nc.vector.tensor_tensor(xs, bank[2 * tt + half][:, :], xs, ALU.add)
                last.then_inc(x_ready, 1)
                counts["x"] = counts.get("x", 0) + 1
            dve.wait_ge(x_ready, counts["x"] + counts.get("x_more", 0))

        def rope(dve, view, cos, sin, heads, tiles):
            v = view.rearrange("p t (h d) -> p t h d", d=DH)
            x1, x2 = v[:, :, :, 0:8], v[:, :, :, 8:16]
            n = tiles * heads * 8
            t1, t2, t3, t4 = (scr[:, i * 256:i * 256 + n].rearrange("p (t h d) -> p t h d", t=tiles, d=8) for i in range(4))
            for tt in range(tiles):
                c = cos[:, tt, :].unsqueeze(1).to_broadcast([128, heads, 8])
                s = sin[:, tt, :].unsqueeze(1).to_broadcast([128, heads, 8])
                nc.vector.tensor_tensor(t1[:, tt], x1[:, tt], c, ALU.mult)
                nc.vector.tensor_tensor(t2[:, tt], x2[:, tt], s, ALU.mult)
                nc.vector.tensor_tensor(t3[:, tt], x2[:, tt], c, ALU.mult)
                last = nc.vector.tensor_tensor(t4[:, tt], x1[:, tt], s, ALU.mult)
            link(dve, last)
            for tt in range(tiles):
                nc.vector.tensor_tensor(x1[:, tt], t1[:, tt], t2[:, tt], ALU.subtract)
                last = nc.vector.tensor_tensor(x2[:, tt], t3[:, tt], t4[:, tt], ALU.add)
            link(dve, last)

        def head_sums(dve, c0):
            for tt in range(TT):
                last = nc.vector.tensor_tensor(O[:, tt, :], P[:, tt, c0:c0 + D], P[:, tt, c0:c0 + D], ALU.mult)
            link(dve, last)
            for tt in range(TT):
                last = nc.vector.tensor_reduce(stat[:, 16 + 16 * tt:32 + 16 * tt],
                                               O[:, tt, :].rearrange("p (h d) -> p h d", d=DH), AX.X, ALU.add)
            link(dve, last)
            counts["root"] = counts.get("root", 0) + 1
            nc.vector.tensor_scalar(stat[:, 16:48], stat[:, 16:48], 1.0 / DH, EPS, ALU.mult, ALU.add).then_inc(ss_ready, 1)

        def head_norm(dve, c0, gains):
            dve.wait_ge(ms_ready, counts["root"])
            link(dve, nc.vector.reciprocal(stat[:, 16:48], stat[:, 16:48]))
            for tt in range(TT):
                v = P[:, tt, c0:c0 + D].rearrange("p (h d) -> p h d", d=DH)
                last = nc.vector.tensor_tensor(v, v, stat[:, 16 + 16 * tt:32 + 16 * tt].unsqueeze(2).to_broadcast([128, 16, DH]),
                                               ALU.mult)
            link(dve, last)
            for tt in range(TT):
                for h, n, name in gains:
                    v = P[:, tt, c0 + h * DH:c0 + (h + n) * DH].rearrange("p (h d) -> p h d", d=DH)
                    last = nc.vector.tensor_tensor(v, v, row(name).unsqueeze(1).to_broadcast([128, n, DH]), ALU.mult)
            link(dve, last)

        cos0 = con("cos").rearrange("p (t d) -> p t d", d=8)
        sin0 = con("sin").rearrange("p (t d) -> p t d", d=8)
        cos2 = cs2[:, 0, :].rearrange("p (t d) -> p t d", d=8)
        sin2 = cs2[:, 1, :].rearrange("p (t d) -> p t d", d=8)

        def expert_chunk(n):
            return (2, D) if moe_order[(n - N0) % MOE_CHUNKS][0] == "down" else (4, 512)

        def select(dve, w):
            for tt in range(TT):
                last = nc.vector.tensor_scalar(MSEL[:, tt, :], IOTA, KS[:, tt, bass.ds(w, 1)], None, ALU.is_equal)
            last.then_inc(m_sel, 1)

        def gathered_hi(act, w):
            for j in range(2):
                act.wait_ge(m_x, w * 2 + (j + 1))
                for k in range(4):
                    last = nc.scalar.activation(XTH[:, 4 * j + k, 0:128], bank[2 + j][:, k * 128:k * 128 + 128], ACT.Copy,
                                                scale=col("od_ffn", 4 * j + k))
                last.then_inc(m_xh, 1)

        def gathered_lo(dve, w):
            for j in range(2):
                dve.wait_ge(m_xh, w * 2 + (j + 1))
                for k in range(4):
                    last = nc.vector.scalar_tensor_tensor(out=XTL[:, 4 * j + k, 0:128],
                                                          in0=bank[2 + j][:, k * 128:k * 128 + 128],
                                                          scalar=col("od_ffn", 4 * j + k),
                                                          in1=XTH[:, 4 * j + k, 0:128].bitcast(F32),
                                                          op0=ALU.mult, op1=ALU.subtract)
                last.then_inc(m_xl, 1)

        def gather(pe, w):
            pe.wait_ge(m_sel, w + 1)
            for k in range(8):
                for tt in range(TT):
                    last = nc.tensor.matmul(bank[2 + k // 4][:, (k % 4) * 128:(k % 4) * 128 + 128],
                                            O[:, tt, k * 128:k * 128 + 128], MSEL[:, tt, :], start=tt == 0, stop=tt == 1,
                                            skip_group_check=True)
                if k % 4 == 3:
                    last.then_inc(m_x, 1)

        def scatter(pe, w):
            pe.wait_ge(m_ya, w + 1)
            pe.wait_ge(m_yd, w + 1)
            for tt in range(TT):
                for half in range(2):
                    last = nc.tensor.matmul(bank[4 + 2 * tt + half][:, :], MCOMB[:, tt * 128:tt * 128 + 128],
                                            MY[:, half * 512:half * 512 + 512], start=True, stop=True)
            last.then_inc(m_s, 1)

        def scatter_add(dve, w, signal):
            dve.wait_ge(m_s, w + 1)
            for tt in range(TT):
                for half in range(2):
                    xs = X[:, tt, half * 512:half * 512 + 512]
                    last = nc.vector.tensor_tensor(xs, bank[4 + 2 * tt + half][:, :], xs, ALU.add)
                if tt or signal is x_ready:
                    last.then_inc(signal, 1)

        def moe_hi(act, w, cs):
            for c in cs:
                n = N0 + c
                act.wait_ge(landed[n % RING], w * (16 * MOE_CHUNKS // RING) + 16 * (n // RING + 1))
                act.wait_ge(consumed, w * MOE_CHUNKS + (n - SPLIT + 1))
                split_hi(act, n, *expert_chunk(n))

        def moe_lo(dve, w, cs):
            for c in cs:
                n = N0 + c
                dve.wait_ge(hi_made, w * MOE_CHUNKS + (n + 1))
                split_lo(dve, n, *expert_chunk(n))

        block = ctx.enter_context(nc.Block())

        @block.sync
        def _(sp):
            def load(n):
                ap, nk, width = stream[n]
                if n >= RING:
                    reach(sp, lo_made, n - RING + 1, n)
                sp.dma_start(slot_ap(n, nk, width), ap).then_inc(landed[n % RING], 16)

            for n in range(N0):
                load(n)
            sp.wait_ge(list_set, 1)
            tiles = sp.value_load(WORK[0:1, TILE_MAX:TILE_MAX + 1], min_val=4, max_val=TILE_MAX)
            moe_tiles[sp.engine] = tiles
            gate, up, down = (t[n][0] for n in ("od_we_gate_2", "od_we_up_2", "od_we_down_2"))
            with sp.Fori(0, tiles) as i:
                e = sp.value_load(WORK[0:1, bass.ds(i, 1)], min_val=0, max_val=NEXP - 1)
                for c, (what, f, half) in enumerate(moe_order):
                    n = N0 + c
                    sp.wait_ge(lo_made, i * MOE_CHUNKS + (n - RING + 1))
                    if what == "down":
                        k0 = 4 * f + 2 * half
                        src = down[bass.ds(e, 1), k0 * 128:(k0 + 2) * 128, :].rearrange("e (k p) n -> p (e k) n", p=128)
                    else:
                        src = (gate if what == "gate" else up)[bass.ds(e, 1), 512 * half:512 * half + 512, 512 * f:512 * f + 512]
                        src = src.rearrange("e (k p) n -> p (e k) n", p=128)
                    sp.dma_start(slot_ap(n, *expert_chunk(n)), src).then_inc(landed[n % RING], 16)
            for n in range(N0, len(stream)):
                load(n)
            sp.wait_ge(out_set, 1)
            sp.dma_start(t["out"].rearrange("b (t p) n -> p (b t) n", p=128), X[:, :, :]).then_inc(out_sent, 16)
            sp.wait_ge(out_sent, 16)

        @block.gpsimd
        def _(pool):
            for tile, value in ((ident, 0.0), (identb, 0.0), (mask_causal, 0.0), (mask_chunk, 0.0), (mask_past, 0.0),
                                (past01, 1.0), (neg_tri, -1.0), (neg_ones, -1.0), (ones, 1.0)):
                nc.gpsimd.memset(tile[:, :], value).then_inc(ones_set, 1)
            pool.wait_ge(ones_set, 9)

            def select(tile, step, base, multiplier, op, fill):
                nc.gpsimd.affine_select(out=tile[:, :], in_=tile[:, :], compare_op=op, fill=fill, base=base,
                                        pattern=[[step, 128]], channel_multiplier=multiplier).then_inc(const_set, 1)

            select(ident, -1, 0, 1, ALU.not_equal, 1.0)
            select(identb, -1, 0, 1, ALU.not_equal, 1.0)
            select(mask_causal, -1, 0, 1, ALU.is_ge, -BIG)
            select(mask_past, 1, 0, -1, ALU.is_gt, -BIG)
            select(past01, 1, 0, -1, ALU.is_gt, 0.0)
            select(neg_tri, -1, 0, 1, ALU.is_ge, 0.0)
            nc.gpsimd.memset(mask_chunk[0:64, 64:128], -BIG).then_inc(const_set, 1)
            pool.wait_ge(p_free, 1)
            nc.gpsimd.iota(IOTA, pattern=[[1, 128]], base=0, channel_multiplier=0,
                           allow_small_or_imprecise_dtypes=True).then_inc(iota_set, 1)
            nc.gpsimd.iota(IDX, pattern=[[1, NEXP]], base=0, channel_multiplier=0,
                           allow_small_or_imprecise_dtypes=True).then_inc(iota_set, 1)
            nc.gpsimd.iota(WIDX, pattern=[[1, TILE_MAX]], base=0, channel_multiplier=0,
                           allow_small_or_imprecise_dtypes=True).then_inc(iota_set, 1)
            pool.wait_ge(iota_set, 3)

        N_CONST = 7

        @block.scalar
        def _(act):
            act.dma_start(O[0:NVEC, 1, 0:128], t["vec"]).then_inc(vec_in, 16)
            act.dma_start(B_ADA, t["b_ada"].rearrange("a n -> (a n)").partition_broadcast(128)).then_inc(ada_in, 16)
            act.dma_start(G_NORM, t["g_norm"].rearrange("a n -> (a n)").partition_broadcast(128)).then_inc(ada_in, 16)
            act.dma_start(X[:, :, :], t["x"].rearrange("b (t p) n -> p (b t) n", p=128)).then_inc(small_in, 16)
            act.dma_start(small[:, :], t["small"].partition_broadcast(128)).then_inc(small_in, 16)
            act.dma_start(co[:, :], t["co"]).then_inc(small_in, 16)
            with nc.allow_non_contiguous_dma(reason="256 positions"):
                act.dma_start(posi[:, :], t["positions_2"].rearrange("b (t p) -> p (b t)", p=128)).then_inc(small_in, 16)

            act.wait_ge(vec_set, 1)
            nc.scalar.activation(C_PARTS[0], C_COLUMNS, ACT.Copy).then_inc(c_hi0, 1)
            split_until(act, c_ada[1][-1][0] + SPLIT)
            rms_act(act, XN)
            split_until(act, c_ada[5][-1][0] + SPLIT)
            T1.act(act)
            T1.wait(act)
            act.dma_start(BAND, t["band"]).then_inc(band_in, 16)
            act.dma_start(GRP, t["w_pool_grp"][0].rearrange("g c d -> c g d")).then_inc(band_in, 16)
            P1.act(act)
            TQ1.act(act)
            A1.act(act)
            TY1.act(act)
            TA1.act(act)
            act.wait_ge(h1, 1)
            act.dma_start(GAIN, t["g_final"].partition_broadcast(128)).then_inc(gfin_in, 16)
            UP1.splits(act)
            AUP1.splits(act)
            TM1.act(act)
            TM1.wait(act)
            for j in range(2):
                act.dma_start(P[:, j, 3072:5120].rearrange("p (h n) -> p h n", h=8),
                              t["rel"][:, 8 * j:8 * j + 8, :]).then_inc(rel_in, 16)
            OUT1.splits(act)
            rms_act(act, O)

            norm_act(act)
            T2.act(act)

            def tables():
                act.wait_ge(cs_ang, 1)
                link_act(act, nc.scalar.activation(cs2[:, 0, :], cs2[:, 0, :], ACT.Sin))
                nc.scalar.activation(cs2[:, 1, :], cs2[:, 1, :], ACT.Sin).then_inc(cs_set, 1)
                act.wait_ge(lam_dot, 1)
                nc.scalar.activation(lam[:, 2:4], lam[:, 2:4], ACT.Exp).then_inc(lam_exp, 1)

            P2.act(act, {1: tables, 2: lambda: roots(act, stat[:, 16:48])})
            TS2.act(act)
            TD2.act(act)
            for i in range(9):
                if i < 8:
                    act.wait_ge(st_z, i + 1)
                    if i >= 2:
                        act.wait_ge(st_r, i - 1)
                    e = E[i % 2]
                    link_act(act, nc.scalar.activation(e, bank[4 + i % 2][:, 0:384], ACT.Abs))
                    link_act(act, nc.scalar.activation(e, e, ACT.Exp, scale=-1.0))
                    nc.scalar.activation(e, e, ACT.Ln, bias=1.0).then_inc(st_ln, 1)
                if i >= 1:
                    j = i - 1
                    act.wait_ge(st_r, j + 1)
                    if j >= 2:
                        act.wait_ge(st_v, j - 1)
                    nc.scalar.activation(PT[j % 2], bank[6 + j % 2][:, 0:384], ACT.Exp).then_inc(st_w, 1)
            A2.act(act)
            TO2[0].act(act)
            roots(act, stat[:, 8:16])
            OUT2[0].splits(act)
            TO2[1].act(act)
            OUT2[1].splits(act)
            norm_act(act)
            T3.act(act)
            for f, (c0, n) in enumerate(ff):
                split_until(act, c_gate[f][-1][0] + SPLIT)
                used(act, c_gate[f][-1][0])
                if f >= 2:
                    act.wait_ge(ffn_T, f - 1)
                for tt in range(TT):
                    nc.scalar.activation(HID[:, f % 2, tt, 0:n], bank[4 + 2 * tt][:, 0:n], ACT.Silu).then_inc(ffn_silu, 1)
                split_until(act, (c_down[f - 1] if f else c_up[0])[-1][0] + SPLIT)
                act.wait_ge(ffn_T, f + 1)
                for tt in range(TT):
                    last = nc.scalar.activation(HTH[:, 0:n // 128, tt * 128:tt * 128 + 128],
                                                bank[5 + 2 * tt][:, 0:n].rearrange("p (k s) -> p k s", s=128), ACT.Copy)
                last.then_inc(ffn_Th, 1)
            DOWN[-1].splits(act)

            norm_act(act)
            T4.act(act)
            P4.act(act, {2: lambda: roots(act, stat[:, 16:48]), 4: lambda: roots(act, stat[:, 16:48])})
            TQ4.act(act)
            A4.act(act)
            TO4.act(act)
            OUT4.splits(act)
            norm_act(act)
            T5.act(act)
            split_until(act, N0)
            act.wait_ge(lg_exp, 1)
            nc.scalar.activation(MM[:, :, 2], MM[:, :, 2], ACT.Exp).then_inc(lg_exped, 1)

            act.wait_ge(list_set, 1)
            tiles = act.value_load(WORK[0:1, TILE_MAX:TILE_MAX + 1], min_val=4, max_val=TILE_MAX)
            moe_tiles[act.engine] = tiles
            moe_hi(act, 0, range(0, SPLIT))
            gathered_hi(act, 0)
            with act.Fori(0, tiles) as w:
                def hidden_hi(f):
                    act.wait_ge(m_T, w * CF + (f + 1))
                    nc.scalar.activation(MHT[f % 2][0], bank[4 + f % 2][:, :], ACT.Copy).then_inc(m_Th, 1)

                done = SPLIT
                for f in range(CF):
                    last_gate = moe_at["gate", f, 1]
                    moe_hi(act, w, range(done, last_gate + SPLIT))
                    done = last_gate + SPLIT
                    act.wait_ge(consumed, w * MOE_CHUNKS + (N0 + last_gate + 1))
                    nc.scalar.activation(MHID[:, f % 2, 0, :], bank[f % 2 * 2][:, :], ACT.Silu).then_inc(m_silu, 1)
                    if f >= 1:
                        hidden_hi(f - 1)
                moe_hi(act, w, range(done, MOE_CHUNKS - 2))
                gathered_hi(act, w + 1)
                moe_hi(act, w, [MOE_CHUNKS - 2])
                hidden_hi(CF - 1)
                moe_hi(act, w, range(MOE_CHUNKS - 1, MOE_CHUNKS + 2))
                act.wait_ge(consumed, w * MOE_CHUNKS + (N0 + MOE_CHUNKS))
                nc.scalar.activation(MY[:, 0:512], bank[6][:, :], ACT.Copy).then_inc(m_ya, 1)
                moe_hi(act, w, [MOE_CHUNKS + 2])
            next_split[act.engine] = N0 + SPLIT

            norm_act(act)
            T6.act(act)

            def forget():
                act.wait_ge(f_in, 1)
                link_act(act, nc.scalar.activation(FA, FX, ACT.Abs))
                link_act(act, nc.scalar.activation(FA, FA, ACT.Exp, scale=-1.0))
                nc.scalar.activation(FA, FA, ACT.Ln, bias=1.0).then_inc(f_ln, 1)

            P6.act(act, {7: forget})
            TQ6.act(act)
            A6.act(act)
            TO6.act(act)
            OUT6.splits(act)

            norm_act(act)
            T7.act(act)
            P7.act(act)
            TQ7.act(act)
            for i in range(2):
                act.wait_ge(c_full, i + 1)
                if i:
                    used(act, c_ck[i - 1][0][-1][0])
                for j in range(2):
                    last = nc.scalar.activation(xblocks[0][:, 8 * j:8 * j + 8, :], block_tiles(j), ACT.Copy)
                last.then_inc(c_hi, 1)
                split_until(act, c_ck[i][0][-1][0] + SPLIT)
                used(act, c_ck[i][0][-1][0])
                nc.scalar.activation(CH[i], bank[4 + i][:, 0:256], ACT.Silu).then_inc(c_s, 1)
                act.wait_ge(c_hT, i + 1)
                nc.scalar.activation(CHT[i][0], bank[6 + i][:, 0:256].rearrange("p (k r) -> p k r", k=2),
                                     ACT.Copy).then_inc(c_hTh, 1)
            for tt in range(TT):
                act.wait_ge(q_m, tt + 1)
                nc.scalar.activation(CS, CS, ACT.Exp).then_inc(q_e, 1)
            A7.act(act)
            A7.wait(act)
            act.dma_start(GAIN, t["final_g_3"].partition_broadcast(128)).then_inc(gfin2_in, 16)
            TO7.act(act)
            OUT7.splits(act)
            rms_act(act, O)

        @block.vector
        def _(dve):
            dve.wait_ge(vec_ready, 1)
            link(dve, nc.vector.tensor_copy(vec[:, :], bank[7][:, 0:NVEC]))
            dve.sem_inc(vec_set, 1)
            dve.wait_ge(c_hi0, 1)
            nc.vector.tensor_tensor(C_PARTS[1], C_COLUMNS, C_PARTS[0].bitcast(F32), ALU.subtract).then_inc(c_lo0, 1)
            def modulation(m):
                split_until(dve, c_ada[m][-1][0] + SPLIT)
                if m == 0:
                    dve.wait_ge(ada_in, 16 * 2)
                used(dve, c_ada[m][-1][0])
                kind, half = ada_order[m] // 2, slice(512 * (ada_order[m] % 2), 512 * (ada_order[m] % 2) + 512)
                dest = (SHIFT, GAIN, GATE)[kind][:, half]
                nc.vector.tensor_tensor(dest, bank[m % 4][:, :], B_ADA[:, 512 * ada_order[m]:512 * ada_order[m] + 512],
                                        ALU.add).then_inc(ada_used, 1)
                if kind == 1:
                    dve.wait_ge(ada_used, m + 1)
                    link(dve, nc.vector.scalar_tensor_tensor(out=dest, in0=dest, scalar=1.0, in1=G_NORM[:, half],
                                                             op0=ALU.add, op1=ALU.mult))

            modulation(0)
            modulation(1)
            dve.wait_ge(small_in, 16 * 4)
            dve.sem_inc(x_ready, TT)
            rms(dve)
            for tt in range(TT):
                last = nc.vector.scalar_tensor_tensor(out=XN[:, tt, :], in0=X[:, tt, :], scalar=stat[:, tt:tt + 1],
                                                      in1=GAIN, op0=ALU.mult, op1=ALU.mult)
            link(dve, last)
            modulation(2)
            modulation(3)
            dve.wait_ge(ada_used, 4)
            split_until(dve, c_ada[4][-1][0] + SPLIT)
            link(dve, nc.vector.tensor_tensor(O[:, 1, :], XN[:, 1, :], SHIFT, ALU.add))
            nc.vector.tensor_tensor(O[:, 0, :], XN[:, 0, :], SHIFT, ALU.add).then_inc(h1, 1)
            modulation(4)
            modulation(5)
            T1.dve(dve)
            P1.dve(dve, {0: lambda: rope(dve, P[:, :, 1024:1536], cos0, sin0, 8, TT),
                         1: lambda: rope(dve, P[:, :, 1536:2048], cos0, sin0, 8, TT)})
            dve.sem_inc(roped1, 1)
            P1.wait(dve)
            TQ1.dve(dve)
            dve.wait_ge(d_made, 1)
            for g in range(4):
                last = nc.vector.tensor_copy(scr[:, 256 * g:256 * g + 256], bank[4 + g // 2][:, 256 * (g % 2):256 * (g % 2) + 256])
            last.then_inc(d_copied, 1)
            dve.wait_ge(y_made, 1)
            for tt in range(TT):
                last = nc.vector.tensor_tensor(P[:, tt, 0:512], bank[2 + tt][:, :], P[:, tt, 512:1024], ALU.mult)
            last.then_inc(y_gated, 1)
            A1.dve(dve)
            A1.wait(dve)
            last = nc.vector.tensor_tensor(O[:, :, 0:512], O[:, :, 0:512], P[:, :, 2560:3072], ALU.mult)
            last.then_inc(gated1, 1)
            TY1.dve(dve)
            TA1.dve(dve)
            for stage, c0 in ((UP1, 3072), (AUP1, 4096)):
                stage.splits(dve)
                stage.wait(dve)
                for tt in range(TT):
                    for half in range(2):
                        m = P[:, tt, c0 + half * 512:c0 + half * 512 + 512]
                        last = nc.vector.tensor_tensor(m, bank[2 * tt + half][:, :], m, ALU.mult)
                last.then_inc(up_used, 1)
            dve.wait_ge(up_used, 2)
            nc.vector.tensor_tensor(P[:, :, 3072:4096], P[:, :, 3072:4096], P[:, :, 4096:5120], ALU.add).then_inc(merged, 1)
            TM1.dve(dve)
            OUT1.splits(dve)
            OUT1.wait(dve)
            for tt in range(TT):
                for half in range(2):
                    last = nc.vector.tensor_tensor(O[:, tt, half * 512:half * 512 + 512], bank[2 * tt + half][:, :],
                                                   GATE[:, half * 512:half * 512 + 512], ALU.mult)
            link(dve, last)
            for tt in range(TT):
                nc.vector.tensor_tensor(X[:, tt, :], X[:, tt, :], O[:, tt, :], ALU.add).then_inc(x_ready, 1)
            rms(dve)
            dve.wait_ge(gfin_in, 16)
            for tt in range(TT):
                last = nc.vector.scalar_tensor_tensor(out=X[:, tt, :], in0=X[:, tt, :], scalar=stat[:, tt:tt + 1],
                                                      in1=GAIN, op0=ALU.mult, op1=ALU.mult)
                last.then_inc(x_ready, 1)
            dve.wait_ge(x_ready, 3 * TT)
            counts["x_more"] = 3 * TT

            norm(dve)
            T2.dve(dve)

            def angles():
                posf, ang, turns = stat[:, 48:50], cs2[:, 2, :], cs2[:, 3, :]
                link(dve, nc.vector.tensor_copy(posf, posi[:, :]))
                for tt in range(TT):
                    last = nc.vector.tensor_scalar(ang[:, 8 * tt:8 * tt + 8], con("invf"), posf[:, tt:tt + 1], None, ALU.mult)
                link(dve, last)
                magic, two_pi = 12582912.0, 2.0 * np.pi
                hi = 6.28125
                mid = round((two_pi - hi) * 2 ** 24) / 2 ** 24
                lo = two_pi - hi - mid
                for k, quarter in ((0, 0.25), (1, 0.0)):
                    r = cs2[:, k, :]
                    link(dve, nc.vector.tensor_scalar(turns, ang, float(1.0 / two_pi), quarter, ALU.mult, ALU.add))
                    link(dve, nc.vector.tensor_scalar(turns, turns, magic, None, ALU.add))
                    link(dve, nc.vector.tensor_scalar(turns, turns, magic, None, ALU.subtract))
                    link(dve, nc.vector.scalar_tensor_tensor(out=r, in0=turns, scalar=-hi, in1=ang, op0=ALU.mult, op1=ALU.add))
                    link(dve, nc.vector.scalar_tensor_tensor(out=r, in0=turns, scalar=-mid, in1=r, op0=ALU.mult, op1=ALU.add))
                    link(dve, nc.vector.scalar_tensor_tensor(out=r, in0=turns, scalar=-lo, in1=r, op0=ALU.mult, op1=ALU.add))
                    if quarter:
                        link(dve, nc.vector.tensor_scalar(r, r, float(np.pi / 2), None, ALU.add))
                    last = nc.vector.tensor_scalar(r, r, 3.1415925, -3.1415925, ALU.min, ALU.max)
                    if k == 0:
                        link(dve, last)
                last.then_inc(cs_ang, 1)
                for k, (a, b) in enumerate((("lq1", "lk1"), ("lq2", "lk2"))):
                    last = nc.vector.tensor_tensor_reduce(out=scr[:, 64 * k:64 * k + 64], in0=row(a), in1=row(b), scale=1.0,
                                                          scalar=0.0, op0=ALU.mult, op1=ALU.add, accum_out=lam[:, 2 + k:3 + k])
                last.then_inc(lam_dot, 1)

            def scale_heads():
                dve.wait_ge(lam_exp, 1)
                link(dve, nc.vector.tensor_tensor(lam[:, 0:1], lam[:, 3:4], lam[:, 2:3], ALU.subtract))
                link(dve, nc.vector.tensor_scalar(lam[:, 0:1], lam[:, 0:1], -LAM_INIT, None, ALU.add))
                head_norm(dve, 1536, [(0, 8, "ev_q"), (8, 8, "ev_k")])

            def rotate_queries():
                dve.wait_ge(cs_set, 1)
                rope(dve, P[:, :, 1536:2048], cos2, sin2, 8, TT)

            P2.dve(dve, {0: angles, 1: lambda: head_sums(dve, 1536), 2: scale_heads, 3: rotate_queries,
                         4: lambda: rope(dve, P[:, :, 2048:2560], cos2, sin2, 8, TT)})
            dve.sem_inc(roped2, 1)
            P2.wait(dve)
            TS2.dve(dve)
            TD2.dve(dve)
            for i in range(8):
                dve.wait_ge(st_ln, i + 1)
                e = E[i % 2]
                link(dve, nc.vector.scalar_tensor_tensor(out=e, in0=bank[4 + i % 2][:, 0:384], scalar=0.0, in1=e,
                                                         op0=ALU.max, op1=ALU.add))
                nc.vector.tensor_tensor(e[:, 0:128], e[:, 0:128], past01[:, :], ALU.mult)
                nc.vector.tensor_tensor(e[:, 256:384], e[:, 256:384], past01[:, :], ALU.mult).then_inc(st_sp, 1)
            dve.wait_ge(st_v, 8)
            for tt in range(TT):
                last = nc.vector.tensor_copy(O[:, tt, 0:512], bank[tt][:, :])
            last.then_inc(st_done, 1)
            A2.dve(dve)
            A2.wait(dve)
            TO2[0].dve(dve)
            for tt in range(TT):
                last = nc.vector.tensor_tensor(P[:, tt, 0:512], O[:, tt, 512:1024], O[:, tt, 512:1024], ALU.mult)
            link(dve, last)
            for tt in range(TT):
                last = nc.vector.tensor_reduce(stat[:, 8 + 4 * tt:12 + 4 * tt],
                                               P[:, tt, 0:512].rearrange("p (h d) -> p h d", d=128), AX.X, ALU.add)
            link(dve, last)
            inverse_roots(dve, stat[:, 8:16], 128)
            link(dve, nc.vector.tensor_scalar(stat[:, 8:16], stat[:, 8:16], 1.0 - LAM_INIT, None, ALU.mult))
            for tt in range(TT):
                v = O[:, tt, 512:1024].rearrange("p (h d) -> p h d", d=128)
                last = nc.vector.tensor_tensor(v, v, stat[:, 8 + 4 * tt:12 + 4 * tt].unsqueeze(2).to_broadcast([128, 4, 128]),
                                               ALU.mult)
            link(dve, last)
            for tt in range(TT):
                v = O[:, tt, 512:1024].rearrange("p (h d) -> p h d", d=128)
                last = nc.vector.tensor_tensor(v, v, row("subln").unsqueeze(1).to_broadcast([128, 4, 128]), ALU.mult)
            last.then_inc(o2, 1)
            OUT2[0].splits(dve)
            TO2[1].dve(dve)
            add_to_x(dve, OUT2[1])
            norm(dve)
            T3.dve(dve)
            for f, (c0, n) in enumerate(ff):
                split_until(dve, c_up[f][-1][0] + SPLIT)
                used(dve, c_up[f][-1][0])
                for tt in range(TT):
                    dve.wait_ge(ffn_silu, 2 * f + tt + 1)
                    v = HID[:, f % 2, tt, 0:n]
                    nc.vector.tensor_tensor(v, bank[5 + 2 * tt][:, 0:n], v, ALU.mult).then_inc(ffn_mul, 1)
                split_until(dve, (c_down[f - 1] if f else c_up[0])[-1][0] + SPLIT)
                dve.wait_ge(ffn_Th, f + 1)
                for tt in range(TT):
                    hi_part = HTH[:, 0:n // 128, tt * 128:tt * 128 + 128]
                    last = nc.vector.tensor_tensor(HTL[:, 0:n // 128, tt * 128:tt * 128 + 128],
                                                   bank[5 + 2 * tt][:, 0:n].rearrange("p (k s) -> p k s", s=128),
                                                   hi_part.bitcast(F32), ALU.subtract)
                last.then_inc(ffn_Tl, 1)
            add_to_x(dve, DOWN[-1])

            norm(dve)
            T4.dve(dve)
            P4.dve(dve, {1: lambda: head_sums(dve, 0), 2: lambda: head_norm(dve, 0, [(0, 16, "od_q")]),
                         3: lambda: head_sums(dve, 1024), 4: lambda: head_norm(dve, 1024, [(0, 16, "od_k")])})
            dve.sem_inc(roped4, 1)
            P4.wait(dve)
            TQ4.dve(dve)
            A4.dve(dve)
            A4.wait(dve)
            TO4.dve(dve)
            add_to_x(dve, OUT4)
            TO4.wait(dve)
            nc.vector.memset(stat[:, 60:61], 0.0).then_inc(p_free, 1)
            norm(dve)
            T5.dve(dve)
            split_until(dve, N0)

            dve.wait_ge(iota_set, 3)
            used(dve, c_router[-1][0])
            link(dve, nc.vector.tensor_copy(LG, bank[0][:, 0:2 * NEXP].rearrange("p (t e) -> p t e", t=2)))
            link(dve, nc.vector.tensor_scalar(RIDX, IDX, -1.0, float(NEXP), ALU.mult, ALU.add))
            ridx = RIDX.unsqueeze(1).to_broadcast([128, 2, NEXP])

            def spread(v):
                return v.unsqueeze(2).to_broadcast([128, 2, NEXP])

            for oh, top in ((OH1, MM[:, :, 0]), (OH2, MM[:, :, 1])):
                link(dve, nc.vector.tensor_reduce(top, LG, AX.X, ALU.max))
                link(dve, nc.vector.tensor_tensor(TMP, LG, spread(top), ALU.is_equal))
                link(dve, nc.vector.tensor_tensor(TMP, TMP, ridx, ALU.mult))
                link(dve, nc.vector.tensor_reduce(MM[:, :, 3], TMP, AX.X, ALU.max))
                link(dve, nc.vector.tensor_tensor(oh, ridx, spread(MM[:, :, 3]), ALU.is_equal))
                if oh is OH1:
                    link(dve, nc.vector.scalar_tensor_tensor(out=LG, in0=oh, scalar=-BIG, in1=LG, op0=ALU.mult, op1=ALU.add))
            nc.vector.tensor_tensor(MM[:, :, 2], MM[:, :, 1], MM[:, :, 0], ALU.subtract).then_inc(lg_exp, 1)
            link(dve, nc.vector.tensor_tensor(MASK, OH1, OH2, ALU.add))
            dve.sem_inc(picked, 1)
            dve.wait_ge(lg_exped, 1)
            link(dve, nc.vector.tensor_scalar(MM[:, :, 3], MM[:, :, 2], 1.0, None, ALU.add))
            link(dve, nc.vector.reciprocal(MM[:, :, 3], MM[:, :, 3]))
            link(dve, nc.vector.tensor_tensor(MM[:, :, 2], MM[:, :, 2], MM[:, :, 3], ALU.mult))
            link(dve, nc.vector.tensor_tensor(GW, OH1, spread(MM[:, :, 3]), ALU.mult))
            link(dve, nc.vector.tensor_tensor(TMP, OH2, spread(MM[:, :, 2]), ALU.mult))
            link(dve, nc.vector.tensor_tensor(GW, GW, TMP, ALU.add))
            dve.wait_ge(cnt_ps, 1)
            link(dve, nc.vector.tensor_copy(KEY, bank[1][:, 0:16].rearrange("p (t e) -> p t e", t=2)))
            link(dve, nc.vector.tensor_copy(CNT, bank[2][:, 0:NEXP]))
            link(dve, nc.vector.scalar_tensor_tensor(out=KEY, in0=KEY, scalar=1000.0, in1=MASK, op0=ALU.add, op1=ALU.mult))
            link(dve, nc.vector.tensor_scalar(KEY, KEY, -1000.0, None, ALU.add))
            link(dve, nc.vector.tensor_scalar(TE, CNT, 0.5, None, ALU.is_gt))
            link(dve, nc.vector.scalar_tensor_tensor(out=TE, in0=CNT, scalar=128.5, in1=TE, op0=ALU.is_gt, op1=ALU.add))
            link(dve, nc.vector.tensor_copy(CUM, TE))
            for e in range(1, NEXP):
                link(dve, nc.vector.tensor_tensor(CUM[:, e:e + 1], CUM[:, e:e + 1], CUM[:, e - 1:e], ALU.add))
            over_e = [128, TILE_MAX, NEXP]
            wide = WIDX.unsqueeze(2).to_broadcast(over_e)
            link(dve, nc.vector.tensor_tensor(WE, CUM.unsqueeze(1).to_broadcast(over_e), wide, ALU.is_le))
            link(dve, nc.vector.tensor_reduce(EW, WE, AX.X, ALU.add))
            link(dve, nc.vector.tensor_tensor(WE2, WE, TE.unsqueeze(1).to_broadcast(over_e), ALU.mult))
            link(dve, nc.vector.tensor_reduce(JW, WE2, AX.X, ALU.add))
            link(dve, nc.vector.tensor_tensor(JW, WIDX, JW, ALU.subtract))
            link(dve, nc.vector.tensor_scalar(JW, JW, 128.0, None, ALU.mult))
            link(dve, nc.vector.tensor_tensor(WE, IDX.unsqueeze(1).to_broadcast(over_e), EW.unsqueeze(2).to_broadcast(over_e),
                                              ALU.is_equal))
            for tt in range(TT):
                for src, dest in ((KEY, KS), (GW, GSEL)):
                    link(dve, nc.vector.tensor_tensor(WI[:, tt], WE, src[:, tt, :].unsqueeze(1).to_broadcast(over_e), ALU.mult))
                    link(dve, nc.vector.tensor_reduce(dest[:, tt, 0:TILE_MAX], WI[:, tt], AX.X, ALU.add))
                link(dve, nc.vector.tensor_tensor(KS[:, tt, 0:TILE_MAX], KS[:, tt, 0:TILE_MAX], JW, ALU.subtract))
            link(dve, nc.vector.memset(KS[:, :, TILE_MAX:TILE_MAX + 1], -1.0))
            link(dve, nc.vector.tensor_copy(WORK[:, 0:TILE_MAX], EW))
            nc.vector.tensor_copy(WORK[:, TILE_MAX:TILE_MAX + 1], CUM[:, NEXP - 1:NEXP]).then_inc(list_set, 1)

            dve.wait_ge(list_set, 1)
            tiles = dve.value_load(WORK[0:1, TILE_MAX:TILE_MAX + 1], min_val=4, max_val=TILE_MAX)
            moe_tiles[dve.engine] = tiles
            link(dve, nc.vector.memset(MCOMB, 0.0))
            nc.vector.memset(MY, 0.0).then_inc(m_yd, 1)
            dve.wait_ge(m_yd, 1)
            dve.sem_inc(m_ya, 1)
            select(dve, 0)
            moe_lo(dve, 0, range(0, SPLIT))
            gathered_lo(dve, 0)
            with dve.Fori(0, tiles) as w:
                for tt in range(TT):
                    last = nc.vector.tensor_scalar(MSELG[:, tt, :], IOTA, KS[:, tt, bass.ds(w, 1)],
                                                   GSEL[:, tt, bass.ds(w, 1)], ALU.is_equal, ALU.mult)
                last.then_inc(m_selg, 1)
                select(dve, w + 1)
                moe_lo(dve, w, range(SPLIT, SPLIT + 2))
                scatter_add(dve, w, m_acc)

                def hidden_lo(f):
                    dve.wait_ge(m_Th, w * CF + (f + 1))
                    nc.vector.tensor_tensor(MHT[f % 2][1], bank[4 + f % 2][:, :], MHT[f % 2][0].bitcast(F32),
                                            ALU.subtract).then_inc(m_Tl, 1)

                done = SPLIT + 2
                for f in range(CF):
                    if f >= 1:
                        last_gate = moe_at["gate", f, 1]
                        moe_lo(dve, w, range(done, last_gate + SPLIT))
                        hidden_lo(f - 1)
                        if f == 1:
                            dve.wait_ge(m_ct, w + 1)
                            nc.vector.tensor_copy(MCOMB, bank[5][:, 0:S]).then_inc(m_ctc, 1)
                        done = last_gate + SPLIT
                    last_up = moe_at["up", f, 1]
                    moe_lo(dve, w, range(done, last_up + SPLIT))
                    done = last_up + SPLIT
                    dve.wait_ge(m_silu, w * CF + (f + 1))
                    dve.wait_ge(consumed, w * MOE_CHUNKS + (N0 + last_up + 1))
                    if f >= 2:
                        dve.wait_ge(m_T, w * CF + (f - 1))
                    nc.vector.tensor_tensor(MHID[:, f % 2, 1, :], bank[f % 2 * 2 + 1][:, :], MHID[:, f % 2, 0, :],
                                            ALU.mult).then_inc(m_mul, 1)
                moe_lo(dve, w, range(done, MOE_CHUNKS - 2))
                gathered_lo(dve, w + 1)
                moe_lo(dve, w, [MOE_CHUNKS - 2])
                hidden_lo(CF - 1)
                moe_lo(dve, w, range(MOE_CHUNKS - 1, MOE_CHUNKS + 2))
                dve.wait_ge(consumed, w * MOE_CHUNKS + (N0 + MOE_CHUNKS))
                nc.vector.tensor_copy(MY[:, 512:1024], bank[7][:, :]).then_inc(m_yd, 1)
                moe_lo(dve, w, [MOE_CHUNKS + 2])
            next_split[dve.engine] = N0 + SPLIT
            scatter_add(dve, tiles, x_ready)
            dve.wait_ge(x_ready, counts["x"] + counts["x_more"] + TT)

            counts["x_more"] += TT
            norm(dve)
            T6.dve(dve)

            def forget_in():
                for tt in range(TT):
                    last = nc.vector.tensor_tensor(FX[:, tt, :], FX[:, tt, :], row("b_f"), ALU.add)
                last.then_inc(f_in, 1)

            def forget():
                dve.wait_ge(f_ln, 1)
                nc.vector.scalar_tensor_tensor(out=FX, in0=FX, scalar=0.0, in1=FA, op0=ALU.min,
                                               op1=ALU.subtract).then_inc(f_log, 1)

            P6.dve(dve, {6: forget_in, 7: forget})
            P6.wait(dve)
            dve.wait_ge(f_c, 1)
            nc.vector.tensor_scalar(FC, bank[0][0:16, 0:S], -1.0, None, ALU.mult).then_inc(f_cc, 1)
            TQ6.dve(dve)
            A6.dve(dve)
            A6.wait(dve)
            nc.vector.tensor_tensor(O[:, :, :], O[:, :, :], P[:, :, 3584:4608], ALU.mult).then_inc(g6, 1)
            TO6.dve(dve)
            add_to_x(dve, OUT6)
            TO6.wait(dve)

            norm(dve)
            T7.dve(dve)

            def twice(pairs):
                for tt in range(TT):
                    for src, dest in pairs:
                        last = nc.vector.tensor_copy(dest(tt).rearrange("p (g a d) -> p g a d", g=4, a=2),
                                                     P[:, tt, src:src + 256].rearrange("p (g d) -> p g d", g=4)
                                                     .unsqueeze(2).to_broadcast([128, 4, 2, DH]))
                return last

            def keys(src, dest):
                rope(dve, P[:, :, src:src + 256], cos0, sin0, 4, TT)
                twice([(src, lambda tt: P[:, tt, dest:dest + 512])])

            P7.dve(dve, {0: lambda: rope(dve, P[:, :, 0:512], cos0, sin0, 8, TT),
                         1: lambda: rope(dve, P[:, :, 512:1024], cos0, sin0, 8, TT),
                         2: lambda: keys(1536, 4096), 3: lambda: keys(2048, 4608),
                         4: lambda: twice([(1024, lambda tt: O[:, tt, 0:512]), (1280, lambda tt: O[:, tt, 512:1024])])
                         .then_inc(roped7, 1)})
            P7.wait(dve)
            TQ7.dve(dve)
            TQ7.wait(dve)
            for j in range(2):
                link(dve, nc.vector.memset(block_tiles(j), 0.0))
            link(dve, nc.vector.memset(VCB, 0.0))

            def blocks(i):
                for g in range(4):
                    n = 4 * i + g
                    dve.wait_ge(c_T, n + 1)
                    src = bank[n % 4][:, 0:S].rearrange("p (c l) -> p l c", l=16)
                    pe_cols = vec[:, VEC_ROWS["pe_k" if i == 0 else "pe_v"][0]:][:, 0:16]
                    for h in range(2):
                        rows = slice(64 * h, 64 * h + 64)
                        for j in range(2):
                            dest = block_tiles(j)[rows, :, g * CPAD:g * CPAD + NCMP]
                            last = nc.vector.tensor_tensor(dest, src[rows, h::2, j:j + NCMP],
                                                           pe_cols[rows, 8 * j:8 * j + 8].unsqueeze(2).to_broadcast([64, 8, NCMP]),
                                                           ALU.add)
                    last.then_inc(c_A, 1)
                dve.wait_ge(c_A, 4 * i + 4)
                dve.sem_inc(c_full, 1)

            def blocks_lo(i):
                dve.wait_ge(c_hi, i + 1)
                for j in range(2):
                    last = nc.vector.tensor_tensor(xblocks[1][:, 8 * j:8 * j + 8, :], block_tiles(j),
                                                   xblocks[0][:, 8 * j:8 * j + 8, :].bitcast(F32), ALU.subtract)
                last.then_inc(c_lo, 1)
                dve.wait_ge(c_lo, i + 1)

            def compress_lo(i):
                split_until(dve, c_ck[i][0][-1][0] + SPLIT)
                dve.wait_ge(c_hTh, i + 1)
                nc.vector.tensor_tensor(CHT[i][1], bank[6 + i][:, 0:256].rearrange("p (k r) -> p k r", k=2),
                                        CHT[i][0].bitcast(F32), ALU.subtract).then_inc(c_hTl, 1)

            blocks(0)
            blocks_lo(0)
            blocks(1)
            compress_lo(0)
            blocks_lo(1)
            compress_lo(1)
            used(dve, c_ck[1][1][-1][0])
            link(dve, nc.vector.tensor_copy(KCN[:, 0, :], bank[4][:, 256:256 + DH]))
            for g in range(4):
                last = nc.vector.tensor_copy(VCB[32 * g:32 * g + 32, 64 * g:64 * g + 64], bank[5][32 * g:32 * g + 32, 256:256 + DH])
            link(dve, last)
            rope(dve, KCN[:, 0:1, :], con("ccos").unsqueeze(1), con("csin").unsqueeze(1), 1, 1)
            nc.vector.tensor_copy(KCN[:, 1, :], KCN[:, 0, :]).then_inc(c_roped, 1)
            dve.wait_ge(c_kT, 1)
            nc.vector.tensor_copy(KCT, bank[6][:, 0:128]).then_inc(c_kTc, 1)
            cs_v = CS.rearrange("p (a c) -> p a c", c=CPAD)
            for tt in range(TT):
                dve.wait_ge(q_s, tt + 1)
                add = con("cmadd")[:, tt * CPAD:tt * CPAD + CPAD].unsqueeze(1).to_broadcast([128, 16, CPAD])
                keep = con("cm01")[:, tt * CPAD:tt * CPAD + CPAD].unsqueeze(1).to_broadcast([128, 16, CPAD])
                if tt:
                    dve.wait_ge(q_T, tt)
                for odd in range(2):
                    last = nc.vector.tensor_tensor(cs_v[:, 8 * odd:8 * odd + 8, :],
                                                   bank[2 * tt + odd][:, 0:256].rearrange("p (a c) -> p a c", c=CPAD),
                                                   add[:, 0:8, :], ALU.add)
                link(dve, last)
                link(dve, nc.vector.tensor_reduce(stat[:, 16:32], cs_v, AX.X, ALU.max))
                nc.vector.tensor_tensor(cs_v, cs_v, stat[:, 16:32].unsqueeze(2).to_broadcast([128, 16, CPAD]),
                                        ALU.subtract).then_inc(q_m, 1)
                dve.wait_ge(q_e, tt + 1)
                link(dve, nc.vector.tensor_reduce(stat[:, 16:32], cs_v, AX.X, ALU.add))
                link(dve, nc.vector.reciprocal(stat[:, 16:32], stat[:, 16:32]))
                gates = P[:, tt, 2560:2608].rearrange("p (g r q b) -> p q r g b", r=2, q=2, b=3)[:, :, :, :, 0]
                sv = stat[:, 16:32].rearrange("p (q r g) -> p q r g", q=2, r=2)
                link(dve, nc.vector.tensor_tensor(sv, sv, gates, ALU.mult))
                link(dve, nc.vector.tensor_tensor(cs_v, cs_v, keep, ALU.mult))
                nc.vector.tensor_tensor(cs_v, cs_v, stat[:, 16:32].unsqueeze(2).to_broadcast([128, 16, CPAD]),
                                        ALU.mult).then_inc(q_p, 1)
                dve.wait_ge(q_T, tt + 1)
                nc.vector.tensor_copy(CPT, bank[7][:, :]).then_inc(q_Tc, 1)
                dve.wait_ge(q_v, tt + 1)
                ov = O[:, tt, :].rearrange("p (g r d) -> p r g d", g=4, r=4)
                for b in range(2):
                    for r in range(2):
                        src = bank[4 + b][:, 256 * r:256 * r + 256].rearrange("p (g d) -> p g d", g=4)
                        last = nc.vector.tensor_copy(ov[:, 2 * r + b], src)
                last.then_inc(q_o, 1)
                dve.wait_ge(q_o, tt + 1)
            A7.dve(dve)
            A7.wait(dve)
            nc.vector.tensor_tensor(O[:, :, :], O[:, :, :], P[:, :, 3072:4096], ALU.mult).then_inc(g7, 1)
            TO7.dve(dve)
            add_to_x(dve, OUT7)
            TO7.wait(dve)
            rms(dve)
            dve.wait_ge(gfin2_in, 16)
            for tt in range(TT):
                last = nc.vector.scalar_tensor_tensor(out=X[:, tt, :], in0=X[:, tt, :], scalar=stat[:, tt:tt + 1],
                                                      in1=GAIN, op0=ALU.mult, op1=ALU.mult)
            last.then_inc(out_set, 1)

        @block.tensor
        def _(pe):
            pe.wait_ge(vec_in, 16)
            pe.wait_ge(const_set, N_CONST)
            nc.tensor.transpose(bank[7][:, 0:NVEC], O[0:NVEC, 1, 0:128], ident[0:NVEC, 0:NVEC]).then_inc(vec_ready, 1)
            pe.wait_ge(c_lo0, 1)
            for m in range(6):
                if m >= 4:
                    pe.wait_ge(ada_used, m - 3)
                for n, k0, nk in c_ada[m]:
                    wt = take(pe, n)
                    for k in range(nk):
                        last = three(bank[m % 4][:, :], [x[:, k0 + k, :] for x in C_PARTS], wt, k, k0 + k == 0,
                                     k0 + k == KD - 1, check=True)
                    last.then_inc(consumed, 1)
            pe.wait_ge(h1, 1)
            T1.pe(pe)
            pe.wait_ge(ada_used, 6)
            P1.pe(pe, T1)
            pe.wait_ge(roped1, 1)
            P1.wait(pe)
            TQ1.pe(pe)
            TQ1.wait(pe)
            pe.wait_ge(band_in, 32)
            for g in range(4):
                out = bank[4 + g // 2][:, 256 * (g % 2):256 * (g % 2) + 256]
                nc.tensor.matmul(out, P[:, 0, g * 128:g * 128 + 128], BAND[:, g, 0:256], start=True, stop=False,
                                 skip_group_check=True)
                last = nc.tensor.matmul(out[:, 128:256], P[:, 1, g * 128:g * 128 + 128], BAND[:, g, 256:384], start=False,
                                        stop=True, skip_group_check=True)
            last.then_inc(d_made, 1)
            pe.wait_ge(d_copied, 1)
            for tt in range(TT):
                for g in range(4):
                    last = nc.tensor.matmul(bank[2 + tt][:, g * 128:g * 128 + 128],
                                            scr[:, 256 * g + 128 * tt:256 * g + 128 * tt + 128], GRP[:, g, :], start=True,
                                            stop=True, skip_group_check=True)
            last.then_inc(y_made, 1)
            A1.pe(pe)
            A1.wait(pe)
            pe.wait_ge(gated1, 1)
            pe.wait_ge(y_gated, 1)
            TY1.pe(pe)
            pe.wait_ge(gated1, 1)
            TY1.wait(pe)
            TA1.pe(pe)
            UP1.pe(pe)
            TA1.wait(pe)
            pe.wait_ge(up_used, 1)
            AUP1.pe(pe)
            pe.wait_ge(merged, 1)
            TM1.pe(pe)
            OUT1.pe(pe, operand=TM1)

            pe.wait_ge(n_made, 2)
            T2.pe(pe)
            P2.pe(pe, T2)
            P2.wait(pe)
            TS2.pe(pe)
            pe.wait_ge(roped2, 1)
            TS2.wait(pe)
            TD2.pe(pe)
            TD2.wait(pe)
            for i in range(10):
                if i < 8:
                    if i >= 2:
                        pe.wait_ge(st_sp, i - 1)
                    (a, b) = at(i)
                    q, k = QT[b:b + 64, a, :], KT[b:b + 64, a, :]
                    z = bank[4 + i % 2]
                    nc.tensor.matmul(z[:, 0:256], k[:, 0:128], q, start=True, stop=True, skip_group_check=True)
                    nc.tensor.matmul(z[:, 256:384], k[:, 128:256], q[:, 128:256], start=True, stop=True,
                                     skip_group_check=True).then_inc(st_z, 1)
                if 1 <= i <= 8:
                    j = i - 1
                    pe.wait_ge(st_sp, j + 1)
                    if j >= 2:
                        pe.wait_ge(st_w, j - 1)
                    (a, b) = at(j)
                    q, k = QT[b:b + 64, a, :], KT[b:b + 64, a, :]
                    r, e = bank[6 + j % 2], E[j % 2]
                    nc.tensor.matmul(r[:, 0:256], k[:, 0:128], q, start=True, stop=False, skip_group_check=True)
                    nc.tensor.matmul(r[:, 0:256], neg_tri[:, :], e[:, 0:256], start=False, stop=False, skip_group_check=True)
                    nc.tensor.matmul(r[:, 128:256], neg_ones[:, :], e[:, 256:384], start=False, stop=False,
                                     skip_group_check=True)
                    nc.tensor.matmul(r[:, 0:128], identb[:, :], mask_past[:, :], start=False, stop=True,
                                     skip_group_check=True)
                    nc.tensor.matmul(r[:, 256:384], k[:, 128:256], q[:, 128:256], start=True, stop=False,
                                     skip_group_check=True)
                    nc.tensor.matmul(r[:, 256:384], neg_tri[:, :], e[:, 256:384], start=False, stop=False,
                                     skip_group_check=True)
                    nc.tensor.matmul(r[:, 256:384], identb[:, :], mask_past[:, :], start=False, stop=True,
                                     skip_group_check=True).then_inc(st_r, 1)
                if i >= 2:
                    j = i - 2
                    pe.wait_ge(st_w, j + 1)
                    p, o = PT[j % 2], slice(j * 64, j * 64 + 64)
                    v = values(1024 + 64 * j, 64)
                    nc.tensor.matmul(bank[0][:, o], p[:, 0:128], v(0), start=True, stop=True, skip_group_check=True)
                    nc.tensor.matmul(bank[1][:, o], p[:, 128:256], v(0), start=True, stop=False, skip_group_check=True)
                    nc.tensor.matmul(bank[1][:, o], p[:, 256:384], v(1), start=False, stop=True,
                                     skip_group_check=True).then_inc(st_v, 1)
            pe.wait_ge(st_done, 1)
            A2.pe(pe)
            A2.wait(pe)
            TO2[0].pe(pe)
            TO2[0].wait(pe)
            OUT2[0].pe(pe, last_=False)
            pe.wait_ge(o2, 1)
            TO2[1].pe(pe)
            TO2[1].wait(pe)
            OUT2[1].pe(pe, first=False)
            pe.wait_ge(n_made, 4)
            T3.pe(pe)
            T3.wait(pe)
            def hidden(chunks, b, n):
                for c, k0, nk in chunks:
                    wt = take(pe, c)
                    for tt in range(TT):
                        for k in range(nk):
                            last = three(bank[b + 2 * tt][:, 0:n], xt(k0 + k, tt), wt, k, k0 + k == 0, k0 + k == KD - 1,
                                         check=True)
                    last.then_inc(consumed, 1)

            for f, (c0, n) in enumerate(ff):
                if f >= 1:
                    pe.wait_ge(ffn_silu, 2 * f)
                hidden(c_gate[f], 4, n)
                if f >= 1:
                    pe.wait_ge(ffn_Tl, f)
                hidden(c_up[f], 5, n)
                if f >= 1:
                    DOWN[f - 1].pe(pe, first=f == 1, last_=False)
                pe.wait_ge(ffn_mul, 2 * f + 2)
                for tt in range(TT):
                    for k in range(n // 128):
                        last = nc.tensor.transpose(bank[5 + 2 * tt][:, k * 128:k * 128 + 128],
                                                   HID[:, f % 2, tt, k * 128:k * 128 + 128], ident[:, :])
                last.then_inc(ffn_T, 1)
            pe.wait_ge(ffn_Tl, NF)
            DOWN[-1].pe(pe, first=False)

            pe.wait_ge(n_made, 6)
            T4.pe(pe)
            P4.pe(pe, T4)
            P4.wait(pe)
            pe.wait_ge(roped4, 1)
            TQ4.pe(pe)
            TQ4.wait(pe)
            pe.wait_ge(rel_in, 32)
            A4.pe(pe)
            A4.wait(pe)
            TO4.pe(pe)
            OUT4.pe(pe, operand=TO4)
            pe.wait_ge(n_made, 8)
            T5.pe(pe)
            T5.wait(pe)
            wt = take(pe, c_router[0][0])
            for tt in range(TT):
                for kt in range(KD):
                    last = three(bank[0][:, NEXP * tt:NEXP * tt + NEXP], xt(kt, tt), wt, kt, kt == 0, kt == KD - 1, check=True)
            last.then_inc(consumed, 1)
            pe.wait_ge(picked, 1)
            nc.tensor.matmul(bank[1][:, 0:8], past01[:, :], MASK[:, 0, :], start=True, stop=True, skip_group_check=True)
            nc.tensor.matmul(bank[1][:, 8:16], ones[:, :], MASK[:, 0, :], start=True, stop=False, skip_group_check=True)
            nc.tensor.matmul(bank[1][:, 8:16], past01[:, :], MASK[:, 1, :], start=False, stop=True, skip_group_check=True)
            nc.tensor.matmul(bank[2][:, 0:8], ones[:, :], MASK[:, 0, :], start=True, stop=False)
            nc.tensor.matmul(bank[2][:, 0:8], ones[:, :], MASK[:, 1, :], start=False, stop=True).then_inc(cnt_ps, 1)

            pe.wait_ge(list_set, 1)
            tiles = pe.value_load(WORK[0:1, TILE_MAX:TILE_MAX + 1], min_val=4, max_val=TILE_MAX)
            gather(pe, 0)
            with pe.Fori(0, tiles) as w:
                def product(key, k0, outs):
                    n = N0 + moe_at[key]
                    nk, width = expert_chunk(n)
                    pe.wait_ge(lo_made, w * MOE_CHUNKS + (n + 1))
                    wt = parts(n, nk, width)
                    down_ = key[0] == "down"
                    for k in range(nk):
                        kt = k0 + k
                        x = ([y[:, kt * 128:kt * 128 + 128] for y in MHT[key[1] % 2]] if down_ else
                             [y[:, kt, 0:128] for y in (XTH, XTL)])
                        for j, out in enumerate(outs):
                            last = three(out, x, [y[:, :, 512 * j:512 * j + 512] for y in wt], k,
                                         kt == 0 and (not down_ or key[1] == 0),
                                         kt == 3 and key[1] == CF - 1 if down_ else kt == KD - 1, check=True)
                    last.then_inc(consumed, 1)

                def hidden_product(what, f, b):
                    for i in range(2):
                        product((what, f, i), 4 * i, [bank[b][:, :]])

                def moe_T(f):
                    pe.wait_ge(m_mul, w * CF + (f + 1))
                    if f >= 2:
                        pe.wait_ge(m_Tl, w * CF + (f - 1))
                    for k in range(4):
                        last = nc.tensor.transpose(bank[4 + f % 2][:, k * 128:k * 128 + 128],
                                                   MHID[:, f % 2, 1, k * 128:k * 128 + 128], ident[:, :])
                    last.then_inc(m_T, 1)

                def output_product(f, i):
                    pe.wait_ge(m_Tl, w * CF + (f + 1))
                    product(("down", f, i), 2 * i, [bank[6][:, :], bank[7][:, :]])

                pe.wait_ge(m_xl, w * 2 + 2)
                for f in range(CF):
                    if f >= 2:
                        pe.wait_ge(m_silu, w * CF + (f - 1))
                    hidden_product("gate", f, f % 2 * 2)
                    if f == 0:
                        scatter(pe, w)
                    if f >= 1:
                        if f == 1:
                            pe.wait_ge(m_acc, w + 1)
                        if f == 2:
                            pe.wait_ge(m_ctc, w + 1)
                        moe_T(f - 1)
                    if f == 1:
                        pe.wait_ge(m_selg, w + 1)
                        for tt in range(TT):
                            last = nc.tensor.transpose(bank[5][:, tt * 128:tt * 128 + 128], MSELG[:, tt, :], ident[:, :])
                        last.then_inc(m_ct, 1)
                    if f >= 2:
                        pe.wait_ge(m_mul, w * CF + (f - 1))
                    hidden_product("up", f, f % 2 * 2 + 1)
                    if f == CF - 1:
                        gather(pe, w + 1)
                    if f >= 1:
                        output_product(f - 1, 0)
                        if f == CF - 1:
                            moe_T(f)
                        output_product(f - 1, 1)
                output_product(CF - 1, 0)
                output_product(CF - 1, 1)
            scatter(pe, tiles)
            moe_tiles[pe.engine] = tiles

            pe.wait_ge(n_made, 10)
            T6.pe(pe)
            P6.pe(pe, T6)
            pe.wait_ge(f_log, 1)
            P6.wait(pe)
            FL = lambda tt: FX[:, tt, :]
            nc.tensor.matmul(bank[0][0:16, 0:128], FL(0), past01[:, :], start=True, stop=False, skip_group_check=True)
            nc.tensor.matmul(bank[0][0:16, 0:128], FL(0), ident[:, :], start=False, stop=True, skip_group_check=True)
            nc.tensor.matmul(bank[0][0:16, 128:256], FL(0), ones[:, :], start=True, stop=False, skip_group_check=True)
            nc.tensor.matmul(bank[0][0:16, 128:256], FL(1), past01[:, :], start=False, stop=False, skip_group_check=True)
            nc.tensor.matmul(bank[0][0:16, 128:256], FL(1), ident[:, :], start=False, stop=True,
                             skip_group_check=True).then_inc(f_c, 1)
            TQ6.pe(pe)
            TQ6.wait(pe)
            pe.wait_ge(f_cc, 1)
            A6.pe(pe)
            pe.wait_ge(g6, 1)
            TO6.pe(pe)
            OUT6.pe(pe, operand=TO6)

            pe.wait_ge(n_made, 12)
            T7.pe(pe)
            P7.pe(pe, T7)
            P7.wait(pe)
            pe.wait_ge(roped7, 1)
            TQ7.pe(pe)
            for n in range(8):
                if n >= 4:
                    pe.wait_ge(c_A, n - 3)
                for tt in range(TT):
                    last = nc.tensor.transpose(bank[n % 4][:, tt * 128:tt * 128 + 128],
                                               twice_o(n)(tt), ident[:, :])
                last.then_inc(c_T, 1)
            for i in range(2):
                if i == 0:
                    TQ7.wait(pe)
                pe.wait_ge(c_lo, i + 1)
                for n, k0, nk in c_ck[i][0]:
                    wt = take(pe, n)
                    for k in range(nk):
                        last = three(bank[4 + i][:, 0:256], [x[:, k0 + k, :] for x in xblocks], wt, k, k0 + k == 0,
                                     k0 + k == 15, check=True)
                    last.then_inc(consumed, 1)
                pe.wait_ge(c_s, i + 1)
                for k in range(2):
                    last = nc.tensor.transpose(bank[6 + i][:, k * 128:k * 128 + 128], CH[i][:, k * 128:k * 128 + 128], ident[:, :])
                last.then_inc(c_hT, 1)
                pe.wait_ge(c_hTl, i + 1)
                wt = take(pe, c_ck[i][1][0][0])
                for k in range(2):
                    last = three(bank[4 + i][:, 256:256 + DH], [x[:, k, :] for x in CHT[i]], wt, k, k == 0, k == 1, check=True)
                last.then_inc(consumed, 1)
            pe.wait_ge(c_roped, 1)
            nc.tensor.transpose(bank[6][:, 0:128], KCN.rearrange("p a d -> p (a d)"), ident[:, :]).then_inc(c_kT, 1)
            pe.wait_ge(c_kTc, 1)
            for tt in range(TT):
                for r in range(4):
                    for g in range(4):
                        a, b = at(4 * g + r)
                        c = (r // 2) * 128 + g * CPAD
                        last = nc.tensor.matmul(bank[2 * tt + r % 2][:, c:c + CPAD],
                                                QT[b:b + 64, a, tt * 128:tt * 128 + 128], KCT[b:b + 64, g * CPAD:g * CPAD + CPAD],
                                                start=True, stop=True, skip_group_check=True)
                last.then_inc(q_s, 1)
            for tt in range(TT):
                pe.wait_ge(q_p, tt + 1)
                for r in range(4):
                    last = nc.tensor.transpose(bank[7][:, r * 128:r * 128 + 128], CS[:, r * 128:r * 128 + 128], ident[:, :])
                last.then_inc(q_T, 1)
                pe.wait_ge(q_Tc, tt + 1)
                if tt:
                    pe.wait_ge(q_o, tt)
                for r in range(4):
                    last = nc.tensor.matmul(bank[4 + r // 2][:, 256 * (r % 2):256 * (r % 2) + 256],
                                            CPT[:, r * 128:r * 128 + 128], VCB, start=True, stop=True, skip_group_check=True)
                last.then_inc(q_v, 1)
            pe.wait_ge(q_o, 2)
            A7.pe(pe)
            pe.wait_ge(g7, 1)
            TO7.pe(pe)
            OUT7.pe(pe, operand=TO7)


def kernel(**inputs):
    import concourse.bacc as bacc
    from concourse.bass_utils import run_bass_kernel_spmd

    arrays = {n: np.ascontiguousarray(inputs[n]) for n in (
        "x", "w_ada", "b_ada", "g_norm", "w_in", "w_pool_grp", "w_pool_up", "w_attn_up", "w_out", "g_final",
        "positions_2", "ev_w_in_2", "ev_w_out_2", "ev_w_gate_2", "ev_w_up_2", "ev_w_down_2", "od_w_qkv_2", "od_w_out_2",
        "od_router_2", "od_we_gate_2", "od_we_up_2", "od_we_down_2", "fox_w_in_3", "fox_w_out_3", "nsa_w_in_3",
        "nsa_w_ck1_3", "nsa_w_ck2_3", "nsa_w_cv1_3", "nsa_w_cv2_3", "nsa_w_out_3", "final_g_3")}
    arrays["vec"] = np.concatenate([np.asarray(inputs[n]).reshape(-1, 128) for n in (
        "ev_attn_norm_2", "ev_ffn_norm_2", "od_attn_norm_2", "od_ffn_norm_2", "norm_g_3", "pool_scale", "c",
        "nsa_pe_k_3", "nsa_pe_v_3")])
    arrays["small"] = np.concatenate([np.asarray(inputs[n]).reshape(-1) for n in (
        "ev_q_norm_2", "ev_k_norm_2", "od_q_norm_2", "od_k_norm_2", "ev_subln_2", "fox_b_f_3", "ev_lambda_q1_2",
        "ev_lambda_k1_2", "ev_lambda_q2_2", "ev_lambda_k2_2")])
    distance = np.clip(128 + np.arange(128)[:, None] - np.arange(256)[None, :], -128, 128) + 128
    arrays["rel"] = np.ascontiguousarray(np.asarray(inputs["od_rel_bias_2"])[0][:, distance].transpose(1, 0, 2))
    arrays["co"], arrays["band"] = shape_constants()

    nc = bacc.Bacc("TRN2", target_bir_lowering=False, num_devices=1)
    tensors = {n: nc.dram_tensor(f"in_{n}", a.shape, mybir.dt.from_np(a.dtype), kind="ExternalInput").ap()
               for n, a in arrays.items()}
    tensors["out"] = nc.dram_tensor("out_x", (1, S, D), F32, kind="ExternalOutput").ap()
    build(nc, tensors)
    result = run_bass_kernel_spmd(nc, [{f"in_{n}": a for n, a in arrays.items()}], core_ids=[0])
    return result.results[0]["out_x"]
```
